# Optimizing a Trainium2 kernel written in Bass

```python
import math
import jax, jax.numpy as jnp
from jax import lax
import numpy as np

D_MODEL = 1024
BATCH = 1
SEQ = 256
DEPTH = 1
DEC_BATCH = 8
DEC_SEQ = 8
PAST_LEN = 1024
PAGE_SIZE = 128

H_A = 4
DK_A = 64
DV_A = 2 * DK_A
ROPE_THETA = 10000.0
Q_BLOCK = 128
H_M = 4
DH_M = 128
CONV_W = 4
M_CHUNK = 64
N_EXP = 32
TOP_K = 4
D_FF = D_MODEL
SWIGLU_LIMIT = 7.0
SWIGLU_ALPHA = 1.702
MOE_BLOCK = 128
EPS = 1e-6

W_QA = H_A * 2 * DK_A
W_VA = H_A * DV_A
W_M = H_M * DH_M
SPLIT_SIZES = (W_QA, W_QA, W_VA, W_M, W_M, W_M, W_M, 2 * H_M, D_MODEL, D_MODEL)
D_IN = sum(SPLIT_SIZES)
SPLIT_POINTS = tuple(sum(SPLIT_SIZES[: i + 1]) for i in range(len(SPLIT_SIZES) - 1))

kernel_name = "hybrid_diffattn_mlstm_moe_adaln_step"

F32 = jnp.float32

def rmsnorm(x, g):
    xf = x.astype(F32)
    y = xf * lax.rsqrt(jnp.mean(xf * xf, axis=-1, keepdims=True) + EPS)
    return (y * g.astype(F32)).astype(x.dtype)

def rope(x, pos):
    half = DK_A // 2
    inv = ROPE_THETA ** (-jnp.arange(half, dtype=F32) * 2.0 / DK_A)
    ang = pos.astype(F32)[:, None] * inv[None, :]
    cos = jnp.cos(ang)[None, :, None, None, :]
    sin = jnp.sin(ang)[None, :, None, None, :]
    xf = x.astype(F32)
    x1, x2 = xf[..., :half], xf[..., half:]
    return jnp.concatenate([x1 * cos - x2 * sin, x2 * cos + x1 * sin], axis=-1).astype(x.dtype)

def diff_attend(q, k, v, q_pos, k_pos, lam):
    s = jnp.einsum('bqhcd,bkhcd->bhcqk', q, k, preferred_element_type=F32) * (DK_A ** -0.5)
    mask = k_pos[None, :] <= q_pos[:, None]
    p = jax.nn.softmax(jnp.where(mask, s, -jnp.inf), axis=-1)
    a = p[:, :, 0] - lam * p[:, :, 1]
    return jnp.einsum('bhqk,bkhd->bqhd', a, v.astype(F32))

def causal_conv(u, buf, w, b):
    T = u.shape[1]
    full = jnp.concatenate([buf.astype(u.dtype), u], axis=1)
    out = sum(full[:, j:j + T] * w[j] for j in range(CONV_W)) + b
    return jax.nn.silu(out), full[:, -(CONV_W - 1):]

def mlstm_chunkwise(q, k, v, log_i, log_f, C0, n0, m0):
    B, T, H, D = q.shape
    L = M_CHUNK if T % M_CHUNK == 0 else T
    nc = T // L

    def to_chunks(a):
        a = a.reshape((B, nc, L) + a.shape[2:])
        return jnp.moveaxis(jnp.moveaxis(a, 1, 0), 3, 2)

    tri = jnp.tril(jnp.ones((L, L), dtype=bool))

    def step(carry, xs):
        C, n, m = carry
        qc, kc, vc, li, lf = xs
        b = jnp.cumsum(lf, axis=-1)
        logD = jnp.where(tri, b[..., :, None] - b[..., None, :] + li[..., None, :], -jnp.inf)
        inter = b + m[..., None]
        mt = jnp.maximum(inter, jnp.max(logD, axis=-1))
        S = jnp.einsum('bhtd,bhsd->bhts', qc, kc) * jnp.exp(logD - mt[..., None])
        ei = jnp.exp(inter - mt)
        num = ei[..., None] * jnp.einsum('bhtd,bhde->bhte', qc, C) + jnp.einsum('bhts,bhse->bhte', S, vc)
        den = ei * jnp.einsum('bhtd,bhd->bht', qc, n) + jnp.sum(S, axis=-1)
        h = num / jnp.maximum(jnp.abs(den), jnp.exp(-mt))[..., None]
        g = b[..., -1:] - b + li
        bl = b[..., -1] + m
        m_new = jnp.maximum(bl, jnp.max(g, axis=-1))
        wg = jnp.exp(g - m_new[..., None])
        decay = jnp.exp(bl - m_new)
        C_new = decay[..., None, None] * C + jnp.einsum('bhs,bhsd,bhse->bhde', wg, kc, vc)
        n_new = decay[..., None] * n + jnp.einsum('bhs,bhsd->bhd', wg, kc)
        return (C_new, n_new, m_new), h

    xs = (to_chunks(q), to_chunks(k), to_chunks(v), to_chunks(log_i), to_chunks(log_f))
    (C, n, m), hs = lax.scan(step, (C0.astype(F32), n0.astype(F32), m0.astype(F32)), xs)
    hs = jnp.swapaxes(jnp.moveaxis(hs, 0, 1), 2, 3).reshape(B, T, H, D)
    return hs, C, n, m

def mixer(h, p, lam_init, pos, past, conv_buf, C0, n0, m0):
    B, T, _ = h.shape
    z = h @ p['w_in']
    qa, ka, va, qm, km, vm, om, ifm, ga, gb = jnp.split(z, SPLIT_POINTS, axis=-1)
    qa = rope(qa.reshape(B, T, H_A, 2, DK_A), pos)
    ka = rope(ka.reshape(B, T, H_A, 2, DK_A), pos)
    va = va.reshape(B, T, H_A, DV_A)
    lam = (jnp.exp(jnp.sum(p['lambda_q1'].astype(F32) * p['lambda_k1'].astype(F32)))
           - jnp.exp(jnp.sum(p['lambda_q2'].astype(F32) * p['lambda_k2'].astype(F32))) + lam_init)
    if past is None:
        nb = T // Q_BLOCK

        def one_block(i):
            qs = lax.dynamic_slice_in_dim(qa, i * Q_BLOCK, Q_BLOCK, axis=1)
            qp = lax.dynamic_slice_in_dim(pos, i * Q_BLOCK, Q_BLOCK)
            return diff_attend(qs, ka, va, qp, pos, lam)

        o = lax.map(one_block, jnp.arange(nb))
        o = jnp.moveaxis(o, 0, 1).reshape(B, T, H_A, DV_A)
    else:
        k_all = jnp.concatenate([past[0].astype(ka.dtype), ka], axis=1)
        v_all = jnp.concatenate([past[1].astype(va.dtype), va], axis=1)
        o = diff_attend(qa, k_all, v_all, pos, jnp.arange(k_all.shape[1]), lam)
    o = rmsnorm(o, p['g_subln']) * (1.0 - lam_init)
    qk, new_buf = causal_conv(jnp.concatenate([qm, km], axis=-1), conv_buf, p['w_conv'], p['b_conv'])
    qm2, km2 = jnp.split(qk.astype(F32), 2, axis=-1)
    q = qm2.reshape(B, T, H_M, DH_M)
    k = km2.reshape(B, T, H_M, DH_M) * (DH_M ** -0.5)
    v = vm.astype(F32).reshape(B, T, H_M, DH_M)
    gates = ifm.astype(F32) + p['b_gates'].astype(F32)
    log_i = gates[..., :H_M]
    log_f = jax.nn.log_sigmoid(gates[..., H_M:])
    hm, C, n, m = mlstm_chunkwise(q, k, v, log_i, log_f, C0, n0, m0)
    hm = rmsnorm(hm, p['g_mnorm']) * jax.nn.sigmoid(om.astype(F32)).reshape(B, T, H_M, DH_M)
    ya = o.reshape(B, T, W_VA).astype(h.dtype) @ p['w_up_a']
    yb = hm.reshape(B, T, W_M).astype(h.dtype) @ p['w_up_b']
    y = (jax.nn.sigmoid(ga) * ya + jax.nn.sigmoid(gb) * yb) @ p['w_out']
    return y, (ka, va, new_buf, C, n, m)

def moe(h, p):
    B, T, D = h.shape
    xt = h.reshape(-1, D)
    N = xt.shape[0]
    A = N * TOP_K
    logits = (xt @ p['w_router']).astype(F32) + p['b_router'].astype(F32)
    topv, topi = lax.top_k(logits, TOP_K)
    wts = jax.nn.softmax(topv, axis=-1)
    flat_e = topi.reshape(-1).astype(jnp.int32)
    flat_tok = jnp.repeat(jnp.arange(N, dtype=jnp.int32), TOP_K)
    flat_w = wts.reshape(-1)
    order = jnp.argsort(flat_e)
    se = flat_e[order]
    counts = jnp.bincount(flat_e, length=N_EXP)
    padded = (counts + MOE_BLOCK - 1) // MOE_BLOCK * MOE_BLOCK
    pad_end = jnp.cumsum(padded)
    pad_start = pad_end - padded
    start = jnp.cumsum(counts) - counts
    dest = pad_start[se] + jnp.arange(A, dtype=jnp.int32) - start[se]
    nblk = -(-(A + N_EXP * (MOE_BLOCK - 1)) // MOE_BLOCK)
    P = nblk * MOE_BLOCK
    tok_slot = jnp.full((P,), N, jnp.int32).at[dest].set(flat_tok[order])
    w_slot = jnp.zeros((P,), F32).at[dest].set(flat_w[order])
    blk_exp = jnp.minimum(jnp.searchsorted(pad_end, jnp.arange(nblk) * MOE_BLOCK, side='right'), N_EXP - 1)
    xpad = jnp.concatenate([xt, jnp.zeros((1, D), xt.dtype)], axis=0)

    def run(args):
        tok, w, e = args
        xb = xpad[tok]
        gu = xb @ p['w_gu'][e] + p['b_gu'][e]
        gate = jnp.minimum(gu[:, :D_FF], SWIGLU_LIMIT)
        up = jnp.clip(gu[:, D_FF:], -SWIGLU_LIMIT, SWIGLU_LIMIT)
        act = (up + 1.0) * gate * jax.nn.sigmoid(SWIGLU_ALPHA * gate)
        return (act @ p['w_down'][e] + p['b_down'][e]).astype(F32) * w[:, None]

    yb = lax.map(run, (tok_slot.reshape(nblk, MOE_BLOCK), w_slot.reshape(nblk, MOE_BLOCK), blk_exp))
    out = jnp.zeros((N + 1, D), F32).at[tok_slot].add(yb.reshape(P, D))
    return out[:N].astype(h.dtype).reshape(B, T, D)

def layer(x, c, p, lam_init, pos, past, conv_buf, C0, n0, m0):
    mod = (jax.nn.silu(c) @ p['w_ada'] + p['b_ada'])[:, None, :]
    sh1, sc1, gt1, sh2, sc2, gt2 = jnp.split(mod, 6, axis=-1)
    h = rmsnorm(x, p['g_norm1']) * (1.0 + sc1) + sh1
    y, st = mixer(h, p, lam_init, pos, past, conv_buf, C0, n0, m0)
    x = x + gt1 * y
    h = rmsnorm(x, p['g_norm2']) * (1.0 + sc2) + sh2
    x = x + gt2 * moe(h, p)
    return x, st

def setup_inputs(seed: int = 0) -> dict:
    key = jax.random.key(seed)
    ks = iter(jax.random.split(key, 48))
    n_pages = PAST_LEN // PAGE_SIZE
    n_pool = (5 * DEC_BATCH * n_pages + 3) // 4

    def nrm(shape, s):
        return jax.random.normal(next(ks), shape, F32) * s

    perm = jax.random.permutation(next(ks), n_pool)[: DEC_BATCH * n_pages]
    b_gates = jnp.concatenate([
        nrm((DEPTH, H_M), 0.1),
        jnp.broadcast_to(jnp.linspace(3.0, 6.0, H_M, dtype=F32), (DEPTH, H_M)) + nrm((DEPTH, H_M), 0.01)], axis=-1)
    return {
        'x_prompt': nrm((BATCH, SEQ, D_MODEL), 1.0),
        'x_sample': nrm((DEC_BATCH, DEC_SEQ, D_MODEL), 1.0),
        'c_prompt': nrm((BATCH, D_MODEL), 1.0),
        'c_sample': nrm((DEC_BATCH, D_MODEL), 1.0),
        'cache_k': nrm((DEPTH, n_pool, PAGE_SIZE, H_A, 2, DK_A), 1.0),
        'cache_v': nrm((DEPTH, n_pool, PAGE_SIZE, H_A, DV_A), 1.0),
        'state_conv': nrm((DEPTH, DEC_BATCH, CONV_W - 1, 2 * W_M), 1.0),
        'state_C': nrm((DEPTH, DEC_BATCH, H_M, DH_M, DH_M), 0.05),
        'state_n': nrm((DEPTH, DEC_BATCH, H_M, DH_M), 0.05),
        'state_m': nrm((DEPTH, DEC_BATCH, H_M), 0.5),
        'page_table': perm.reshape(DEC_BATCH, n_pages).astype(jnp.int32),
        'w_ada': nrm((DEPTH, D_MODEL, 6 * D_MODEL), 0.5 * D_MODEL ** -0.5),
        'b_ada': nrm((DEPTH, 6 * D_MODEL), 0.01),
        'g_norm1': 1.0 + nrm((DEPTH, D_MODEL), 0.02),
        'g_norm2': 1.0 + nrm((DEPTH, D_MODEL), 0.02),
        'w_in': nrm((DEPTH, D_MODEL, D_IN), D_MODEL ** -0.5),
        'b_gates': b_gates,
        'lambda_q1': nrm((DEPTH, DK_A), 0.1),
        'lambda_k1': nrm((DEPTH, DK_A), 0.1),
        'lambda_q2': nrm((DEPTH, DK_A), 0.1),
        'lambda_k2': nrm((DEPTH, DK_A), 0.1),
        'g_subln': 1.0 + nrm((DEPTH, DV_A), 0.02),
        'w_conv': nrm((DEPTH, CONV_W, 2 * W_M), CONV_W ** -0.5),
        'b_conv': nrm((DEPTH, 2 * W_M), 0.01),
        'g_mnorm': 1.0 + nrm((DEPTH, H_M, DH_M), 0.02),
        'w_up_a': nrm((DEPTH, W_VA, D_MODEL), W_VA ** -0.5),
        'w_up_b': nrm((DEPTH, W_M, D_MODEL), W_M ** -0.5),
        'w_out': nrm((DEPTH, D_MODEL, D_MODEL), D_MODEL ** -0.5),
        'w_router': nrm((DEPTH, D_MODEL, N_EXP), D_MODEL ** -0.5),
        'b_router': nrm((DEPTH, N_EXP), 0.01),
        'w_gu': nrm((DEPTH, N_EXP, D_MODEL, 2 * D_FF), D_MODEL ** -0.5),
        'b_gu': nrm((DEPTH, N_EXP, 2 * D_FF), 0.01),
        'w_down': nrm((DEPTH, N_EXP, D_FF, D_MODEL), D_FF ** -0.5),
        'b_down': nrm((DEPTH, N_EXP, D_MODEL), 0.01),
        'g_final': 1.0 + nrm((D_MODEL,), 0.02),
    }

def reference(x_prompt, x_sample, c_prompt, c_sample, cache_k, cache_v, state_conv, state_C, state_n, state_m,
              page_table, w_ada, b_ada, g_norm1, g_norm2, w_in, b_gates, lambda_q1, lambda_k1, lambda_q2, lambda_k2,
              g_subln, w_conv, b_conv, g_mnorm, w_up_a, w_up_b, w_out, w_router, b_router, w_gu, b_gu, w_down,
              b_down, g_final):
    B, S, _ = x_prompt.shape
    Bd, Td, _ = x_sample.shape
    past_len = page_table.shape[1] * PAGE_SIZE
    pos_p = jnp.arange(S, dtype=jnp.int32)
    pos_s = past_len + jnp.arange(Td, dtype=jnp.int32)
    hp, hs = x_prompt, x_sample
    kp_l, vp_l, bp_l, Cp_l, np_l, mp_l = [], [], [], [], [], []
    ks_l, vs_l, bs_l, Cs_l, ns_l, ms_l = [], [], [], [], [], []
    for l in range(DEPTH):
        p = dict(w_ada=w_ada[l], b_ada=b_ada[l], g_norm1=g_norm1[l], g_norm2=g_norm2[l], w_in=w_in[l],
                 b_gates=b_gates[l], lambda_q1=lambda_q1[l], lambda_k1=lambda_k1[l], lambda_q2=lambda_q2[l],
                 lambda_k2=lambda_k2[l], g_subln=g_subln[l], w_conv=w_conv[l], b_conv=b_conv[l],
                 g_mnorm=g_mnorm[l], w_up_a=w_up_a[l], w_up_b=w_up_b[l], w_out=w_out[l], w_router=w_router[l],
                 b_router=b_router[l], w_gu=w_gu[l], b_gu=b_gu[l], w_down=w_down[l], b_down=b_down[l])
        lam_init = 0.8 - 0.6 * math.exp(-0.3 * l)
        hp, (kp, vp, bp, Cp, np_, mp) = layer(
            hp, c_prompt, p, lam_init, pos_p, None,
            jnp.zeros((B, CONV_W - 1, 2 * W_M), hp.dtype), jnp.zeros((B, H_M, DH_M, DH_M), F32),
            jnp.zeros((B, H_M, DH_M), F32), jnp.zeros((B, H_M), F32))
        past = (cache_k[l][page_table].reshape(Bd, past_len, H_A, 2, DK_A),
                cache_v[l][page_table].reshape(Bd, past_len, H_A, DV_A))
        hs, (ksn, vsn, bsn, Csn, nsn, msn) = layer(
            hs, c_sample, p, lam_init, pos_s, past, state_conv[l], state_C[l], state_n[l], state_m[l])
        kp_l.append(kp); vp_l.append(vp); bp_l.append(bp); Cp_l.append(Cp); np_l.append(np_); mp_l.append(mp)
        ks_l.append(ksn); vs_l.append(vsn); bs_l.append(bsn); Cs_l.append(Csn); ns_l.append(nsn); ms_l.append(msn)
    y_prompt = rmsnorm(hp, g_final)
    y_sample = rmsnorm(hs, g_final)
    return (y_prompt, y_sample,
            jnp.stack(kp_l), jnp.stack(vp_l), jnp.stack(bp_l), jnp.stack(Cp_l), jnp.stack(np_l), jnp.stack(mp_l),
            jnp.stack(ks_l), jnp.stack(vs_l), jnp.stack(bs_l), jnp.stack(Cs_l), jnp.stack(ns_l), jnp.stack(ms_l))


_drawn_inputs = setup_inputs


def setup_inputs(seed=0):
    import zlib

    import numpy as np

    out = dict(_drawn_inputs(seed))
    spreads = {}
    factors = {'g_norm2': 3.003,
     'lambda_q2': 8.0,
     'lambda_k2': 6.34,
     'g_subln': 8.0,
     'b_conv': 3.433,
     'g_mnorm': 8.0,
     'b_router': 6.78,
     'b_gu': 8.0,
     'b_down': 58.91,
     'g_final': 8.68}
    for name, (base, spread) in spreads.items():
        noise = np.random.default_rng([zlib.crc32(name.encode()), seed]).standard_normal(out[name].shape)
        drawn = base * np.exp(spread * noise) if base else spread * noise
        out[name] = __import__('jax').numpy.asarray(drawn.astype(out[name].dtype))
    for name, factor in factors.items():
        out[name] = (out[name] * factor).astype(out[name].dtype)
    return out
```

```python
from contextlib import ExitStack

import concourse.bass as bass
import numpy as np
from concourse import mybir

F32 = mybir.dt.float32
I32 = mybir.dt.int32
U32 = mybir.dt.uint32
ALU = mybir.AluOpType
ACT = mybir.ActivationFunctionType
AX = mybir.AxisListType.X

P = 128
D = 1024
KT = D // P
TP = 256
NB, TD = 8, 8
TS = NB * TD
NT = TP + TS
TILES = [(0, 128), (128, 128), (256, 64)]
H = 4
DK = 64
PAGES, PAGE = 8, 128
N_POOL = 80
NE = 32
TOPK = 4
FF = 1024
EPS = 1e-6
LAM_INIT = 0.8 - 0.6
LIMIT, ALPHA = 7.0, 1.702
BIG = -1e30
RING = 6
REGION = 18120
UNIT = 4096
NARROW, WIDE = 64, 128
ROUNDS = 3
MAX_MORE = 16
AT_COUNT = 64
AT_COLUMN = AT_COUNT + NE
AT_EXPERT = AT_COLUMN + MAX_MORE
AT_MORE = AT_EXPERT + MAX_MORE


def const_pack():
    cols, at, n = [], {}, 0

    def put(name, a):
        nonlocal n
        full = np.zeros((P, a.shape[1]), np.float32)
        full[:a.shape[0]] = a
        at[name] = (n, a.shape[1])
        cols.append(full)
        n += a.shape[1]

    i = np.arange(P)
    le = (i[:, None] <= i[None, :]).astype(np.float32)
    s = np.arange(TS)
    blk = ((s[:, None] // TD == s[None, :] // TD) & (s[:, None] <= s[None, :])).astype(np.float32)
    blk128 = np.zeros((P, TS), np.float32)
    blk128[:TS] = blk
    put("ident", np.eye(P, dtype=np.float32))
    put("causal", np.concatenate([le, np.ones((P, P), np.float32), le, blk128], 1))
    put("before", (i[:, None] < i[None, :]).astype(np.float32))
    put("iota", np.tile(i.astype(np.float32), (P, 1)))
    put("valid", np.stack([np.ones(P), np.ones(P), i < TS], 1).astype(np.float32))
    put("blkind", (s[:, None] // TD == np.arange(NB)[None, :]).astype(np.float32))
    put("more", np.stack([np.repeat(np.arange(1, ROUNDS) * WIDE, NE) + 0.5,
                          NE + np.arange(NE * (ROUNDS - 1)), np.tile(np.arange(NE), ROUNDS - 1)],
                         1).astype(np.float32))
    keep = n
    put("attmask", np.concatenate([np.zeros((P, P)), np.where(i[None, :] <= i[:, None], 0, BIG)],
                                  1).astype(np.float32))
    r = np.arange(2 * H * TD)
    key = s
    ok = (key[None, None, :] // TD == np.arange(NB)[None, :, None]) & \
         (key[None, None, :] % TD <= (r % TD)[:, None, None])
    put("newmask", np.where(ok, 0, BIG).astype(np.float32).reshape(len(r), -1))
    pos = np.concatenate([np.arange(TP), PAGES * PAGE + np.arange(TS) % TD]).astype(np.float32)
    inv = np.float32(10000.0) ** (-np.arange(DK // 2, dtype=np.float32) * np.float32(2.0) / np.float32(DK))
    ang = pos[:, None] * inv[None, :].astype(np.float32)
    for name, f in (("cos", np.cos), ("sin", np.sin)):
        t = np.zeros((P, 3, DK // 2), np.float32)
        for j, (t0, m) in enumerate(TILES):
            t[:m, j] = f(ang[t0:t0 + m])
        put(name, t.reshape(P, -1))
    put("comp", np.stack([(r // TD) % 2 == 0, (r // TD) % 2 == 1], 1).astype(np.float32))
    sel = np.zeros((H, H, P), np.float32)
    for h in range(H):
        sel[h, h] = 1
    put("hsel", sel.reshape(H, -1))
    start = np.zeros(NT, bool)
    start[[0] + [TP + TD * b for b in range(NB)]] = True
    put("carry", np.tile(np.where(start, 0, 1).astype(np.float32), (H, 1)))
    put("drop", np.tile(np.where(start, BIG, 0).astype(np.float32), (H, 1)))
    return np.concatenate(cols, 1), at, keep


def build(nc, I, O, const_at, n_const, n_keep):
    ctx = ExitStack()
    with ctx:
        def sb(name, shape, dt=F32):
            return ctx.enter_context(nc.sbuf_tensor(name, shape, dt))

        def sem(name):
            return ctx.enter_context(nc.semaphore(name))

        ring = sb("ring", [P, RING, UNIT])
        xT = sb("xT", [P, KT, NT])
        hT = sb("hT", [P, KT, NT])
        keep = sb("keep", [P, n_keep])
        vecT = sb("vecT", [P, 128])
        gu_biasT = sb("gu_biasT", [P, NE * 16])
        modT = sb("modT", [P, 48, 9])
        gainT = sb("gainT", [P, 2, KT, 9])
        rstd = sb("rstd", [P, NT])
        cT = sb("cT", [P, KT, 9])
        small = sb("small", [P, 64])
        oT = sb("oT", [P, H, NT])
        hmT = sb("hmT", [P, H, NT])
        region = sb("region", [P, REGION])
        ints = sb("ints", [1, AT_MORE + 8], I32)
        psum = ctx.enter_context(nc.psum_tensor("psum", [P, 8, 512], F32))

        def const(name, rows=P):
            a, m = const_at[name]
            if a + m <= n_keep:
                return keep[0:rows, a:a + m]
            return front_const[0:rows, a - n_keep:a - n_keep + m]

        class Area:
            def __init__(self, start):
                self.at = start

            def take(self, *shape):
                m = int(np.prod(shape))
                v = region[:, self.at:self.at + m]
                self.at += m
                assert self.at <= REGION, self.at
                if len(shape) == 2:
                    v = v.rearrange("p (a b) -> p a b", a=shape[0])
                if len(shape) == 3:
                    v = v.rearrange("p (a b c) -> p a b c", a=shape[0], b=shape[1])
                return v

        front_area = Area(0)
        front_const = front_area.take(n_const - n_keep)
        A = Area(front_area.at)
        va = A.take(3, 512)
        qT = A.take(H, NT)
        kT = A.take(H, NT)
        q_rot = A.take(2, 512)
        k_rot = A.take(3, 512)
        pairs = A.take(H, 256)
        q_blocks = A.take(NB, H * 64)
        kTb = A.take(H, PAGES * PAGE)
        B = Area(A.at - H * PAGES * PAGE)
        x_tok = B.take(3, D)
        c_rows = B.take(D)
        B = Area(A.at - H * PAGES * PAGE)
        s_pair = B.take(2, 2, 256)
        aT = B.take(2, 256)
        x_sq = Area(front_area.at).take(KT, NT)
        c_sig = q_rot.rearrange("p a b -> p (a b)")
        vec_rows = k_rot[:, 0, 0:P]
        bgu_rows = q_blocks.rearrange("p a b -> p (a b)")[:, 0:512].rearrange("p (a b) -> p a b", a=4)
        lam_rows = k_rot[:, 1, 0:256].rearrange("p (a b) -> p a b", a=4)
        p_dec = A.take(PAGES * PAGE + TS)
        pT_dec = A.take(PAGES, 64)
        pTn = A.take(64)
        s_new = A.take(64)
        o_sq = Area(front_area.at).take(H, NT)
        o_rms = Area(front_area.at + H * NT).take(H, NT)
        M = Area(front_area.at)
        raw_p = M.take(8, TP + 3)
        raw_s = M.take(8, NB, 11)
        cv = M.take(8, NT)
        cv_sig = M.take(H, NT)
        vm = M.take(3, 512)
        so = M.take(H, NT)
        rowsR = M.take(704)
        rows_u = M.take(NT)
        rows_w = M.take(NT)
        rows_f = M.take(NT)
        rows_li = M.take(NT)
        rows_t = M.take(NT)
        w_if = M.take(KT, 8)
        uw = M.take(3, 8)
        dT = M.take(448)
        bcS = M.take(384)
        qe = M.take(2, 64)
        kw = M.take(3, P)
        v_blk = M.take(NB, P)
        hr = M.take(H, NT)
        hsq = M.take(NT)
        den_s = rstd[:]
        C_p = cv_sig.rearrange("p a b -> p (a b)")[:, 0:512].rearrange("p (a b) -> p a b", a=H)
        tail = dT[:, 0:216].rearrange("p (a b) -> p a b", a=8)
        tail_rows = raw_p.rearrange("p a b -> p (a b)")[:, 0:D]
        n0T = M.take(32)
        nT = M.take(36)
        n_rows = M.take(P)
        cs_rows = cv.rearrange("p a b -> p (a b)")[:, 0:D]
        G = Area(front_area.at)
        sg = G.take(KT, NT)
        mT = G.take(KT, NT)
        E = Area(0)
        h2_tok = E.take(3, D)
        accT = E.take(KT, NT)
        fin_sq = Area(E.at).take(KT, NT)
        act_g = E.take(H, P)
        act_u = E.take(H, P)
        act_s = E.take(H, P)
        actT = E.take(KT, P)
        hgT = E.take(KT, P)
        yT = E.take(KT, P)
        y_rows = E.take(D)
        sel = E.take(3, P)
        selw = E.take(3, P)
        selwT = E.take(NT)
        bias_e = E.take(16)
        logits = E.take(3, NE)
        mask = E.take(3, NE)
        wts = E.take(3, NE)
        eq = E.take(3, NE)
        eqw = E.take(3, NE)
        pos = E.take(3, ROUNDS * NE)
        wts3 = E.take(3, ROUNDS * NE)
        top8 = E.take(3, 8)
        idxf = E.take(3, 8)
        ew = E.take(3, 4)
        esum = E.take(3)
        b_rt = E.take(NE)
        w_rt = E.take(KT, NE)
        wT = E.take(NT)
        bd_rows = E.take(D)
        more = E.take(3 + 3 * MAX_MORE)
        y_out = h2_tok
        top_ix = sb("top_ix", [P, 3, 8], U32)

        V_ADA, V_G1, V_G2, V_GF, V_WC, V_BC, V_GS, V_GM = 0, 48, 56, 64, 72, 104, 112, 113

        LAM, NLAM, COEF, GS = small[:, 0:4], small[:, 4:5], small[:, 5:6], small[:, 6:7]
        MX, LS, RC = small[:, 8:12], small[:, 12:16], small[:, 16:20]
        M0 = small[0:H, 20:29]
        BG = small[0:H, 29:31]
        SC = small[:, 32:40]

        bank_full = [sem(f"bank_full{i}") for i in range(8)]
        bank_free = [sem(f"bank_free{i}") for i in range(8)]
        unit_landed = [sem(f"unit_landed{i}") for i in range(RING)]
        const_in = sem("const_in")
        x_in = sem("x_in")
        c_in = sem("c_in")
        vec_in = sem("vec_in")
        table_in = sem("table_in")
        mrows_in = sem("mrows_in")
        moe_in = sem("moe_in")
        dve_step = sem("dve_step")
        act_step = sem("act_step")
        pool_step = sem("pool_step")
        unit_used = sem("unit_used")
        c_sig_done = sem("c_sig_done")
        c_silu = sem("c_silu")
        x_squared = sem("x_squared")
        lam_dot = sem("lam_dot")
        lam_exp = sem("lam_exp")
        h_ready = sem("h_ready")
        rotated = sem("rotated")
        k_stored = sem("k_stored")
        q_blocked = sem("q_blocked")
        att_max = sem("att_max")
        att_exp = sem("att_exp")
        att_a = sem("att_a")
        dec_max = sem("dec_max")
        dec_exp = sem("dec_exp")
        dec_p = sem("dec_p")
        o_squared = sem("o_squared")
        o_ready = sem("o_ready")
        region_m = sem("region_m")
        conv_done = sem("conv_done")
        conv_sig = sem("conv_sig")
        conv_ready = sem("conv_ready")
        tail_ready = sem("tail_ready")
        tail_out = sem("tail_out")
        f_abs = sem("f_abs")
        f_ln = sem("f_ln")
        m_rows = sem("m_rows")
        m_exp = sem("m_exp")
        d_ready = sem("d_ready")
        d_exp = sem("d_exp")
        p_ready = sem("p_ready")
        qe_ready = sem("qe_ready")
        kw_ready = sem("kw_ready")
        h_squared = sem("h_squared")
        hm_ready = sem("hm_ready")
        c_ready = sem("c_ready")
        state_out = sem("state_out")
        merged = sem("merged")
        x1_ready = sem("x1_ready")
        x1_squared = sem("x1_squared")
        h2_ready = sem("h2_ready")
        top_diff = sem("top_diff")
        top_exp = sem("top_exp")
        routed = sem("routed")
        more_flags = sem("more_flags")
        more_hot = sem("more_hot")
        tables = sem("tables")
        mean_inverse = sem("mean_inverse")
        mean_root = sem("mean_root")
        page_in = sem("page_in")
        tail_step = sem("tail_step")
        moe_start = sem("moe_start")
        pad_ready = sem("pad_ready")
        gu_half = [sem("guA_half"), sem("guB_half")]
        gu_done = [sem("guA_done"), sem("guB_done")]
        gu_taken = [sem("guA_taken"), sem("guB_taken")]
        gate_ready = sem("gate_ready")
        gate_sig = sem("gate_sig")
        act_ready = sem("act_ready")
        down_half = sem("down_half")
        down_done = sem("down_done")
        sel_ready = sem("sel_ready")
        gathered = sem("gathered")
        hg_copied = sem("hg_copied")
        selw_ready = sem("selw_ready")
        selw_turned = sem("selw_turned")
        selw_copied = sem("selw_copied")
        yT_copied = sem("yT_copied")
        y_turned = sem("y_turned")
        y_copied = sem("y_copied")
        combined = sem("combined")
        added = sem("added")
        acc_final = sem("acc_final")
        x2_ready = sem("x2_ready")
        x2_squared = sem("x2_squared")
        y_stored = sem("y_stored")

        groups, used, turn = {}, [0] * 8, {}

        def claim(pe, pool, *key):
            k = turn.get(pool, 0)
            turn[pool] = k + 1
            b = pool[k % len(pool)]
            if used[b]:
                pe.wait_ge(bank_free[b], used[b])
            used[b] += 1
            groups[key] = (b, used[b])
            return psum[:, b, :]

        def bank(*key):
            return psum[:, groups[key][0], :]

        def full(*key):
            return bank_full[groups[key][0]], groups[key][1]

        def full_sem(*key):
            return bank_full[groups[key][0]]

        def drained(*key):
            return bank_free[groups[key][0]], groups[key][1]

        def free_sem(*key):
            return bank_free[groups[key][0]]

        units, last_use, ada_used = [], {}, [0]

        def next_used():
            ada_used[0] += 1
            return ada_used[0]

        def add_unit(name, n_dma=1):
            units.append((name, n_dma))

        for i in range(4):
            add_unit(("ada", i))
        for w in "qkv":
            add_unit((w, 0))
        for b in range(NB):
            add_unit(("K", b), PAGES)
            add_unit(("V", b), PAGES)
        for w in ("qm", "km", "vm", "om"):
            add_unit((w, 0))
        for i in range(4, 12):
            add_unit(("ada", i))
        add_unit(("C", 0))
        for w in ("ga0", "ga1", "upa", "gb0", "gb1", "upb", "wo0", "wo1"):
            add_unit((w, 0))
        slot_of, landed_at, count = {}, {}, [0] * RING
        for i, (name, n_dma) in enumerate(units):
            s = i % RING
            count[s] += 16 * n_dma
            slot_of[name], landed_at[name] = s, count[s]
        first_slot = len(units) % RING
        moe_slot = [(first_slot + i) % RING for i in range(RING)]
        landed_base = [count[moe_slot[i]] for i in range(RING)]

        def unit(name, a, b=None):
            v = ring[:, slot_of[name], :]
            return v.rearrange("p (a b) -> p a b", a=a)

        def landed(name):
            return unit_landed[slot_of[name]], landed_at[name]

        W_IN = I["w_in"]
        PIECE = {"q": 0, "k": 512, "v": 1024, "qm": 1536, "km": 2048, "vm": 2560, "om": 3072,
                 "ga0": 3592, "ga1": 4104, "gb0": 4616, "gb1": 5128}

        def unit_source(name):
            w, i = name
            if w == "ada":
                return I["w_ada"].rearrange("(k p) c -> p k c", p=P)[:, :, 512 * i:512 * (i + 1)], 8
            if w in PIECE:
                return W_IN.rearrange("(k p) c -> p k c", p=P)[:, :, PIECE[w]:PIECE[w] + 512], 8
            if w in ("upa", "upb"):
                return I["w_up_a" if w == "upa" else "w_up_b"].rearrange("(k p) c -> p k c", p=P), 4
            if w in ("wo0", "wo1"):
                k = 4 * int(w[2])
                return I["w_out"].rearrange("(k p) c -> p k c", p=P)[:, k:k + 4, :], 4
            assert w == "C"
            return I["state_C"].rearrange("b h d e -> d (b h) e"), 32

        GA = psum[:, 0:2, :]
        GB = psum[:, 2:4, :]
        BANK_P, BANK_Q = (4, 5), (6, 7)

        block = ctx.enter_context(nc.Block())

        @block.tensor
        def _(pe):
            def mm(out, lhsT, rhs, start, stop):
                return pe.matmul(out, lhsT, rhs, start=start, stop=stop, skip_group_check=True)

            ident = const("ident")
            ones = const("causal")[:, P:2 * P]
            LOW, HIGH, ALLB = (0, 1, 2, 3), (4, 5, 6, 7), (0, 1, 2, 3, 4, 5, 6, 7)

            pe.wait_ge(const_in, 16)
            pe.wait_ge(vec_in, 16 * 9)
            out = claim(pe, ALLB, "vec")
            pe.transpose(out[:, 0:117], vec_rows[0:117, :], ident[0:117, 0:117]).then_inc(full_sem("vec"), 1)
            pe.wait_ge(c_silu, 1)
            out = claim(pe, ALLB, "cT")
            for k in range(KT):
                last = pe.transpose(out[:, 9 * k:9 * k + 9], c_rows[0:9, P * k:P * k + P], ident[0:9, 0:9])
            last.then_inc(full_sem("cT"), 1)
            pe.wait_ge(table_in, 16 * 11)
            out = claim(pe, ALLB, "bgu")
            for t in range(4):
                last = pe.transpose(out[:, P * t:P * t + P], bgu_rows[:, t, :], ident)
            last.then_inc(full_sem("bgu"), 1)
            pe.wait_ge(x_in, 48)
            for j, (t0, n) in enumerate(TILES):
                for half in range(2):
                    out = claim(pe, ALLB, "xT", j, half)
                    for i in range(4):
                        k = 4 * half + i
                        last = pe.transpose(out[:, P * i:P * i + n], x_tok[0:n, j, P * k:P * k + P],
                                            ident[0:n, 0:n])
                    last.then_inc(full_sem("xT", j, half), 1)
            pe.wait_ge(x_squared, 1)
            out = claim(pe, ALLB, "ss1")
            for k in range(KT):
                last = mm(out[:, 0:NT], ones, x_sq[:, k, :], k == 0, k == KT - 1)
            last.then_inc(full_sem("ss1"), 1)

            def ada(i0, i1, key):
                out = claim(pe, ALLB, key)
                for i in range(i0, i1):
                    pe.wait_ge(*landed(("ada", i)))
                    w = unit(("ada", i), 8)
                    for m in range(4):
                        c = 9 * (4 * (i - i0) + m)
                        for k in range(KT):
                            last = mm(out[:, c:c + 9], w[:, k, P * m:P * m + P], cT[:, k, :],
                                      k == 0, k == KT - 1)
                    if i < i1 - 1:
                        last.then_inc(unit_used, 1)
                        last_use[("ada", i)] = (unit_used, next_used())
                last.then_inc(full_sem(key), 1)
                last_use[("ada", i1 - 1)] = full(key)

            pe.wait_ge(*drained("cT"))
            ada(0, 4, "ada0")

            pe.wait_ge(h_ready, 1)

            def token_major(name, pool, after=None):
                pe.wait_ge(*landed((name, 0)))
                w = unit((name, 0), 8)
                for j, (t0, n) in enumerate(TILES):
                    out = claim(pe, pool, name, j)
                    for k in range(KT):
                        last = mm(out[0:n, :], hT[:, k, t0:t0 + n], w[:, k, :], k == 0, k == KT - 1)
                    last.then_inc(full_sem(name, j), 1)
                    if after:
                        after(j)
                last_use[(name, 0)] = full(name, 2)

            def turn_heads(name, j):
                t0, n = TILES[j]
                pe.wait_ge(rotated, (0 if name == "q" else 3) + j + 1)
                out = claim(pe, HIGH, name + "T", j)
                src = q_rot[:, j % 2, :] if name == "q" else k_rot[:, j, :]
                for h in range(H):
                    last = pe.transpose(out[:, P * h:P * h + n], src[0:n, P * h:P * h + P], ident[0:n, 0:n])
                last.then_inc(full_sem(name + "T", j), 1)

            token_major("q", LOW)
            turn_heads("q", 0)
            token_major("k", LOW, lambda j: turn_heads("q", j + 1) if j < 2 else None)
            token_major("v", LOW, lambda j: turn_heads("k", j))

            items = [(h, qb) for h in range(H) for qb in range(2)]

            def att_scores(i):
                h, qb = items[i]
                for c in range(2):
                    out = claim(pe, LOW, "S", i, c)
                    mm(out[:, 0:P * (qb + 1)], qT[DK * c:DK * c + DK, h, P * qb:P * qb + P],
                       kT[DK * c:DK * c + DK, h, 0:P * (qb + 1)], True, True).then_inc(full_sem("S", i, c), 1)

            for w in "qk":
                for j in range(3):
                    pe.wait_ge(*drained(w + "T", j))
            for j in range(3):
                pe.wait_ge(*drained("v", j))
            att_scores(0)
            for i, (h, qb) in enumerate(items):
                if i + 1 < len(items):
                    att_scores(i + 1)
                pe.wait_ge(att_a, i + 1)
                out = claim(pe, (4, 5), "aT", i)
                for t in range(qb + 1):
                    last = pe.transpose(out[:, P * t:P * t + P], s_pair[:, i % 2, 0, P * t:P * t + P], ident)
                last.then_inc(full_sem("aT", i), 1)
                out = claim(pe, (6, 7), "PV", i)
                pe.wait_ge(*drained("aT", i))
                for t in range(qb + 1):
                    last = mm(out[:, 0:P], va[:, t, P * h:P * h + P], aT[:, i % 2, P * t:P * t + P],
                              t == 0, t == qb)
                last.then_inc(full_sem("PV", i), 1)

            def turn_keys(b):
                pe.wait_ge(*landed(("K", b)))
                kc = unit(("K", b), PAGES)
                for g in range(PAGES):
                    out = claim(pe, LOW, "kTb", b, g)
                    for h in range(H):
                        last = pe.transpose(out[:, P * h:P * h + P], kc[:, g, P * h:P * h + P], ident)
                    last.then_inc(full_sem("kTb", b, g), 1)
                last_use[("K", b)] = full("kTb", b, PAGES - 1)

            pe.wait_ge(q_blocked, 1)
            turn_keys(0)
            for b in range(NB):
                for half in range(2):
                    out = claim(pe, (4 + half,), "Sd", b, half)
                    for g in range(4 * half, 4 * half + 4):
                        pe.wait_ge(*drained("kTb", b, g))
                    for h in range(H):
                        last = mm(out[0:64, :], q_blocks[:, b, 64 * h:64 * h + 64],
                                  kTb[:, h, 512 * half:512 * half + 512], h == 0, h == H - 1)
                    last.then_inc(full_sem("Sd", b, half), 1)
                out = claim(pe, (6,), "Sn", b)
                for h in range(H):
                    last = mm(out[0:64, 0:TS], q_blocks[:, b, 64 * h:64 * h + 64], kT[:, h, TP:NT],
                              h == 0, h == H - 1)
                last.then_inc(full_sem("Sn", b), 1)
                if b + 1 < NB:
                    turn_keys(b + 1)
                pe.wait_ge(dec_p, b + 1)
                out = claim(pe, (7,), "pT", b)
                for g in range(PAGES):
                    last = pe.transpose(out[:, 64 * g:64 * g + 64], p_dec[0:64, P * g:P * g + P],
                                        ident[0:64, 0:64])
                last.then_inc(full_sem("pT", b), 1)
                out = claim(pe, (6,), "pTn", b)
                pe.transpose(out[0:TS, 0:64], p_dec[0:64, PAGES * PAGE:PAGES * PAGE + TS],
                             ident[0:64, 0:64]).then_inc(full_sem("pTn", b), 1)
                pe.wait_ge(*landed(("V", b)))
                vc = unit(("V", b), PAGES)
                out = claim(pe, LOW, "od", b)
                pe.wait_ge(*drained("pT", b))
                pe.wait_ge(*drained("pTn", b))
                for h in range(H):
                    for g in range(PAGES):
                        mm(out[:, 16 * h:16 * h + 16], vc[:, g, P * h:P * h + P],
                           pT_dec[:, g, 16 * h:16 * h + 16], g == 0, False)
                    last = mm(out[:, 16 * h:16 * h + 16], va[0:TS, 2, P * h:P * h + P],
                              pTn[0:TS, 16 * h:16 * h + 16], False, True)
                last.then_inc(full_sem("od", b), 1)
                last_use[("V", b)] = full("od", b)
            pe.wait_ge(o_squared, 1)
            for h in range(H):
                out = claim(pe, LOW, "oss", h)
                mm(out[:, 0:NT], ones, o_sq[:, h, :], True, True).then_inc(full_sem("oss", h), 1)

            def feature_major(name, key, pool):
                pe.wait_ge(*landed((name, 0)))
                w = unit((name, 0), 8)
                for m in range(4):
                    out = claim(pe, pool, key, m)
                    for k in range(KT):
                        last = mm(out[:, 0:NT], w[:, k, P * m:P * m + P], hT[:, k, :], k == 0, k == KT - 1)
                    last.then_inc(full_sem(key, m), 1)
                last_use[(name, 0)] = full(key, 3)

            feature_major("qm", "qm", ALLB)
            feature_major("km", "km", ALLB)
            pe.wait_ge(mrows_in, 48)
            for r, key in enumerate(("gi", "gf")):
                out = claim(pe, ALLB, key)
                for k in range(KT):
                    last = mm(out[0:H, 0:NT], w_if[:, k, 4 * r:4 * r + 4], hT[:, k, :], k == 0, k == KT - 1)
                last.then_inc(full_sem(key), 1)
            out = claim(pe, ALLB, "cs")
            for m in range(8):
                pe.transpose(out[:, 24 * m:24 * m + 24], cs_rows[0:24, P * m:P * m + P], ident[0:24, 0:24])
            pe.transpose(out[:, 192:224], n_rows[0:32, :], ident[0:32, 0:32]).then_inc(full_sem("cs"), 1)
            token_major("vm", ALLB)
            feature_major("om", "om", ALLB)
            ada(4, 12, "ada1")
            pe.wait_ge(tail_ready, 1)
            for half in range(2):
                out = claim(pe, ALLB, "tail", half)
                for i in range(4):
                    last = pe.transpose(out[0:27, P * i:P * i + P], tail[:, 4 * half + i, :], ident)
                last.then_inc(full_sem("tail", half), 1)
            pe.wait_ge(m_exp, 3)
            out = claim(pe, ALLB, "uw")
            for j, (t0, n) in enumerate(TILES):
                pe.transpose(out[0:n, 8 * j:8 * j + 4], rows_u[0:H, t0:t0 + n], ident[0:H, 0:H])
                last = pe.transpose(out[0:n, 8 * j + 4:8 * j + 8], rows_w[0:H, t0:t0 + n], ident[0:H, 0:H])
            last.then_inc(full_sem("uw"), 1)
            pe.wait_ge(conv_ready, 2)
            hsel = const("hsel").rearrange("p (h m) -> p h m", h=H)
            pe.wait_ge(*landed(("C", 0)))
            c0 = unit(("C", 0), 32)
            for j in range(3):
                pe.wait_ge(*drained("vm", j))
            for h in range(H):
                cq, ck = cv[:, h, :], cv[:, 4 + h, :]
                out = claim(pe, ALLB, "bc0", h)
                mm(out[:, 0:NT], hsel[0:H, h, :], rowsR[0:H, 0:NT], True, True).then_inc(full_sem("bc0", h), 1)
                out = claim(pe, ALLB, "bc1", h)
                mm(out[:, 0:384], hsel[0:H, h, :], rowsR[0:H, NT:704], True, True)\
                    .then_inc(full_sem("bc1", h), 1)
                out = claim(pe, ALLB, "st", h)
                mm(out[:, 0:256], ck[:, 0:P], cq[:, 0:TP], True, True)
                mm(out[:, 256:384], ck[:, P:TP], cq[:, P:TP], True, True)
                mm(out[0:TS, 384:448], ck[:, TP:NT], cq[:, TP:NT], True, True).then_inc(full_sem("st", h), 1)
                out = claim(pe, ALLB, "kt", h)
                for j, (t0, n) in enumerate(TILES):
                    last = pe.transpose(out[0:n, P * j:P * j + P], ck[:, t0:t0 + n], ident)
                last.then_inc(full_sem("kt", h), 1)
                pe.wait_ge(kw_ready, h + 1)
                out = claim(pe, ALLB, "C", h)
                for j in range(2):
                    mm(out[:, 0:P], kw[:, j, :], vm[:, j, P * h:P * h + P], j == 0, j == 1)
                for j in range(2):
                    mm(out[:, P:P + 1], kw[:, j, :], ones[:, 0:1], j == 0, j == 1)
                mm(out[:, 130:138], kw[0:TS, 2, :], const("blkind", TS), True, True)\
                    .then_inc(full_sem("C", h), 1)
                for half in range(2):
                    out = claim(pe, ALLB, "Cs", h, half)
                    mm(out[:, :], kw[0:TS, 2, :],
                       v_blk[0:TS, 4 * half:4 * half + 4, :].rearrange("p a b -> p (a b)"),
                       True, True).then_inc(full_sem("Cs", h, half), 1)
                pe.wait_ge(p_ready, h + 1)
                pe.wait_ge(*drained("st", h))
                pe.wait_ge(qe_ready, h + 1)
                out = claim(pe, ALLB, "num", h)
                vh = vm[:, :, P * h:P * h + P]
                mm(out[:, 0:TP], vh[:, 0, :], dT[:, 0:TP], True, False)
                mm(out[:, P:TP], vh[:, 1, :], dT[:, 256:384], False, True)
                mm(out[:, TP:NT], vh[0:TS, 2, :], dT[0:TS, 384:448], False, False)
                for b in range(NB):
                    last = mm(out[:, TP + TD * b:TP + TD * b + TD], c0[:, H * b + h, :],
                              qe[:, 0, TD * b:TD * b + TD], False, True)
                last.then_inc(full_sem("num", h), 1)
                out = claim(pe, ALLB, "den", h)
                mm(out[:, 0:TP], ones, dT[:, 0:TP], True, False)
                mm(out[:, P:TP], ones, dT[:, 256:384], False, True)
                mm(out[:, TP:NT], ones[0:TS, :], dT[0:TS, 384:448], False, False)
                mm(out[:, TP:NT], ones, qe[:, 1, :], False, True).then_inc(full_sem("den", h), 1)
                pe.wait_ge(h_squared, h + 1)
                out = claim(pe, ALLB, "hss", h)
                mm(out[:, 0:NT], ones, hsq, True, True).then_inc(full_sem("hss", h), 1)
            pe.wait_ge(c_ready, H)
            out = claim(pe, ALLB, "n_out")
            pe.transpose(out[0:36, 0:P], nT, ident).then_inc(full_sem("n_out"), 1)

            def up(name, w, src):
                pe.wait_ge(*landed((w, 0)))
                u = unit((w, 0), 4)
                for m in range(KT):
                    out = claim(pe, ALLB, w, m)
                    for k in range(4):
                        last = mm(out[:, 0:NT], u[:, k, P * m:P * m + P], src[:, k, :], k == 0, k == 3)
                    last.then_inc(full_sem(w, m), 1)
                last_use[(w, 0)] = full(w, KT - 1)

            feature_major("ga0", "ga0", ALLB)
            feature_major("ga1", "ga1", ALLB)
            pe.wait_ge(o_ready, 1)
            up("a", "upa", oT)
            feature_major("gb0", "gb0", ALLB)
            feature_major("gb1", "gb1", ALLB)
            pe.wait_ge(hm_ready, 1)
            up("b", "upb", hmT)
            pe.wait_ge(*landed(("wo0", 0)))
            pe.wait_ge(*landed(("wo1", 0)))
            pe.wait_ge(merged, 1)
            for m in range(KT):
                out = claim(pe, ALLB, "wo", m)
                for k in range(KT):
                    w = unit(("wo0" if k < 4 else "wo1", 0), 4)
                    last = mm(out[:, 0:NT], w[:, k % 4, P * m:P * m + P], mT[:, k, :], k == 0, k == KT - 1)
                last.then_inc(full_sem("wo", m), 1)
            last_use[("wo0", 0)] = last_use[("wo1", 0)] = full("wo", KT - 1)

            pe.wait_ge(x1_squared, 1)
            out = claim(pe, ALLB, "ss2")
            for k in range(KT):
                last = mm(out[:, 0:NT], ones, fin_sq[:, k, :], k == 0, k == KT - 1)
            last.then_inc(full_sem("ss2"), 1)
            pe.wait_ge(h2_ready, 1)
            pe.wait_ge(moe_in, 48)
            out = claim(pe, ALLB, "logit")
            for j, (t0, n) in enumerate(TILES):
                for k in range(KT):
                    last = mm(out[0:n, NE * j:NE * j + NE], hT[:, k, t0:t0 + n], w_rt[:, k, :],
                              k == 0, k == KT - 1)
            last.then_inc(full_sem("logit"), 1)
            for j, (t0, n) in enumerate(TILES):
                for half in range(2):
                    out = claim(pe, ALLB, "h2", j, half)
                    for i in range(4):
                        last = pe.transpose(out[0:n, P * i:P * i + P], hT[:, 4 * half + i, t0:t0 + n], ident)
                    last.then_inc(full_sem("h2", j, half), 1)
            pe.wait_ge(routed, 1)
            out = claim(pe, ALLB, "pos")
            for j in range(3):
                for i in range(j + 1):
                    mm(out[:, NE * j:NE * j + NE], const("before") if i == j else ones, mask[:, i, :],
                       i == 0, i == j)
            for i in range(3):
                mm(out[:, 96:128], ones, mask[:, i, :], i == 0, i == 2)
            for r in range(ROUNDS - 1):
                for i in range(3):
                    last = mm(out[NE * r:NE * r + NE, 128:129], mask[:, i, :], ones[:, 0:1], i == 0, i == 2)
            last.then_inc(full_sem("pos"), 1)
            out = claim(pe, ALLB, "wT")
            for j, (t0, n) in enumerate(TILES):
                last = pe.transpose(out[0:NE, t0:t0 + n], wts[0:n, j, :], ident[0:n, 0:n])
            last.then_inc(full_sem("wT"), 1)
            pe.wait_ge(more_flags, 1)
            out = claim(pe, ALLB, "place")
            mm(out[0:64, 0:1], const("before", 64)[:, 0:64], more[0:64, 0:1], True, True)\
                .then_inc(full_sem("place"), 1)
            pe.wait_ge(more_hot, 1)
            out = claim(pe, ALLB, "list")
            cm = const("more", 64)
            mm(out[0:1, 0:MAX_MORE], cm[:, 1:2], more[0:64, 3:3 + MAX_MORE], True, True)
            mm(out[0:1, MAX_MORE:2 * MAX_MORE], cm[:, 2:3], more[0:64, 3:3 + MAX_MORE], True, True)
            mm(out[0:1, 2 * MAX_MORE:2 * MAX_MORE + 1], more[0:64, 0:1], ones[0:64, 0:1], True, True)\
                .then_inc(full_sem("list"), 1)
            pe.wait_ge(*drained("wT"))
            for m in range(KT):
                out = claim(pe, ALLB, "bd", m)
                mm(out[:, 0:NT], bd_rows[0:NE, P * m:P * m + P], wT[0:NE, :], True, True)\
                    .then_inc(full_sem("bd", m), 1)

            pe.wait_ge(moe_start, 1)

            def by_count(count_n, at_width):
                if count_n is None:
                    at_width(WIDE)
                    return
                with pe.If(count_n > NARROW):
                    at_width(WIDE)
                with pe.Else():
                    at_width(NARROW)

            def gather(g, count_n):
                pe.wait_ge(sel_ready, g + 1)

                def at_width(w):
                    for half in range(2):
                        for i in range(4):
                            k = 4 * half + i
                            for j, (t0, m) in enumerate(TILES):
                                last = mm(psum[:, BANK_Q[half], P * i:P * i + w],
                                          h2_tok[0:m, j, P * k:P * k + P], sel[0:m, j, 0:w],
                                          i == 0 and j == 0, j == 2)
                        last.then_inc(gathered, 1)
                by_count(count_n, at_width)

            def expert_block(n, g, count_n, next_count):
                prefetch = next_count is not None
                pe.wait_ge(selw_ready, g + 1)
                pe.wait_ge(yT_copied, 2 * n)
                for j, (t0, m) in enumerate(TILES):
                    last = pe.transpose(psum[:, BANK_P[0], t0:t0 + m], selw[0:m, j, :], ident[0:m, 0:m])
                last.then_inc(selw_turned, 1)
                pe.wait_ge(hg_copied, 2 * g + 2)

                def gate_up(w):
                    for c in range(2):
                        pe.wait_ge(gu_taken[c], n)
                        for half in range(2):
                            s = 2 * c + half
                            pe.wait_ge(unit_landed[moe_slot[s]], 32 * n + (landed_base[s] + 32))
                            u = ring[:, moe_slot[s], :].rearrange("p (k g f) -> p k g f", k=4, g=2)
                            for q in range(2):
                                for m in range(4):
                                    for k in range(4):
                                        last = mm(psum[:, 2 * c + q, P * m:P * m + w],
                                                  u[:, k, q, P * m:P * m + P],
                                                  hgT[:, 4 * half + k, 0:w],
                                                  half == 0 and m == 0 and k == 0, half == 1 and k == 3)
                            last.then_inc((gu_half if half == 0 else gu_done)[c], 1)

                def down(w):
                    for half in range(2):
                        s = 4 + half
                        pe.wait_ge(unit_landed[moe_slot[s]], 16 * n + (landed_base[s] + 16))
                        pe.wait_ge(act_ready, 2 * n + (1 + half))
                        u = ring[:, moe_slot[s], :].rearrange("p (k f) -> p k f", k=4)
                        for m in range(KT):
                            out = psum[:, BANK_P[m // 4], P * (m % 4):P * (m % 4) + w]
                            for k in range(4):
                                last = mm(out, u[:, k, P * m:P * m + P], actT[:, 4 * half + k, 0:w],
                                          half == 0 and m % 4 == 0 and k == 0, half == 1 and k == 3)
                        last.then_inc(down_half if half == 0 else down_done, 1)

                def combine(w):
                    pe.wait_ge(hg_copied, 2 * g + (4 if prefetch else 2))
                    for half in range(2):
                        pe.wait_ge(yT_copied, 2 * n + (1 + half))
                        for i in range(4):
                            last = pe.transpose(psum[:, BANK_Q[half], P * i:P * i + P],
                                                yT[:, 4 * half + i, :], ident)
                        last.then_inc(y_turned, 1)
                    for m in range(KT):
                        if m < 2:
                            pe.wait_ge(y_copied, 2 * n + (1 + m))
                        else:
                            pe.wait_ge(added, KT * n + (m - 1))
                        mm(psum[:, BANK_Q[m % 2], 0:NT], y_rows[0:w, P * m:P * m + P], selwT[0:w, :],
                           True, True).then_inc(combined, 1)

                by_count(count_n, gate_up)
                if prefetch:
                    pe.wait_ge(added, KT * n)
                    gather(g + 1, next_count)
                pe.wait_ge(selw_copied, n + 1)

                def down_and_combine(w):
                    down(w)
                    combine(w)
                by_count(count_n, down_and_combine)

            pe.wait_ge(tables, 1)
            gather(0, pe.value_load(ints[0:1, AT_COUNT:AT_COUNT + 1], min_val=0, max_val=NT))
            with pe.Fori(0, NE) as n:
                count_n = pe.value_load(ints[0:1, bass.ds(n + AT_COUNT, 1)], min_val=0, max_val=NT)
                next_count = pe.value_load(ints[0:1, bass.ds(n + (AT_COUNT + 1), 1)], min_val=0, max_val=NT)
                expert_block(n, n, count_n, next_count)
            more_n = pe.value_load(ints[0:1, AT_MORE:AT_MORE + 1], min_val=0, max_val=MAX_MORE)
            with pe.If(more_n > 0):
                with pe.Fori(0, more_n) as i:
                    pe.wait_ge(added, KT * i + KT * NE)
                    gather(i + (NE + 1), None)
                    expert_block(i + NE, i + (NE + 1), None, None)
            with pe.Else():
                pe.nop()
            pe.wait_ge(acc_final, 1)

            pe.wait_ge(x2_squared, 1)
            out = claim(pe, ALLB, "ss3")
            for k in range(KT):
                last = mm(out[:, 0:NT], ones, fin_sq[:, k, :], k == 0, k == KT - 1)
            last.then_inc(full_sem("ss3"), 1)
            pe.wait_ge(x2_ready, 1)
            for j, (t0, n) in enumerate(TILES):
                for half in range(2):
                    out = claim(pe, ALLB, "y", j, half)
                    for i in range(4):
                        last = pe.transpose(out[0:n, P * i:P * i + P], xT[:, 4 * half + i, t0:t0 + n], ident)
                    last.then_inc(full_sem("y", j, half), 1)

        own_count = {}

        def own(s):
            own_count[s.name] = own_count.get(s.name, 0) + 1
            return s, own_count[s.name]

        def over(ap, axis, n):
            v = ap.unsqueeze(axis)
            shape = list(v.shape)
            shape[axis] = n
            return v.to_broadcast(shape)

        @block.vector
        def _(dve):
            steps = [0, dve_step]

            def step(ins):
                steps[0] += 1
                ins.then_inc(steps[1], 1)
                dve.wait_ge(steps[1], steps[0])

            iota, valid = const("iota"), const("valid")
            step(dve.memset(M0[:, 0:1], 0.0))

            norms = [0]

            def mean_square(out, src, n, *key):
                dve.tensor_scalar(out, src, 1.0 / n, EPS, ALU.mult, ALU.add).then_inc(free_sem(*key), 1)
                dve.wait_ge(*drained(*key))

            def rsqrt(t):
                norms[0] += 1
                dve.reciprocal(t, t).then_inc(mean_inverse, 1)
                dve.wait_ge(mean_root, norms[0])

            dve.wait_ge(c_sig_done, 1)
            dve.tensor_tensor(c_rows[0:9, :], c_rows[0:9, :], c_sig[0:9, :], ALU.mult).then_inc(c_silu, 1)
            dve.wait_ge(*own(c_silu))
            dve.wait_ge(*full("vec"))
            dve.tensor_copy(vecT[:, 0:117], bank("vec")[:, 0:117]).then_inc(free_sem("vec"), 1)
            dve.wait_ge(*drained("vec"))
            dve.wait_ge(*full("cT"))
            dve.tensor_copy(cT[:], bank("cT")[:, 0:72].rearrange("p (k r) -> p k r", k=KT))\
                .then_inc(free_sem("cT"), 1)
            dve.wait_ge(*drained("cT"))
            dve.wait_ge(*full("bgu"))
            dve.tensor_copy(gu_biasT[:], bank("bgu")).then_inc(free_sem("bgu"), 1)
            dve.wait_ge(*drained("bgu"))
            dve.wait_ge(table_in, 16 * 11)
            for i in range(2):
                step(dve.tensor_tensor(lam_rows[:, 2 * i, :], lam_rows[:, 2 * i, :],
                                       lam_rows[:, 2 * i + 1, :], ALU.mult))
                step(dve.tensor_reduce(LAM[:, i:i + 1], lam_rows[:, 2 * i, :], AX, ALU.add))
            dve.tensor_copy(LAM[:, 0:2], LAM[:, 0:2]).then_inc(lam_dot, 1)
            dve.wait_ge(*own(lam_dot))
            dve.wait_ge(lam_exp, 1)
            step(dve.tensor_tensor(NLAM, LAM[:, 3:4], LAM[:, 2:3], ALU.subtract))
            step(dve.tensor_scalar(NLAM, NLAM, -LAM_INIT, None, ALU.add))
            comp = const("comp")
            step(dve.scalar_tensor_tensor(COEF, comp[:, 1:2], NLAM, comp[:, 0:1], ALU.mult, ALU.add))
            step(dve.tensor_scalar(GS, vecT[:, V_GS:V_GS + 1], 1.0 - LAM_INIT, None, ALU.mult))

            for j in range(3):
                for half in range(2):
                    dve.wait_ge(*drained("xT", j, half))
            dve.tensor_tensor(x_sq, xT[:], xT[:], ALU.mult).then_inc(x_squared, 1)
            dve.wait_ge(*own(x_squared))
            dve.wait_ge(*full("ss1"))
            mean_square(rstd[:], bank("ss1")[:, 0:NT], D, "ss1")
            rsqrt(rstd[:])
            step(dve.tensor_tensor(hT[:], xT[:], over(rstd[:], 1, KT), ALU.mult))

            def ada_bias(key, m0, m1):
                dve.wait_ge(*full(key))
                n = m1 - m0
                dve.tensor_tensor(modT[:, m0:m1, :],
                                  bank(key)[:, 0:9 * n].rearrange("p (m r) -> p m r", m=n),
                                  over(vecT[:, V_ADA + m0:V_ADA + m1], 2, 9), ALU.add)\
                    .then_inc(free_sem(key), 1)
                dve.wait_ge(*drained(key))

            def modulate(which, g_col, shift_m, scale_m, done):
                gain, shift = gainT[:, which], modT[:, shift_m:shift_m + KT, :]
                step(dve.scalar_tensor_tensor(gain, modT[:, scale_m:scale_m + KT, :], 1.0,
                                              over(vecT[:, g_col:g_col + KT], 2, 9), ALU.add, ALU.mult))
                samples = hT[:, :, TP:NT].rearrange("p k (b t) -> p k b t", b=NB)
                for k in range(KT):
                    dve.tensor_scalar(hT[:, k, 0:TP], hT[:, k, 0:TP], gain[:, k, 0:1], shift[:, k, 0:1],
                                      ALU.mult, ALU.add)
                step(dve.tensor_tensor(samples, samples, over(gain[:, :, 1:9], 3, TD), ALU.mult))
                dve.tensor_tensor(samples, samples, over(shift[:, :, 1:9], 3, TD), ALU.add)\
                    .then_inc(done, 1)
                dve.wait_ge(*own(done))

            ada_bias("ada0", 0, 16)
            modulate(0, V_G1, 0, 8, h_ready)

            cos = const("cos").rearrange("p (j c) -> p j c", j=3)
            sin = const("sin").rearrange("p (j c) -> p j c", j=3)
            flat = pairs.rearrange("p a b -> p (a b)")
            for w in "qk":
                for j, (t0, n) in enumerate(TILES):
                    dve.wait_ge(*full(w, j))
                    z = bank(w, j)[0:n, :].rearrange("p (g s c) -> p g s c", g=8, s=2)
                    tc_ = flat[0:n, 0:512].rearrange("p (g s c) -> p g s c", g=8, s=2)
                    ts_ = flat[0:n, 512:1024].rearrange("p (g s c) -> p g s c", g=8, s=2)
                    cj = over(over(cos[0:n, j, :], 1, 2), 1, 8)
                    sj = over(over(sin[0:n, j, :], 1, 2), 1, 8)
                    dve.tensor_tensor(tc_, z, cj, ALU.mult)
                    dve.tensor_tensor(ts_, z, sj, ALU.mult).then_inc(free_sem(w, j), 1)
                    dve.wait_ge(*drained(w, j))
                    if w == "q" and j == 2:
                        dve.wait_ge(*full("qT", 0))
                    dst = (q_rot[0:n, j % 2, :] if w == "q" else k_rot[0:n, j, :])\
                        .rearrange("p (g s c) -> p g s c", g=8, s=2)
                    dve.tensor_tensor(dst[:, :, 0, :], tc_[:, :, 0, :], ts_[:, :, 1, :], ALU.subtract)
                    dve.tensor_tensor(dst[:, :, 1, :], tc_[:, :, 1, :], ts_[:, :, 0, :], ALU.add)\
                        .then_inc(rotated, 1)
                    dve.wait_ge(*own(rotated))
            step(dve.memset(q_blocks, 0.0))
            dve.wait_ge(*drained("qT", 2))
            qb_v = q_blocks.rearrange("p b (h c) -> p b h c", h=H)
            for h in range(H):
                for c in range(2):
                    rows = slice(DK * c, DK * c + DK)
                    last = dve.tensor_copy(qb_v[rows, :, h, 16 * h + 8 * c:16 * h + 8 * c + 8],
                                           qT[rows, h, TP:NT].rearrange("p (b t) -> p b t", b=NB))
            last.then_inc(q_blocked, 1)
            dve.wait_ge(*own(q_blocked))

            items = [(h, qb) for h in range(H) for qb in range(2)]
            am = const("attmask")

            def att_mask_max(i):
                h, qb = items[i]
                n = P * (qb + 1)
                if i >= 2:
                    dve.wait_ge(*full("aT", i - 2))
                for c in range(2):
                    dve.wait_ge(*full("S", i, c))
                    dve.tensor_tensor(s_pair[:, i % 2, c, 0:n], bank("S", i, c)[:, 0:n], am[:, 256 - n:256],
                                      ALU.add).then_inc(free_sem("S", i, c), 1)
                    dve.wait_ge(*drained("S", i, c))
                mx = MX[:, 2 * (i % 2):2 * (i % 2) + 2]
                step(dve.tensor_reduce(mx, s_pair[:, i % 2, :, 0:n], AX, ALU.max))
                dve.tensor_scalar(mx, mx, -DK ** -0.5, None, ALU.mult).then_inc(att_max, 1)
                dve.wait_ge(*own(att_max))

            att_mask_max(0)
            for i, (h, qb) in enumerate(items):
                if i + 1 < len(items):
                    att_mask_max(i + 1)
                n = P * (qb + 1)
                dve.wait_ge(att_exp, 2 * i + 2)
                rc = RC[:, 2 * (i % 2):2 * (i % 2) + 2]
                step(dve.reciprocal(rc, LS[:, 2 * (i % 2):2 * (i % 2) + 2]))
                step(dve.tensor_tensor(rc[:, 1:2], rc[:, 1:2], NLAM, ALU.mult))
                step(dve.tensor_scalar(s_pair[:, i % 2, 0, 0:n], s_pair[:, i % 2, 0, 0:n], rc[:, 0:1], None,
                                       ALU.mult))
                dve.scalar_tensor_tensor(s_pair[:, i % 2, 0, 0:n], s_pair[:, i % 2, 1, 0:n], rc[:, 1:2],
                                         s_pair[:, i % 2, 0, 0:n], ALU.mult, ALU.add).then_inc(att_a, 1)
                dve.wait_ge(*own(att_a))

            nm = const("newmask", 64).rearrange("p (b k) -> p b k", b=NB)
            last_key = PAGES * PAGE

            def key_pages(b):
                for g in range(1, PAGES, 2):
                    dve.wait_ge(*full("kTb", b, g))
                    dve.tensor_copy(kTb[:, :, PAGE * g:PAGE * g + PAGE],
                                    bank("kTb", b, g).rearrange("p (h k) -> p h k", h=H))\
                        .then_inc(free_sem("kTb", b, g), 1)
                    dve.wait_ge(*drained("kTb", b, g))

            key_pages(0)
            for b in range(NB):
                dve.wait_ge(*full("Sn", b))
                s0 = groups[("Sd", b, 0)][0]
                step(dve.tensor_reduce(SC[0:64, 0:1],
                                       psum[0:64, s0:s0 + 2, :], mybir.AxisListType.XY, ALU.max))
                dve.tensor_tensor(s_new[0:64, :], bank("Sn", b)[0:64, 0:TS], nm[:, b, :], ALU.add)\
                    .then_inc(free_sem("Sn", b), 1)
                dve.wait_ge(*drained("Sn", b))
                step(dve.tensor_reduce(SC[0:64, 1:2], s_new[0:64, :], AX, ALU.max))
                step(dve.tensor_tensor(SC[0:64, 0:1], SC[0:64, 0:1], SC[0:64, 1:2], ALU.max))
                dve.tensor_scalar(SC[0:64, 2:3], SC[0:64, 0:1], -DK ** -0.5, None, ALU.mult)\
                    .then_inc(dec_max, 1)
                dve.wait_ge(*own(dec_max))
                if b + 1 < NB:
                    key_pages(b + 1)
                dve.wait_ge(dec_exp, b + 1)
                step(dve.tensor_reduce(SC[0:64, 6:7], SC[0:64, 3:6], AX, ALU.add))
                step(dve.reciprocal(SC[0:64, 6:7], SC[0:64, 6:7]))
                step(dve.tensor_tensor(SC[0:64, 6:7], SC[0:64, 6:7], COEF[0:64, :], ALU.mult))
                dve.tensor_scalar(p_dec[0:64, :], p_dec[0:64, :], SC[0:64, 6:7], None, ALU.mult)\
                    .then_inc(dec_p, 1)
                dve.wait_ge(*own(dec_p))
                dve.wait_ge(*full("pT", b))
                dve.tensor_copy(pT_dec, bank("pT", b).rearrange("p (g c) -> p g c", g=PAGES))\
                    .then_inc(free_sem("pT", b), 1)
                dve.wait_ge(*drained("pT", b))
                dve.wait_ge(*full("od", b))
                dve.tensor_reduce(oT[:, :, TP + TD * b:TP + TD * b + TD],
                                  bank("od", b)[:, 0:64].rearrange("p (h c q) -> p h q c", h=H, c=2),
                                  AX, ALU.add).then_inc(free_sem("od", b), 1)
                dve.wait_ge(*drained("od", b))
            dve.wait_ge(*drained("PV", len(items) - 1))
            dve.wait_ge(*drained("od", NB - 1))
            dve.wait_ge(k_stored, 96)
            dve.tensor_tensor(o_sq, oT[:], oT[:], ALU.mult).then_inc(o_squared, 1)
            dve.wait_ge(*own(o_squared))
            for h in range(H):
                dve.wait_ge(*full("oss", h))
                mean_square(o_rms[:, h, :], bank("oss", h)[:, 0:NT], P, "oss", h)
            rsqrt(o_rms)
            dve.scalar_tensor_tensor(oT[:], oT[:], GS, o_rms, ALU.mult, ALU.mult).then_inc(o_ready, 1)
            dve.wait_ge(*own(o_ready))
            step(dve.memset(raw_p[:, :, 0:3], 0.0))
            dve.memset(nT, 0.0).then_inc(region_m, 1)
            dve.wait_ge(*own(region_m))

            dve.wait_ge(mrows_in, 48)
            dve.wait_ge(*full("gi"))
            dve.tensor_scalar(rows_li[0:H, :], bank("gi")[0:H, 0:NT], BG[:, 0:1], None, ALU.add)\
                .then_inc(free_sem("gi"), 1)
            dve.wait_ge(*drained("gi"))
            dve.wait_ge(*full("gf"))
            dve.tensor_scalar(rows_f[0:H, :], bank("gf")[0:H, 0:NT], BG[:, 1:2], None, ALU.add)\
                .then_inc(free_sem("gf"), 1)
            dve.wait_ge(*drained("gf"))
            dve.wait_ge(*drained("gi"))
            dve.wait_ge(*drained("gf"))
            dve.scalar_tensor_tensor(rows_t[0:H, :], rows_f[0:H, :], -1.0, rows_f[0:H, :], ALU.mult,
                                     ALU.max).then_inc(f_abs, 1)
            dve.wait_ge(*own(f_abs))
            dve.wait_ge(*full("cs"))
            step(dve.tensor_copy(n0T, bank("cs")[:, 192:224]))
            dve.tensor_copy(raw_s[:, :, :, 0:3],
                            bank("cs")[:, 0:192].rearrange("p (m b j) -> p m b j", m=8, b=NB))\
                .then_inc(free_sem("cs"), 1)
            dve.wait_ge(*drained("cs"))

            def conv(m0):
                for m in range(m0, m0 + 4):
                    dve.wait_ge(*drained("qm" if m < 4 else "km", m % 4))
                    cp, cs_ = cv[:, m, 0:TP], cv[:, m, TP:NT].rearrange("p (b t) -> p b t", b=NB)
                    for tap in range(4):
                        w = vecT[:, V_WC + 8 * tap + m:V_WC + 8 * tap + m + 1]
                        sp_, ss_ = raw_p[:, m, tap:tap + TP], raw_s[:, m, :, tap:tap + TD]
                        if tap == 0:
                            bias = vecT[:, V_BC + m:V_BC + m + 1]
                            dve.tensor_scalar(cp, sp_, w, bias, ALU.mult, ALU.add)
                            step(dve.tensor_scalar(cs_, ss_, w, bias, ALU.mult, ALU.add))
                        else:
                            dve.scalar_tensor_tensor(cp, sp_, w, cp, ALU.mult, ALU.add)
                            last = dve.scalar_tensor_tensor(cs_, ss_, w, cs_, ALU.mult, ALU.add)
                            if m < m0 + 3 or tap < 3:
                                step(last)
                last.then_inc(conv_done, 1)
                dve.wait_ge(*own(conv_done))

            conv(0)
            dve.wait_ge(f_ln, 1)
            F, u, M_, up = rows_f[0:H, :], rows_u[0:H, :], rows_w[0:H, :], rows_t[0:H, :]
            step(dve.scalar_tensor_tensor(up, F, 0.0, up, ALU.min, ALU.subtract))
            step(dve.tensor_tensor_scan(F, const("carry", H), up, 0.0, ALU.mult, ALU.add))
            step(dve.tensor_tensor(u, rows_li[0:H, :], F, ALU.subtract))
            step(dve.tensor_copy(up, u))
            step(dve.tensor_tensor(up[:, 0:1], up[:, 0:1], M0[:, 0:1], ALU.max))
            step(dve.tensor_tensor(up[:, TP:NT:TD], up[:, TP:NT:TD], M0[:, 1:9], ALU.max))
            step(dve.tensor_tensor_scan(M_, const("drop", H), up, 0.0, ALU.add, ALU.max))
            negM = rowsR[0:H, 0:NT]
            step(dve.tensor_tensor(up, F, M_, ALU.add))
            step(dve.tensor_scalar(negM, M_, -1.0, None, ALU.mult))
            nms = negM[:, TP:NT].rearrange("p (b t) -> p b t", b=NB)
            step(dve.tensor_tensor(rowsR[0:H, 2 * NT:2 * NT + TS].rearrange("p (b t) -> p b t", b=NB), nms,
                                   over(M0[:, 1:9], 2, TD), ALU.add))
            step(dve.tensor_scalar(rows_w[0:H, 0:TP], u[:, 0:TP], negM[:, TP - 1:TP], None, ALU.add))
            dve.tensor_tensor(rows_w[0:H, TP:NT].rearrange("p (b t) -> p b t", b=NB),
                              u[:, TP:NT].rearrange("p (b t) -> p b t", b=NB),
                              over(nms[:, :, TD - 1], 2, TD), ALU.add).then_inc(m_rows, 1)
            dve.wait_ge(*own(m_rows))
            conv(4)
            dve.wait_ge(conv_sig, 1)
            dve.tensor_tensor(cv[:, 0:4, :], cv[:, 0:4, :], cv_sig, ALU.mult).then_inc(conv_ready, 1)
            dve.wait_ge(*own(conv_ready))
            step(dve.tensor_copy(tail[:, :, 0:3], raw_p[:, :, TP:TP + 3]))
            dve.tensor_copy(tail[:, :, 3:27].rearrange("p m (b j) -> p m b j", b=NB),
                            raw_s[:, :, :, 8:11]).then_inc(tail_ready, 1)
            dve.wait_ge(*own(tail_ready))
            dve.wait_ge(conv_sig, 2)
            dve.scalar_tensor_tensor(cv[:, 4:8, :], cv[:, 4:8, :], P ** -0.5, cv_sig, ALU.mult, ALU.mult)\
                .then_inc(conv_ready, 1)
            dve.wait_ge(*own(conv_ready))
            ada_bias("ada1", 16, 48)
            dve.wait_ge(*full("uw"))
            step(dve.tensor_copy(uw[:, 0:2, :], bank("uw")[:, 0:16].rearrange("p (j c) -> p j c", j=2)))
            dve.tensor_copy(uw[0:TS, 2, :], bank("uw")[0:TS, 16:24]).then_inc(free_sem("uw"), 1)
            dve.wait_ge(*drained("uw"))
            dve.wait_ge(conv_ready, 2)
            for j in range(3):
                dve.wait_ge(*drained("vm", j))
            for m in range(4):
                dve.wait_ge(*drained("om", m))
            causal = const("causal")
            blkind = const("blkind", TS)
            dve.wait_ge(*landed(("C", 0)))
            c0 = unit(("C", 0), 32)
            for h in range(H):
                dve.wait_ge(*full("bc0", h))
                if h:
                    dve.wait_ge(*full("hss", h - 1))
                bc = bank("bc0", h)
                dve.tensor_scalar(dT[:, 0:256], bc[:, 0:256], uw[:, 0, h:h + 1], 0.0, ALU.add, ALU.min)
                dve.tensor_scalar(dT[:, 256:384], bc[:, P:TP], uw[:, 1, h:h + 1], 0.0, ALU.add, ALU.min)
                dve.tensor_scalar(dT[0:TS, 384:448], bc[0:TS, TP:NT], uw[0:TS, 2, h:h + 1], 0.0, ALU.add,
                                  ALU.min).then_inc(free_sem("bc0", h), 1)
                dve.wait_ge(*drained("bc0", h))
                dve.wait_ge(*full("kt", h))
                for j, (t0, n) in enumerate(TILES):
                    last = dve.tensor_scalar(kw[0:n, j, :], bank("kt", h)[0:n, P * j:P * j + P],
                                             uw[0:n, j, 4 + h:5 + h], None, ALU.mult)
                last.then_inc(free_sem("kt", h), 1)
                dve.wait_ge(*drained("kt", h))
                dve.tensor_tensor(v_blk[0:TS], over(vm[0:TS, 2, P * h:P * h + P], 1, NB),
                                  over(blkind, 2, P), ALU.mult).then_inc(kw_ready, 1)
                dve.wait_ge(*own(kw_ready))
                dve.wait_ge(*drained("bc1", h))
                ei = bcS[:, NT:NT + TS]
                step(dve.tensor_tensor(qe[:, 0, :], cv[:, h, TP:NT], ei, ALU.mult))
                n0 = n0T.rearrange("p (b h) -> p b h", b=NB)[:, :, h]
                dve.tensor_tensor(qe[:, 1, :].rearrange("p (b t) -> p b t", b=NB),
                                  qe[:, 0, :].rearrange("p (b t) -> p b t", b=NB),
                                  over(n0, 2, TD), ALU.mult).then_inc(qe_ready, 1)
                dve.wait_ge(*own(qe_ready))
                dve.wait_ge(d_exp, h + 1)
                step(dve.tensor_tensor(dT[:, 0:384], dT[:, 0:384], causal[:, 0:384], ALU.mult))
                step(dve.tensor_tensor(dT[0:TS, 384:448], dT[0:TS, 384:448], causal[0:TS, 384:448],
                                       ALU.mult))
                dve.wait_ge(*full("st", h))
                dve.tensor_tensor(dT[:, 0:384], dT[:, 0:384], bank("st", h)[:, 0:384], ALU.mult)\
                    .then_inc(p_ready, 1)
                dve.wait_ge(*own(p_ready))
                dve.tensor_tensor(dT[0:TS, 384:448], dT[0:TS, 384:448], bank("st", h)[0:TS, 384:448],
                                  ALU.mult).then_inc(free_sem("st", h), 1)
                dve.wait_ge(*drained("st", h))
                dve.wait_ge(*full("C", h))
                dec = ei.rearrange("p (b t) -> p b t", b=NB)[:, :, TD - 1]
                step(dve.tensor_copy(C_p[:, h, :], bank("C", h)[:, 0:P]))
                step(dve.tensor_copy(nT[:, h:h + 1], bank("C", h)[:, P:P + 1]))
                nTs = nT[:, 4:36].rearrange("p (b h) -> p b h", b=NB)[:, :, h]
                step(dve.tensor_tensor(nTs, n0, dec, ALU.mult))
                dve.tensor_tensor(nTs, nTs, bank("C", h)[:, 130:138], ALU.add).then_inc(free_sem("C", h), 1)
                dve.wait_ge(*drained("C", h))
                dve.wait_ge(*full("num", h))
                dve.wait_ge(*full("den", h))
                step(dve.tensor_tensor(den_s, bank("den", h)[:, 0:NT], bcS[:, 0:NT], ALU.max))
                dve.scalar_tensor_tensor(den_s, bank("den", h)[:, 0:NT], -1.0, den_s, ALU.mult,
                                         ALU.max).then_inc(free_sem("den", h), 1)
                dve.wait_ge(*drained("den", h))
                step(dve.reciprocal(den_s, den_s))
                dve.tensor_tensor(hr[:, h, :], bank("num", h)[:, 0:NT], den_s, ALU.mult)\
                    .then_inc(free_sem("num", h), 1)
                dve.wait_ge(*drained("num", h))
                dve.tensor_tensor(hsq, hr[:, h, :], hr[:, h, :], ALU.mult).then_inc(h_squared, 1)
                dve.wait_ge(*own(h_squared))
                ch = c0.rearrange("p (b h) e -> p b h e", b=NB)[:, :, h, :]
                step(dve.tensor_tensor(ch, ch, over(dec, 2, P), ALU.mult))
                for half in range(2):
                    dve.wait_ge(*full("Cs", h, half))
                    dve.tensor_tensor(ch[:, 4 * half:4 * half + 4, :], ch[:, 4 * half:4 * half + 4, :],
                                      bank("Cs", h, half).rearrange("p (b e) -> p b e", b=4), ALU.add)\
                        .then_inc(free_sem("Cs", h, half), 1)
                    dve.wait_ge(*drained("Cs", h, half))
                dve.wait_ge(*drained("C", h))
                step(dve.tensor_copy(SC[:, 7:8], den_s[:, 0:1]))
                dve.tensor_copy(SC[:, 7:8], den_s[:, 0:1]).then_inc(c_ready, 1)
                dve.wait_ge(*own(c_ready))
                dve.wait_ge(*full("hss", h))
                mean_square(hmT[:, h, :], bank("hss", h)[:, 0:NT], P, "hss", h)
            rsqrt(hmT[:])
            for h in range(H):
                dve.scalar_tensor_tensor(hr[:, h, :], hr[:, h, :], vecT[:, V_GM + h:V_GM + h + 1],
                                         hmT[:, h, :], ALU.mult, ALU.mult).then_inc(dve_step, 1)
                steps[0] += 1
            dve.wait_ge(dve_step, steps[0])
            dve.tensor_tensor(hmT[:], hr, so, ALU.mult).then_inc(hm_ready, 1)
            dve.wait_ge(*own(hm_ready))

            for m in range(KT):
                dve.wait_ge(*full("upa", m))
                dve.wait_ge(*drained("ga0" if m < 4 else "ga1", m % 4))
                dve.tensor_tensor(mT[:, m, :], bank("upa", m)[:, 0:NT], sg[:, m, :], ALU.mult)\
                    .then_inc(free_sem("upa", m), 1)
                dve.wait_ge(*drained("upa", m))
            for m in range(KT):
                dve.wait_ge(*full("upb", m))
                dve.wait_ge(*drained("gb0" if m < 4 else "gb1", m % 4))
                dve.tensor_tensor(sg[:, m, :], bank("upb", m)[:, 0:NT], sg[:, m, :], ALU.mult)\
                    .then_inc(free_sem("upb", m), 1)
                dve.wait_ge(*drained("upb", m))
            dve.wait_ge(*drained("upa", KT - 1))
            for m in range(KT):
                dve.wait_ge(*drained("upb", m))
            dve.tensor_tensor(mT, mT, sg, ALU.add).then_inc(merged, 1)
            dve.wait_ge(*own(merged))

            def gated_add(m, src, gate_m, *key):
                gate = modT[:, gate_m + m, :]
                samples = rstd[:, 0:TS].rearrange("p (b t) -> p b t", b=NB)
                step(dve.tensor_tensor(samples, src[:, TP:NT].rearrange("p (b t) -> p b t", b=NB),
                                       over(gate[:, 1:9], 2, TD), ALU.mult))
                dve.tensor_tensor(xT[:, m, TP:NT], xT[:, m, TP:NT], rstd[:, 0:TS], ALU.add)
                last = dve.scalar_tensor_tensor(xT[:, m, 0:TP], src[:, 0:TP], gate[:, 0:1], xT[:, m, 0:TP],
                                                ALU.mult, ALU.add)
                if key:
                    last.then_inc(free_sem(*key), 1)
                    dve.wait_ge(*drained(*key))
                else:
                    step(last)

            for m in range(KT):
                dve.wait_ge(*full("wo", m))
                gated_add(m, bank("wo", m), 16, "wo", m)

            dve.tensor_tensor(fin_sq, xT[:], xT[:], ALU.mult).then_inc(x1_squared, 1)
            dve.wait_ge(*own(x1_squared))
            dve.wait_ge(*full("ss2"))
            mean_square(rstd[:], bank("ss2")[:, 0:NT], D, "ss2")
            rsqrt(rstd[:])
            step(dve.tensor_tensor(hT[:], xT[:], over(rstd[:], 1, KT), ALU.mult))
            modulate(1, V_G2, 24, 32, h2_ready)

            step(dve.memset(logits, 0.0))
            dve.wait_ge(moe_in, 48)
            dve.wait_ge(*full("logit"))
            lg = bank("logit")[:, 0:96].rearrange("p (j e) -> p j e", j=3)
            step(dve.tensor_tensor(logits[:, 0:2, :], lg[:, 0:2, :], over(b_rt, 1, 2), ALU.add))
            dve.tensor_tensor(logits[0:TS, 2, :], lg[0:TS, 2, :], b_rt[0:TS, :], ALU.add)\
                .then_inc(free_sem("logit"), 1)
            dve.wait_ge(*drained("logit"))
            for j in range(3):
                step(dve.max(top8[:, j, :], logits[:, j, :]))
                step(dve.max_index(top_ix[:, j, :], top8[:, j, :], logits[:, j, :]))
            step(dve.tensor_copy(idxf, top_ix[:]))
            dve.tensor_tensor(ew, top8[:, :, 0:4], top8[:, :, 0:1].to_broadcast([P, 3, 4]), ALU.subtract)\
                .then_inc(top_diff, 1)
            dve.wait_ge(*own(top_diff))
            dve.wait_ge(top_exp, 1)
            step(dve.tensor_reduce(esum, ew, AX, ALU.add))
            step(dve.reciprocal(esum, esum))
            step(dve.tensor_tensor(esum, esum, valid, ALU.mult))
            step(dve.tensor_tensor(ew, ew, over(esum, 2, 4), ALU.mult))
            iota_e = over(iota[:, 0:NE], 1, 3)
            for s in range(TOPK):
                step(dve.tensor_tensor(eq, iota_e, idxf[:, :, s:s + 1].to_broadcast([P, 3, NE]),
                                       ALU.is_equal))
                if s == 0:
                    step(dve.tensor_copy(mask, eq))
                    step(dve.tensor_tensor(wts, eq, ew[:, :, s:s + 1].to_broadcast([P, 3, NE]), ALU.mult))
                else:
                    step(dve.tensor_tensor(mask, mask, eq, ALU.add))
                    step(dve.tensor_tensor(eqw, eq, ew[:, :, s:s + 1].to_broadcast([P, 3, NE]), ALU.mult))
                    step(dve.tensor_tensor(wts, wts, eqw, ALU.add))
            dve.tensor_tensor(mask, mask, over(valid, 2, NE), ALU.mult).then_inc(routed, 1)
            dve.wait_ge(*own(routed))
            dve.wait_ge(*full("pos"))
            pp = bank("pos")
            step(dve.scalar_tensor_tensor(eq, pp[:, 0:96].rearrange("p (j e) -> p j e", j=3), 1.0, mask,
                                          ALU.add, ALU.mult))
            for r in range(ROUNDS):
                step(dve.tensor_scalar(pos[:, :, NE * r:NE * r + NE], eq, -1.0 - WIDE * r, None, ALU.add))
                step(dve.tensor_copy(wts3[:, :, NE * r:NE * r + NE], wts))
            step(dve.tensor_copy(ints[0:1, AT_COUNT:AT_COUNT + NE], pp[0:1, 96:128]))
            cm = const("more", 64)
            dve.tensor_tensor(more[0:64, 0:1], pp[0:64, 128:129], cm[:, 0:1], ALU.is_gt)\
                .then_inc(free_sem("pos"), 1)
            dve.wait_ge(*drained("pos"))
            dve.tensor_copy(more[0:64, 2:3], more[0:64, 0:1]).then_inc(more_flags, 1)
            dve.wait_ge(*own(more_flags))
            dve.wait_ge(*full("place"))
            dve.tensor_copy(more[0:64, 1:2], bank("place")[0:64, 0:1]).then_inc(free_sem("place"), 1)
            dve.wait_ge(*drained("place"))
            dve.wait_ge(more_flags, 1)
            dve.tensor_scalar(more[0:64, 3:3 + MAX_MORE], iota[0:64, 0:MAX_MORE], more[0:64, 1:2],
                              more[0:64, 0:1], ALU.is_equal, ALU.mult).then_inc(more_hot, 1)
            dve.wait_ge(*own(more_hot))
            dve.wait_ge(*full("wT"))
            dve.tensor_copy(wT[0:NE, :], bank("wT")[0:NE, 0:NT]).then_inc(free_sem("wT"), 1)
            dve.wait_ge(*drained("wT"))
            dve.wait_ge(*full("list"))
            dve.tensor_copy(ints[0:1, AT_COLUMN:AT_MORE + 1], bank("list")[0:1, 0:2 * MAX_MORE + 1])\
                .then_inc(free_sem("list"), 1)
            dve.wait_ge(*drained("list"))

            def slots(column):
                for j in range(3):
                    last = dve.tensor_scalar(sel[:, j, :], iota, pos[:, j, column], None, ALU.is_equal)
                last.then_inc(sel_ready, 1)

            def slot_weights(column):
                for j in range(3):
                    last = dve.tensor_scalar(selw[:, j, :], iota, pos[:, j, column], wts3[:, j, column],
                                             ALU.is_equal, ALU.mult)
                last.then_inc(selw_ready, 1)

            for m in range(KT):
                dve.wait_ge(*drained("bd", m))
            for j in range(3):
                for half in range(2):
                    dve.wait_ge(*drained("h2", j, half))
            step(dve.memset(psum[:], 0.0))
            dve.tensor_copy(ints[0:1, AT_MORE + 1:AT_MORE + 2], ints[0:1, AT_MORE:AT_MORE + 1])\
                .then_inc(tables, 1)
            dve.wait_ge(*own(tables))
            dve.tensor_copy(ints[0:1, AT_MORE + 1:AT_MORE + 2], ints[0:1, AT_MORE:AT_MORE + 1])\
                .then_inc(moe_start, 1)
            dve.wait_ge(*own(moe_start))
            slots(slice(0, 1))
            slot_weights(slice(0, 1))

            step_base = [steps[0], 0]
            STEPS = 5

            def expert_block(n, g, expert, column, next_column):
                seen = [0]

                def block_step(ins):
                    seen[0] += 1
                    ins.then_inc(dve_step, 1)
                    dve.wait_ge(dve_step, STEPS * n + (step_base[0] + seen[0]))

                if next_column is None:
                    dve.wait_ge(gathered, 2 * g)
                    slots(bass.ds(column, 1))
                    dve.wait_ge(selw_turned, n)
                    slot_weights(bass.ds(column, 1))
                block_step(dve.tensor_copy(bias_e, gu_biasT[:, bass.ds(expert * 16, 16)]))
                if next_column is not None:
                    dve.wait_ge(gathered, 2 * g + 2)
                    slots(bass.ds(next_column, 1))
                for c in range(2):
                    dve.wait_ge(gu_done[c], n + 1)
                    for m in range(4):
                        b = bias_e[:, 4 * c + m:4 * c + m + 1]
                        last = dve.tensor_scalar(act_g[:, m, :], psum[:, 2 * c, P * m:P * m + P], b, LIMIT,
                                                 ALU.add, ALU.min)
                    last.then_inc(gate_ready, 1)
                    dve.wait_ge(act_ready, 2 * n + c)
                    for m in range(4):
                        b = bias_e[:, 8 + 4 * c + m:9 + 4 * c + m]
                        last = dve.tensor_scalar(act_u[:, m, :], psum[:, 2 * c + 1, P * m:P * m + P], b,
                                                 LIMIT, ALU.add, ALU.min)
                    last.then_inc(gu_taken[c], 1)
                    dve.wait_ge(gu_taken[c], n + 1)
                    dve.wait_ge(gate_ready, 2 * n + (1 + c))
                    block_step(dve.tensor_scalar(act_u, act_u, -LIMIT, 1.0, ALU.max, ALU.add))
                    block_step(dve.tensor_tensor(act_u, act_u, act_g, ALU.mult))
                    dve.wait_ge(gate_sig, 2 * n + (1 + c))
                    if c == 0:
                        dve.wait_ge(down_done, n)
                    dve.tensor_tensor(actT[:, 4 * c:4 * c + 4, :], act_u, act_s, ALU.mult)\
                        .then_inc(act_ready, 1)
                if next_column is not None:
                    dve.wait_ge(selw_turned, n + 1)
                    slot_weights(bass.ds(next_column, 1))
                dve.wait_ge(added, KT * n)
                for m in range(KT):
                    dve.wait_ge(combined, KT * n + (m + 1))
                    dve.tensor_tensor(accT[:, m, :], accT[:, m, :], psum[:, BANK_Q[m % 2], 0:NT], ALU.add)\
                        .then_inc(added, 1)
                assert seen[0] == STEPS

            with dve.Fori(0, NE) as n:
                expert_block(n, n, n, n, n + 1)
            more_n = dve.value_load(ints[0:1, AT_MORE:AT_MORE + 1], min_val=0, max_val=MAX_MORE)
            with dve.If(more_n > 0):
                with dve.Fori(0, more_n) as i:
                    column = dve.value_load(ints[0:1, bass.ds(i + AT_COLUMN, 1)], min_val=0,
                                            max_val=ROUNDS * NE - 1)
                    expert = dve.value_load(ints[0:1, bass.ds(i + AT_EXPERT, 1)], min_val=0, max_val=NE - 1)
                    expert_block(i + NE, i + (NE + 1), expert, column, None)
            with dve.Else():
                dve.nop()
            dve.wait_ge(added, KT * NE)
            dve.wait_ge(added, more_n * KT + KT * NE)
            steps[0], steps[1] = 0, tail_step
            dve.tensor_copy(ints[0:1, AT_MORE + 1:AT_MORE + 2], ints[0:1, AT_MORE:AT_MORE + 1])\
                .then_inc(acc_final, 1)
            dve.wait_ge(*own(acc_final))
            for m in range(KT):
                gated_add(m, accT[:, m, :], 40)
            dve.tensor_tensor(fin_sq, xT[:], xT[:], ALU.mult).then_inc(x2_squared, 1)
            dve.wait_ge(*own(x2_squared))
            dve.wait_ge(*full("ss3"))
            mean_square(rstd[:], bank("ss3")[:, 0:NT], D, "ss3")
            rsqrt(rstd[:])
            step(dve.tensor_tensor(xT[:], xT[:], over(rstd[:], 1, KT), ALU.mult))
            dve.tensor_tensor(xT[:], xT[:], over(vecT[:, V_GF:V_GF + KT], 2, NT), ALU.mult)\
                .then_inc(x2_ready, 1)
            dve.wait_ge(*own(x2_ready))

        @block.scalar
        def _(act):
            def copy(out, src):
                return act.activation(out, src, ACT.Copy)

            norms = [0]

            def root(t):
                norms[0] += 1
                act.wait_ge(mean_inverse, norms[0])
                act.activation(t, t, ACT.Sqrt).then_inc(mean_root, 1)

            act.wait_ge(c_in, 32)
            act.activation(c_sig[0:9, :], c_rows[0:9, :], ACT.Sigmoid).then_inc(c_sig_done, 1)
            act.wait_ge(*own(c_sig_done))
            for j, (t0, n) in enumerate(TILES):
                for half in range(2):
                    act.wait_ge(*full("xT", j, half))
                    src = bank("xT", j, half).rearrange("p (k t) -> p k t", k=4)[:, :, 0:n]
                    copy(xT[:, 4 * half:4 * half + 4, t0:t0 + n], src).then_inc(free_sem("xT", j, half), 1)
                    act.wait_ge(*drained("xT", j, half))
            act.wait_ge(lam_dot, 1)
            act.activation(LAM[:, 2:4], LAM[:, 0:2], ACT.Exp).then_inc(lam_exp, 1)
            act.wait_ge(*own(lam_exp))
            root(rstd[:])

            def heads_T(name, j):
                t0, n = TILES[j]
                act.wait_ge(*full(name + "T", j))
                src = bank(name + "T", j).rearrange("p (h t) -> p h t", h=H)[:, :, 0:n]
                copy((qT if name == "q" else kT)[:, :, t0:t0 + n], src).then_inc(free_sem(name + "T", j), 1)
                act.wait_ge(*drained(name + "T", j))

            for j in range(3):
                heads_T("q", j)
            for j, (t0, n) in enumerate(TILES):
                act.wait_ge(*full("v", j))
                copy(va[0:n, j, :], bank("v", j)[0:n, :]).then_inc(free_sem("v", j), 1)
                act.wait_ge(*drained("v", j))
                heads_T("k", j)

            items = [(h, qb) for h in range(H) for qb in range(2)]

            def exps(i):
                n = P * (items[i][1] + 1)
                act.wait_ge(att_max, i + 1)
                for c in range(2):
                    col = 2 * (i % 2) + c
                    act.activation(s_pair[:, i % 2, c, 0:n], s_pair[:, i % 2, c, 0:n], ACT.Exp,
                                   bias=MX[:, col:col + 1], scale=DK ** -0.5,
                                   accum_out=LS[:, col:col + 1]).then_inc(att_exp, 1)
                    act.wait_ge(*own(att_exp))

            exps(0)
            for i, (h, qb) in enumerate(items):
                if i + 1 < len(items):
                    exps(i + 1)
                act.wait_ge(*full("aT", i))
                if i >= 2:
                    act.wait_ge(*full("PV", i - 2))
                n = P * (qb + 1)
                copy(aT[:, i % 2, 0:n], bank("aT", i)[:, 0:n]).then_inc(free_sem("aT", i), 1)
                act.wait_ge(*drained("aT", i))
                act.wait_ge(*full("PV", i))
                copy(oT[:, h, P * qb:P * qb + P], bank("PV", i)[:, 0:P]).then_inc(free_sem("PV", i), 1)
                act.wait_ge(*drained("PV", i))

            def key_pages(b):
                for g in range(0, PAGES, 2):
                    act.wait_ge(*full("kTb", b, g))
                    copy(kTb[:, :, PAGE * g:PAGE * g + PAGE],
                         bank("kTb", b, g).rearrange("p (h k) -> p h k", h=H))\
                        .then_inc(free_sem("kTb", b, g), 1)
                    act.wait_ge(*drained("kTb", b, g))

            key_pages(0)
            nk = PAGES * PAGE
            for b in range(NB):
                act.wait_ge(dec_max, b + 1)
                if b:
                    act.wait_ge(*full("pTn", b - 1))
                for half in range(2):
                    act.activation(p_dec[0:64, 512 * half:512 * half + 512], bank("Sd", b, half)[0:64, :],
                                   ACT.Exp, bias=SC[0:64, 2:3], scale=DK ** -0.5,
                                   accum_out=SC[0:64, 3 + half:4 + half])\
                        .then_inc(free_sem("Sd", b, half), 1)
                    act.wait_ge(*drained("Sd", b, half))
                act.activation(p_dec[0:64, nk:nk + TS], s_new[0:64, :], ACT.Exp, bias=SC[0:64, 2:3],
                               scale=DK ** -0.5, accum_out=SC[0:64, 5:6]).then_inc(dec_exp, 1)
                act.wait_ge(*own(dec_exp))
                if b + 1 < NB:
                    key_pages(b + 1)
                act.wait_ge(*full("pTn", b))
                copy(pTn[0:TS, :], bank("pTn", b)[0:TS, 0:64]).then_inc(free_sem("pTn", b), 1)
                act.wait_ge(*drained("pTn", b))

            root(o_rms)

            act.wait_ge(region_m, 1)
            for i, key in enumerate(("qm", "km")):
                for m in range(4):
                    act.wait_ge(*full(key, m))
                    copy(raw_p[:, 4 * i + m, 3:TP + 3], bank(key, m)[:, 0:TP])
                    copy(raw_s[:, 4 * i + m, :, 3:11],
                         bank(key, m)[:, TP:NT].rearrange("p (b t) -> p b t", b=NB))\
                        .then_inc(free_sem(key, m), 1)
                    act.wait_ge(*drained(key, m))
            act.wait_ge(f_abs, 1)
            act.activation(rows_t[0:H, :], rows_t[0:H, :], ACT.Exp, scale=-1.0).then_inc(act_step, 1)
            act.wait_ge(act_step, 1)
            act.activation(rows_t[0:H, :], rows_t[0:H, :], ACT.Ln, bias=1.0).then_inc(f_ln, 1)
            act.wait_ge(*own(f_ln))
            for j, (t0, n) in enumerate(TILES):
                act.wait_ge(*full("vm", j))
                copy(vm[0:n, j, :], bank("vm", j)[0:n, :]).then_inc(free_sem("vm", j), 1)
                act.wait_ge(*drained("vm", j))
            for m in range(4):
                act.wait_ge(*full("om", m))
                act.activation(so[:, m, :], bank("om", m)[:, 0:NT], ACT.Sigmoid).then_inc(free_sem("om", m), 1)
                act.wait_ge(*drained("om", m))
            act.wait_ge(conv_done, 1)
            act.activation(cv_sig, cv[:, 0:4, :], ACT.Sigmoid).then_inc(conv_sig, 1)
            act.wait_ge(*own(conv_sig))
            act.wait_ge(conv_done, 2)
            act.wait_ge(conv_ready, 1)
            act.activation(cv_sig, cv[:, 4:8, :], ACT.Sigmoid).then_inc(conv_sig, 1)
            act.wait_ge(*own(conv_sig))
            act.wait_ge(tail_ready, 1)
            for half in range(2):
                act.wait_ge(*full("tail", half))
                copy(tail_rows[0:27, 512 * half:512 * half + 512], bank("tail", half)[0:27, :])\
                    .then_inc(free_sem("tail", half), 1)
                act.wait_ge(*drained("tail", half))
            act.wait_ge(m_rows, 1)
            act.activation(rowsR[0:H, NT:2 * NT], rows_t[0:H, :], ACT.Exp, scale=-1.0).then_inc(m_exp, 1)
            act.wait_ge(*own(m_exp))
            act.activation(rowsR[0:H, 2 * NT:2 * NT + TS], rowsR[0:H, 2 * NT:2 * NT + TS], ACT.Exp)\
                .then_inc(m_exp, 1)
            act.wait_ge(*own(m_exp))
            act.activation(rows_w[0:H, :], rows_w[0:H, :], ACT.Exp).then_inc(m_exp, 1)
            act.wait_ge(*own(m_exp))
            for h in range(H):
                act.wait_ge(*full("bc1", h))
                if h:
                    act.wait_ge(c_ready, h)
                copy(bcS, bank("bc1", h)[:, 0:384]).then_inc(free_sem("bc1", h), 1)
                act.wait_ge(*drained("bc1", h))
                act.wait_ge(*drained("bc0", h))
                act.activation(dT[:, 0:384], dT[:, 0:384], ACT.Exp)
                act.activation(dT[0:TS, 384:448], dT[0:TS, 384:448], ACT.Exp).then_inc(d_exp, 1)
                act.wait_ge(*own(d_exp))
            act.wait_ge(*full("n_out"))
            copy(n_rows[0:36, :], bank("n_out")[0:36, 0:P]).then_inc(free_sem("n_out"), 1)
            act.wait_ge(*drained("n_out"))

            root(hmT[:])

            act.wait_ge(tail_out, 32)
            for w in ("ga0", "ga1", "gb0", "gb1"):
                for m in range(4):
                    mm_ = m + 4 * int(w[2])
                    act.wait_ge(*full(w, m))
                    if w[1] == "b":
                        act.wait_ge(*drained("upa", mm_))
                    act.activation(sg[:, mm_, :], bank(w, m)[:, 0:NT], ACT.Sigmoid)\
                        .then_inc(free_sem(w, m), 1)
                    act.wait_ge(*drained(w, m))
            root(rstd[:])
            for j, (t0, n) in enumerate(TILES):
                for half in range(2):
                    act.wait_ge(*full("h2", j, half))
                    copy(h2_tok[0:n, j, 512 * half:512 * half + 512], bank("h2", j, half)[0:n, :])\
                        .then_inc(free_sem("h2", j, half), 1)
                    act.wait_ge(*drained("h2", j, half))
            act.wait_ge(top_diff, 1)
            act.activation(ew, ew, ACT.Exp).then_inc(top_exp, 1)
            act.wait_ge(*own(top_exp))
            for m in range(KT):
                act.wait_ge(*full("bd", m))
                copy(accT[:, m, :], bank("bd", m)[:, 0:NT]).then_inc(free_sem("bd", m), 1)
                act.wait_ge(*drained("bd", m))

            def copy_gathered(g):
                for half in range(2):
                    act.wait_ge(gathered, 2 * g + (1 + half))
                    copy(hgT[:, 4 * half:4 * half + 4, :],
                         psum[:, BANK_Q[half], :].rearrange("p (k s) -> p k s", k=4)).then_inc(hg_copied, 1)

            def expert_block(n, g, prefetch):
                if not prefetch:
                    copy_gathered(g)
                act.wait_ge(selw_turned, n + 1)
                act.wait_ge(combined, KT * n)
                copy(selwT, psum[:, BANK_P[0], 0:NT]).then_inc(selw_copied, 1)
                for c in range(2):
                    act.wait_ge(gate_ready, 2 * n + (1 + c))
                    act.wait_ge(act_ready, 2 * n + c)
                    act.activation(act_s, act_g, ACT.Sigmoid, scale=ALPHA).then_inc(gate_sig, 1)
                if prefetch:
                    copy_gathered(g + 1)
                act.wait_ge(down_done, n + 1)
                for half in range(2):
                    copy(yT[:, 4 * half:4 * half + 4, :],
                         psum[:, BANK_P[half], :].rearrange("p (k s) -> p k s", k=4)).then_inc(yT_copied, 1)
                for half in range(2):
                    act.wait_ge(y_turned, 2 * n + (1 + half))
                    copy(y_rows[:, 512 * half:512 * half + 512], psum[:, BANK_Q[half], :])\
                        .then_inc(y_copied, 1)

            act.wait_ge(tables, 1)
            copy_gathered(0)
            with act.Fori(0, NE) as n:
                expert_block(n, n, True)
            more_n = act.value_load(ints[0:1, AT_MORE:AT_MORE + 1], min_val=0, max_val=MAX_MORE)
            with act.If(more_n > 0):
                with act.Fori(0, more_n) as i:
                    expert_block(i + NE, i + (NE + 1), False)
            with act.Else():
                act.nop()
            root(rstd[:])
            for j, (t0, n) in enumerate(TILES):
                for half in range(2):
                    act.wait_ge(*full("y", j, half))
                    copy(y_out[0:n, j, 512 * half:512 * half + 512], bank("y", j, half)[0:n, :])\
                        .then_inc(free_sem("y", j, half), 1)
                    act.wait_ge(*drained("y", j, half))

        @block.gpsimd
        def _(pool):
            pool.dma_start(keep[:], I["const"][:, 0:n_keep]).then_inc(const_in, 16)
            c2 = I["c_sample"]
            pool.dma_start(c_rows[0:1, :], I["c_prompt"]).then_inc(c_in, 16)
            pool.dma_start(c_rows[1:9, :], c2).then_inc(c_in, 16)
            row = 0
            for name, n in (("b_ada", 48), ("g_norm1", 8), ("g_norm2", 8), ("g_final", 8), ("w_conv", 32),
                            ("b_conv", 8), ("g_subln", 1), ("g_mnorm", 4)):
                src = I[name].rearrange("a b -> (a b)").rearrange("(r c) -> r c", c=P)
                pool.dma_start(vec_rows[row:row + n, :], src).then_inc(vec_in, 16)
                row += n
            pool.dma_start(front_const, I["const"][:, n_keep:n_const]).then_inc(vec_in, 16)
            bg = I["b_gu"].rearrange("e (m c) -> (e m) c", c=P).rearrange("(t r) c -> t r c", r=P)
            for t in range(4):
                pool.dma_start(bgu_rows[:, t, :], bg[t]).then_inc(table_in, 16)
            for i, name in enumerate(("lambda_q1", "lambda_k1", "lambda_q2", "lambda_k2")):
                pool.dma_start(lam_rows[:, i, :], I[name].to_broadcast([P, DK])).then_inc(table_in, 16)
            with nc.allow_non_contiguous_dma(reason="a few words"):
                pool.dma_start(small[0:H, 21:29], I["state_m"].rearrange("b h -> h b")).then_inc(table_in, 16)
                pool.dma_start(small[0:H, 29:30], I["b_gates"].rearrange("o h -> h o")[0:H])\
                    .then_inc(table_in, 16)
                pool.dma_start(small[0:H, 30:31], I["b_gates"].rearrange("o h -> h o")[H:2 * H])\
                    .then_inc(table_in, 16)
            for w, tile_, name in (("k", k_rot, "k"), ("v", va, "v")):
                for j, (t0, n) in enumerate(TILES):
                    if w == "k":
                        pool.wait_ge(rotated, 4 + j)
                    else:
                        pool.wait_ge(*drained("v", j))
                    dst = O[name + "_prompt"][t0:t0 + n, :] if j < 2 else O[name + "_sample"]
                    pool.dma_start(dst, tile_[0:n, j, :]).then_inc(k_stored, 16)
            pool.wait_ge(region_m, 1)
            pool.wait_ge(k_stored, 96)
            pool.dma_start(cs_rows[0:24, :], I["state_conv"]).then_inc(mrows_in, 16)
            pool.dma_start(n_rows[0:32, :], I["state_n"]).then_inc(mrows_in, 16)
            with nc.allow_non_contiguous_dma(reason="eight gate columns"):
                pool.dma_start(w_if, W_IN.rearrange("(k p) c -> p k c", p=P)[:, :, 3584:3592])\
                    .then_inc(mrows_in, 16)
            for half in range(2):
                pool.wait_ge(*drained("tail", half))
            pool.dma_start(O["conv_prompt"], tail_rows[0:3, :]).then_inc(tail_out, 16)
            pool.dma_start(O["conv_sample"], tail_rows[3:27, :]).then_inc(tail_out, 16)
            pool.wait_ge(m_rows, 1)
            with nc.allow_non_contiguous_dma(reason="a few words"):
                pool.dma_start(O["m_prompt"], rows_t[0:H, TP - 1:TP]).then_inc(state_out, 16)
                pool.dma_start(O["m_sample"].rearrange("b h -> h b"), rows_t[0:H, TP + TD - 1:NT:TD])\
                    .then_inc(state_out, 16)
            pool.wait_ge(c_ready, H)
            pool.dma_start(O["C_prompt"].rearrange("h d e -> d h e"), C_p).then_inc(state_out, 16)
            pool.dma_start(O["C_sample"].rearrange("b h d e -> d (b h) e"), unit(("C", 0), 32))\
                .then_inc(state_out, 16)
            pool.wait_ge(*drained("n_out"))
            pool.dma_start(O["n_prompt"], n_rows[0:4, :]).then_inc(state_out, 16)
            pool.dma_start(O["n_sample"], n_rows[4:36, :]).then_inc(state_out, 16)
            pool.wait_ge(state_out, 96)
            pool.wait_ge(hm_ready, 1)
            pool.dma_start(w_rt, I["w_router"].rearrange("(k p) e -> p k e", p=P)).then_inc(moe_in, 16)
            pool.dma_start(b_rt, I["b_router"].to_broadcast([P, NE])).then_inc(moe_in, 16)
            pool.dma_start(bd_rows[0:NE, :], I["b_down"]).then_inc(moe_in, 16)
            for j, (t0, n) in enumerate(TILES):
                for half in range(2):
                    pool.wait_ge(*drained("y", j, half))
                dst = O["y_prompt"][t0:t0 + n, :] if j < 2 else O["y_sample"]
                pool.dma_start(dst, y_out[0:n, j, :]).then_inc(y_stored, 16)
            pool.wait_ge(y_stored, 48)

        @block.sync
        def _(sp):
            sp.dma_start(ints[0:1, 0:64], I["page_table"]).then_inc(page_in, 16)
            x = I["x_prompt"]
            for j in range(2):
                sp.dma_start(x_tok[:, j, :], x[P * j:P * j + P, :]).then_inc(x_in, 16)
            sp.dma_start(x_tok[0:TS, 2, :], I["x_sample"]).then_inc(x_in, 16)
            sp.wait_ge(page_in, 16)
            for i, (name, n_dma) in enumerate(units):
                if i >= RING:
                    freed = units[i - RING][0]
                    if freed == ("C", 0):
                        sp.wait_ge(state_out, 96)
                    else:
                        sp.wait_ge(*last_use[freed])
                s = slot_of[name]
                if name[0] in "KV" and len(name[0]) == 1:
                    cache = I["cache_k" if name[0] == "K" else "cache_v"]
                    dst = unit(name, PAGES)
                    for g in range(PAGES):
                        page = sp.value_load(ints[0:1, PAGES * name[1] + g:PAGES * name[1] + g + 1],
                                             min_val=0, max_val=N_POOL - 1)
                        sp.dma_start(dst[:, g, :],
                                     cache[bass.ds(page, 1), :, :].rearrange("o p c -> p (o c)"))\
                            .then_inc(unit_landed[s], 16)
                else:
                    src, a = unit_source(name)
                    sp.dma_start(unit(name, a), src).then_inc(unit_landed[s], 16)

            gu = I["w_gu"].rearrange("e (k p) (g c f) -> e p k g c f", p=P, g=2, c=2)
            dn = I["w_down"].rearrange("e (k p) f -> e p k f", p=P)
            freed_by = [gu_half[0], gu_done[0], gu_half[1], gu_done[1], down_half, down_done]

            def expert_weights(e, n):
                for i in range(RING):
                    if n is not None:
                        sp.wait_ge(freed_by[i], n)
                    else:
                        freed = units[len(units) - RING + i][0]
                        sp.wait_ge(*last_use[freed])
                    at = e if isinstance(e, int) else None
                    ex = slice(e, e + 1) if at is not None else bass.ds(e, 1)
                    if i < 4:
                        c, half = i // 2, i % 2
                        dst = ring[:, moe_slot[i], :].rearrange("p (k g f) -> p k g f", k=4, g=2)
                        for g in range(2):
                            src = gu[ex, :, 4 * half:4 * half + 4, g, c, :].rearrange("o p k f -> p (o k) f")
                            sp.dma_start(dst[:, :, g, :], src).then_inc(unit_landed[moe_slot[i]], 16)
                    else:
                        half = i - 4
                        src = dn[ex, :, 4 * half:4 * half + 4, :].rearrange("o p k f -> p (o k) f")
                        dst = ring[:, moe_slot[i], :].rearrange("p (k f) -> p k f", k=4)
                        sp.dma_start(dst, src).then_inc(unit_landed[moe_slot[i]], 16)

            expert_weights(0, None)
            with sp.Fori(1, NE) as n:
                expert_weights(n, n)
            sp.wait_ge(tables, 1)
            more_n = sp.value_load(ints[0:1, AT_MORE:AT_MORE + 1], min_val=0, max_val=MAX_MORE)
            with sp.If(more_n > 0):
                with sp.Fori(0, more_n) as i:
                    e = sp.value_load(ints[0:1, bass.ds(i + AT_EXPERT, 1)], min_val=0, max_val=NE - 1)
                    expert_weights(e, i + NE)
            with sp.Else():
                sp.nop()


_OUTS = [
    ("y_prompt", (TP, D), (1, TP, D)), ("y_sample", (TS, D), (NB, TD, D)),
    ("k_prompt", (TP, 512), (1, 1, TP, H, 2, DK)), ("v_prompt", (TP, 512), (1, 1, TP, H, P)),
    ("conv_prompt", (3, D), (1, 1, 3, D)), ("C_prompt", (H, P, P), (1, 1, H, P, P)),
    ("n_prompt", (H, P), (1, 1, H, P)), ("m_prompt", (H, 1), (1, 1, H)),
    ("k_sample", (TS, 512), (1, NB, TD, H, 2, DK)), ("v_sample", (TS, 512), (1, NB, TD, H, P)),
    ("conv_sample", (NB * 3, D), (1, NB, 3, D)), ("C_sample", (NB, H, P, P), (1, NB, H, P, P)),
    ("n_sample", (NB * H, P), (1, NB, H, P)), ("m_sample", (NB, H), (1, NB, H)),
]
_INS = {
    "x_prompt": (TP, D), "x_sample": (TS, D), "c_prompt": (1, D), "c_sample": (NB, D),
    "cache_k": (N_POOL, P, 512), "cache_v": (N_POOL, P, 512), "state_conv": (NB * 3, D),
    "state_C": (NB, H, P, P), "state_n": (NB * H, P), "state_m": (NB, H), "page_table": (1, 64),
    "w_ada": (D, 6 * D), "b_ada": (1, 6 * D), "g_norm1": (1, D), "g_norm2": (1, D), "w_in": (D, 5640),
    "b_gates": (1, 8), "lambda_q1": (1, DK), "lambda_k1": (1, DK), "lambda_q2": (1, DK),
    "lambda_k2": (1, DK), "g_subln": (1, P), "w_conv": (4, D), "b_conv": (1, D), "g_mnorm": (1, 512),
    "w_up_a": (512, D), "w_up_b": (512, D), "w_out": (D, D), "w_router": (D, NE), "b_router": (1, NE),
    "w_gu": (NE, D, 2 * FF), "b_gu": (NE, 2 * FF), "w_down": (NE, FF, D), "b_down": (NE, D),
    "g_final": (1, D),
}


def kernel(**inputs):
    import concourse.bacc as _bacc
    from concourse.bass_utils import run_bass_kernel_spmd as _run

    nc = _bacc.Bacc("TRN2", target_bir_lowering=False, num_devices=1)
    pack, const_at, n_keep = const_pack()
    arrays = {"in_const": pack}
    I = {"const": nc.dram_tensor("in_const", pack.shape, F32, kind="ExternalInput").ap()}
    for name, shape in _INS.items():
        a = np.ascontiguousarray(inputs[name]).reshape(shape)
        arrays["in_" + name] = a
        I[name] = nc.dram_tensor("in_" + name, shape, mybir.dt.from_np(a.dtype), kind="ExternalInput").ap()
    O = {name: nc.dram_tensor("out_" + name, shape, F32, kind="ExternalOutput").ap()
         for name, shape, _ in _OUTS}
    build(nc, I, O, const_at, pack.shape[1], n_keep)
    r = _run(nc, [arrays], core_ids=[0])
    return tuple(r.results[0]["out_" + name].reshape(final) for name, _, final in _OUTS)
```

```python
from contextlib import ExitStack

import concourse.bass as bass
import numpy as np
from concourse import mybir

F32 = mybir.dt.float32
BF16 = mybir.dt.bfloat16
I32 = mybir.dt.int32
U32 = mybir.dt.uint32
ALU = mybir.AluOpType
ACT = mybir.ActivationFunctionType
AX = mybir.AxisListType.X

P = 128
D = 1024
KT = D // P
TP = 256
NB, TD = 8, 8
TS = NB * TD
NT = TP + TS
TILES = [(0, 128), (128, 128), (256, 64)]
H = 4
DK = 64
PAGES, PAGE = 8, 128
N_POOL = 80
NE = 32
TOPK = 4
FF = 1024
EPS = 1e-6
LAM_INIT = 0.8 - 0.6
LIMIT, ALPHA = 7.0, 1.702
BIG = -1e30
RING = 6
REGION = 18120
UNIT = 4096
SLOTS = 64
ROUNDS = -(-NT // SLOTS)
MAX_BLOCKS = NE + NT * TOPK // SLOTS
AT_EXPERT = 64
AT_COLUMN = AT_EXPERT + MAX_BLOCKS + 1
AT_BLOCKS = AT_COLUMN + MAX_BLOCKS + 1
AT_LATER = AT_BLOCKS + NE
N_INTS = AT_LATER + 1


def const_pack():
    cols, at, n = [], {}, 0

    def put(name, a):
        nonlocal n
        full = np.zeros((P, a.shape[1]), np.float32)
        full[:a.shape[0]] = a
        at[name] = (n, a.shape[1])
        cols.append(full)
        n += a.shape[1]

    i = np.arange(P)
    le = (i[:, None] <= i[None, :]).astype(np.float32)
    s = np.arange(TS)
    blk = ((s[:, None] // TD == s[None, :] // TD) & (s[:, None] <= s[None, :])).astype(np.float32)
    blk128 = np.zeros((P, TS), np.float32)
    blk128[:TS] = blk
    put("ident", np.eye(P, dtype=np.float32))
    put("causal", np.concatenate([le, np.ones((P, P), np.float32), le, blk128], 1))
    put("before", (i[:, None] < i[None, :]).astype(np.float32))
    put("iota", np.tile(i.astype(np.float32), (P, 1)))
    put("valid", np.stack([np.ones(P), np.ones(P), i < TS], 1).astype(np.float32))
    put("blkind", (s[:, None] // TD == np.arange(NB)[None, :]).astype(np.float32))
    put("slots", np.tile(i % SLOTS, (P, 1)).astype(np.float32))
    put("rounds", np.tile(np.arange(1, ROUNDS) * SLOTS + 0.5, (P, 1)).astype(np.float32))
    put("expert_hot", np.concatenate([np.tile(np.eye(NE), (3, 1)), np.zeros((3 * NE, 1))],
                                     1).astype(np.float32))
    keep = n
    put("attmask", np.concatenate([np.zeros((P, P)), np.where(i[None, :] <= i[:, None], 0, BIG)],
                                  1).astype(np.float32))
    r = np.arange(P)
    key = s
    ok = (key[None, None, :] // TD == np.arange(NB)[None, :, None]) & \
         (key[None, None, :] % TD <= (r % TD)[:, None, None])
    put("newmask", np.where(ok, 0, BIG).astype(np.float32).reshape(len(r), -1))
    pos = np.concatenate([np.arange(TP), PAGES * PAGE + np.arange(TS) % TD]).astype(np.float32)
    inv = np.float32(10000.0) ** (-np.arange(DK // 2, dtype=np.float32) * np.float32(2.0) / np.float32(DK))
    ang = pos[:, None] * inv[None, :].astype(np.float32)
    for name, f in (("cos", np.cos), ("sin", np.sin)):
        t = np.zeros((P, 3, DK // 2), np.float32)
        for j, (t0, m) in enumerate(TILES):
            t[:m, j] = f(ang[t0:t0 + m])
        put(name, t.reshape(P, -1))
    put("comp", np.stack([(r // TD) % 2 == 0, (r // TD) % 2 == 1], 1).astype(np.float32))
    sel = np.zeros((H, H, P), np.float32)
    for h in range(H):
        sel[h, h] = 1
    put("hsel", sel.reshape(H, -1))
    start = np.zeros(NT, bool)
    start[[0] + [TP + TD * b for b in range(NB)]] = True
    put("carry", np.tile(np.where(start, 0, 1).astype(np.float32), (H, 1)))
    put("drop", np.tile(np.where(start, BIG, 0).astype(np.float32), (H, 1)))
    return np.concatenate(cols, 1), at, keep


def build(nc, I, O, const_at, n_const, n_keep):
    ctx = ExitStack()
    with ctx:
        def sb(name, shape, dt=F32):
            return ctx.enter_context(nc.sbuf_tensor(name, shape, dt))

        def sem(name):
            return ctx.enter_context(nc.semaphore(name))

        ring = sb("ring", [P, RING, UNIT])
        xT = sb("xT", [P, KT, NT])
        hT = sb("hT", [P, KT, NT])
        keep = sb("keep", [P, n_keep])
        vecT = sb("vecT", [P, 128])
        bias_hot = sb("bias_hot", [P, SLOTS], BF16)
        modT = sb("modT", [P, 48, 9])
        gainT = sb("gainT", [P, 2, KT, 9])
        rstd = sb("rstd", [P, NT])
        cT = sb("cT", [P, KT, 32])
        small = sb("small", [P, 64])
        oT = sb("oT", [P, H, NT])
        hmT = sb("hmT", [P, H, NT])
        region = sb("region", [P, REGION])
        ints = sb("ints", [1, N_INTS], I32)
        psum = ctx.enter_context(nc.psum_tensor("psum", [P, 8, 512], F32))

        def const(name, rows=P):
            a, m = const_at[name]
            if a + m <= n_keep:
                return keep[0:rows, a:a + m]
            return front_const[0:rows, a - n_keep:a - n_keep + m]

        class Area:
            def __init__(self, start):
                self.at = start

            def take(self, *shape):
                m = int(np.prod(shape))
                v = region[:, self.at:self.at + m]
                self.at += m
                assert self.at <= REGION, self.at
                if len(shape) == 2:
                    v = v.rearrange("p (a b) -> p a b", a=shape[0])
                if len(shape) == 3:
                    v = v.rearrange("p (a b c) -> p a b c", a=shape[0], b=shape[1])
                return v

        front_area = Area(0)
        front_const = front_area.take(n_const - n_keep)
        A = Area(front_area.at)
        va = A.take(3, 512)
        qT = A.take(H, NT)
        kT = A.take(H, NT)
        q_rot = A.take(2, 512)
        k_rot = A.take(3, 512)
        pairs = A.take(H, 256)
        q_blocks = A.take(NB, P)
        kTb = A.take(H, PAGES * PAGE)
        B = Area(A.at - H * PAGES * PAGE)
        x_tok = B.take(3, D)
        c_rows = B.take(D)
        B = Area(A.at - H * PAGES * PAGE)
        s_pair = B.take(2, 2, 256)
        aT = B.take(2, 256)
        x_sq = Area(front_area.at).take(KT, NT)
        c_sig = q_rot.rearrange("p a b -> p (a b)")
        vec_rows = k_rot[:, 0, 0:P]
        lam_rows = k_rot[:, 1, 0:256].rearrange("p (a b) -> p a b", a=4)
        p_dec = A.take(PAGES * PAGE + TS)
        pT_dec = A.take(PAGES, P)
        pTn = A.take(P)
        o_rows = A.take(P)
        s_new = A.take(64)
        o_sq = Area(front_area.at).take(H, NT)
        o_rms = Area(front_area.at + H * NT).take(H, NT)
        M = Area(front_area.at)
        raw_p = M.take(8, TP + 3)
        raw_s = M.take(8, NB, 11)
        cv = M.take(8, NT)
        cv_sig = M.take(H, NT)
        vm = M.take(3, 512)
        so = M.take(H, NT)
        rowsR = M.take(704)
        rows_u = M.take(NT)
        rows_w = M.take(NT)
        rows_f = M.take(NT)
        rows_li = M.take(NT)
        rows_t = M.take(NT)
        w_if = M.take(KT, 8)
        uw = M.take(3, 8)
        dT = M.take(448)
        bcS = M.take(384)
        qe = M.take(2, 64)
        kw = M.take(3, P)
        v_blk = M.take(NB, P)
        hr = M.take(H, NT)
        hsq = M.take(NT)
        den_s = rstd[:]
        C_p = cv_sig.rearrange("p a b -> p (a b)")[:, 0:512].rearrange("p (a b) -> p a b", a=H)
        tail = dT[:, 0:216].rearrange("p (a b) -> p a b", a=8)
        tail_rows = raw_p.rearrange("p a b -> p (a b)")[:, 0:D]
        n0T = M.take(32)
        nT = M.take(36)
        n_rows = M.take(P)
        cs_rows = cv.rearrange("p a b -> p (a b)")[:, 0:D]
        ada_rows = hmT[:].rearrange("p h t -> p (h t)")[:, 0:1024].rearrange("p (g c) -> p g c", g=2)
        G = Area(front_area.at)
        sg = G.take(KT, NT)
        mT = G.take(KT, NT)
        E = Area(0)
        h2_tok = E.take(3, D)
        accT = E.take(KT, NT)
        fin_at = E.at
        fin_sq = Area(fin_at).take(KT, NT)
        bias_f32 = Area(E.at + KT * NT).take(2 * FF)
        act_g = E.take(512)
        act_s = E.take(512)
        act_u = E.take(512)
        hg_rows = E.take(512)
        y_rows = E.take(512)
        actT = E.take(4, P)
        hgT = E.take(4, P)
        sel = E.take(3, SLOTS)
        selw = E.take(3, P)
        selwT = E.take(NT)
        E.at = max(E.at, fin_at + KT * NT + 2 * FF)
        logits = E.take(3, NE)
        mask = E.take(3, NE)
        wts = E.take(3, NE)
        eq = E.take(3, NE)
        eqw = E.take(3, NE)
        pos = E.take(3, ROUNDS * NE)
        wts3 = E.take(3, ROUNDS * NE)
        top8 = E.take(3, 8)
        idxf = E.take(3, 8)
        ew = E.take(3, 4)
        esum = E.take(3)
        b_rt = E.take(NE)
        w_rt = E.take(KT, NE)
        wT = E.take(NT)
        bd_rows = E.take(D)
        plan = E.take(2 + ROUNDS)
        begun = E.take(MAX_BLOCKS + 1)
        plan_row = E.take(MAX_BLOCKS + 1)
        y_out = h2_tok
        top_ix = sb("top_ix", [P, 3, 8], U32)
        gu_bias = oT[:].rearrange("p h t -> p (h t)").bitcast(BF16)[0:3 * NE, 0:2 * FF]

        V_ADA, V_G1, V_G2, V_GF, V_WC, V_BC, V_GS, V_GM = 0, 48, 56, 64, 72, 104, 112, 113

        LAM, NLAM, COEF, GS = small[:, 0:4], small[:, 4:5], small[:, 5:6], small[:, 6:7]
        MX, LS, RC = small[:, 8:12], small[:, 12:16], small[:, 16:20]
        M0 = small[0:H, 20:29]
        BG = small[0:H, 29:31]
        SC = small[:, 32:40]

        bank_full = [sem(f"bank_full{i}") for i in range(8)]
        bank_free = [sem(f"bank_free{i}") for i in range(8)]
        unit_landed = [sem(f"unit_landed{i}") for i in range(RING)]
        const_in = sem("const_in")
        x_in = sem("x_in")
        c_in = sem("c_in")
        vec_in = sem("vec_in")
        table_in = sem("table_in")
        mrows_in = sem("mrows_in")
        moe_in = sem("moe_in")
        dve_step = sem("dve_step")
        act_step = sem("act_step")
        pool_step = sem("pool_step")
        unit_used = sem("unit_used")
        c_sig_done = sem("c_sig_done")
        c_silu = sem("c_silu")
        x_squared = sem("x_squared")
        lam_dot = sem("lam_dot")
        lam_exp = sem("lam_exp")
        h_ready = sem("h_ready")
        rotated = sem("rotated")
        k_stored = sem("k_stored")
        q_blocked = sem("q_blocked")
        att_max = sem("att_max")
        att_exp = sem("att_exp")
        att_a = sem("att_a")
        dec_max = sem("dec_max")
        dec_exp = sem("dec_exp")
        o_squared = sem("o_squared")
        o_ready = sem("o_ready")
        region_m = sem("region_m")
        conv_done = sem("conv_done")
        conv_sig = sem("conv_sig")
        conv_ready = sem("conv_ready")
        tail_ready = sem("tail_ready")
        tail_out = sem("tail_out")
        f_abs = sem("f_abs")
        f_ln = sem("f_ln")
        m_rows = sem("m_rows")
        m_exp = sem("m_exp")
        d_ready = sem("d_ready")
        d_exp = sem("d_exp")
        p_ready = sem("p_ready")
        qe_ready = sem("qe_ready")
        kw_ready = sem("kw_ready")
        h_squared = sem("h_squared")
        hm_ready = sem("hm_ready")
        c_ready = sem("c_ready")
        state_out = sem("state_out")
        merged = sem("merged")
        x1_ready = sem("x1_ready")
        x1_squared = sem("x1_squared")
        h2_ready = sem("h2_ready")
        top_diff = sem("top_diff")
        top_exp = sem("top_exp")
        routed = sem("routed")
        blocks_ready = sem("blocks_ready")
        begun_ready = sem("begun_ready")
        bias_in = sem("bias_in")
        tables = sem("tables")
        mean_inverse = sem("mean_inverse")
        mean_root = sem("mean_root")
        page_in = sem("page_in")
        tail_step = sem("tail_step")
        unit_read = [sem(f"unit_read{i}") for i in range(RING)]
        gate_clamped = sem("gate_clamped")
        gate_sig = sem("gate_sig")
        gs_ready = sem("gs_ready")
        up_clamped = sem("up_clamped")
        act_ready = sem("act_ready")
        act_turned = sem("act_turned")
        actT_copied = sem("actT_copied")
        bias_hot_ready = sem("bias_hot_ready")
        sel_ready = sem("sel_ready")
        gathered = sem("gathered")
        hg_copied = sem("hg_copied")
        hg_turned = sem("hg_turned")
        hgT_copied = sem("hgT_copied")
        selw_ready = sem("selw_ready")
        selw_turned = sem("selw_turned")
        selwT_copied = sem("selwT_copied")
        y_copied = sem("y_copied")
        combined = sem("combined")
        added = sem("added")
        acc_final = sem("acc_final")
        x2_ready = sem("x2_ready")
        x2_squared = sem("x2_squared")
        y_stored = sem("y_stored")

        groups, used, turn = {}, [0] * 8, {}

        def claim(pe, pool, *key):
            k = turn.get(pool, 0)
            turn[pool] = k + 1
            b = pool[k % len(pool)]
            if used[b]:
                pe.wait_ge(bank_free[b], used[b])
            used[b] += 1
            groups[key] = (b, used[b])
            return psum[:, b, :]

        def bank(*key):
            return psum[:, groups[key][0], :]

        def full(*key):
            return bank_full[groups[key][0]], groups[key][1]

        def full_sem(*key):
            return bank_full[groups[key][0]]

        def drained(*key):
            return bank_free[groups[key][0]], groups[key][1]

        def free_sem(*key):
            return bank_free[groups[key][0]]

        units, last_use, ada_used = [], {}, [0]

        def next_used():
            ada_used[0] += 1
            return ada_used[0]

        def add_unit(name, n_dma=1):
            units.append((name, n_dma))

        for i in range(4):
            add_unit(("ada", i))
        for w in "qkv":
            add_unit((w, 0))
        for b in range(NB):
            add_unit(("K", b), PAGES)
            add_unit(("V", b), PAGES)
        for w in ("qm", "km", "vm", "om"):
            add_unit((w, 0))
        for i in range(4, 12):
            add_unit(("ada", i))
        add_unit(("C", 0))
        for w in ("ga0", "ga1", "upa", "gb0", "gb1", "upb", "wo0", "wo1"):
            add_unit((w, 0))
        slot_of, landed_at, count = {}, {}, [0] * RING
        for i, (name, n_dma) in enumerate(units):
            s = i % RING
            count[s] += 16 * n_dma
            slot_of[name], landed_at[name] = s, count[s]
        first_slot = len(units) % RING
        moe_slot = [(first_slot + i) % RING for i in range(RING)]
        landed_base = [count[moe_slot[i]] for i in range(RING)]

        def unit(name, a, b=None):
            v = ring[:, slot_of[name], :]
            return v.rearrange("p (a b) -> p a b", a=a)

        def landed(name):
            return unit_landed[slot_of[name]], landed_at[name]

        W_IN = I["w_in"]
        PIECE = {"q": 0, "k": 512, "v": 1024, "qm": 1536, "km": 2048, "vm": 2560, "om": 3072,
                 "ga0": 3592, "ga1": 4104, "gb0": 4616, "gb1": 5128}

        def unit_source(name):
            w, i = name
            if w == "ada":
                return I["w_ada"].rearrange("(k p) c -> p k c", p=P)[:, :, 512 * i:512 * (i + 1)], 8
            if w in PIECE:
                return W_IN.rearrange("(k p) c -> p k c", p=P)[:, :, PIECE[w]:PIECE[w] + 512], 8
            if w in ("upa", "upb"):
                return I["w_up_a" if w == "upa" else "w_up_b"].rearrange("(k p) c -> p k c", p=P), 4
            if w in ("wo0", "wo1"):
                k = 4 * int(w[2])
                return I["w_out"].rearrange("(k p) c -> p k c", p=P)[:, k:k + 4, :], 4
            assert w == "C"
            return I["state_C"].rearrange("b h d e -> d (b h) e"), 32

        GA = psum[:, 0:2, :]
        GB = psum[:, 2:4, :]
        B_GATE, B_UP, B_Y, B_HG, B_ACT_T, B_SEL_T, B_HG_T = 0, 1, 2, 3, 4, 5, 6
        B_SUM = (6, 4)

        block = ctx.enter_context(nc.Block())

        @block.tensor
        def _(pe):
            def mm(out, lhsT, rhs, start, stop):
                return pe.matmul(out, lhsT, rhs, start=start, stop=stop, skip_group_check=True)

            ident = const("ident")
            ones = const("causal")[:, P:2 * P]
            LOW, HIGH, ALLB = (0, 1, 2, 3), (4, 5, 6, 7), (0, 1, 2, 3, 4, 5, 6, 7)

            pe.wait_ge(const_in, 16)
            pe.wait_ge(vec_in, 16 * 9)
            out = claim(pe, ALLB, "vec")
            pe.transpose(out[:, 0:117], vec_rows[0:117, :], ident[0:117, 0:117]).then_inc(full_sem("vec"), 1)
            pe.wait_ge(c_silu, 1)
            out = claim(pe, ALLB, "cT")
            for k in range(KT):
                last = pe.transpose(out[:, 9 * k:9 * k + 9], c_rows[0:9, P * k:P * k + P], ident[0:9, 0:9])
            last.then_inc(full_sem("cT"), 1)
            pe.wait_ge(x_in, 48)
            for j, (t0, n) in enumerate(TILES):
                for half in range(2):
                    out = claim(pe, ALLB, "xT", j, half)
                    for i in range(4):
                        k = 4 * half + i
                        last = pe.transpose(out[:, P * i:P * i + n], x_tok[0:n, j, P * k:P * k + P],
                                            ident[0:n, 0:n])
                    last.then_inc(full_sem("xT", j, half), 1)
            pe.wait_ge(x_squared, 1)
            out = claim(pe, ALLB, "ss1")
            for k in range(KT):
                last = mm(out[:, 0:NT], ones, x_sq[:, k, :], k == 0, k == KT - 1)
            last.then_inc(full_sem("ss1"), 1)

            def ada(g):
                out = claim(pe, ALLB, "ada", g)
                for i in range(4 * g, 4 * g + 4):
                    pe.wait_ge(*landed(("ada", i)))
                    w = unit(("ada", i), 8)
                    for k in range(KT):
                        for j in range(4):
                            last = mm(out[32 * j:32 * j + 32, P * (i % 4):P * (i % 4) + P], cT[:, k, :],
                                      w[:, k, P * j:P * j + P], k == 0, k == KT - 1)
                    if i % 4 < 3:
                        last.then_inc(unit_used, 1)
                        last_use[("ada", i)] = (unit_used, next_used())
                last.then_inc(full_sem("ada", g), 1)
                last_use[("ada", 4 * g + 3)] = full("ada", g)

            def turn_ada(g):
                pe.wait_ge(*drained("ada", g))
                out = claim(pe, ALLB, "adaT", g)
                for i in range(4):
                    last = pe.transpose(out[:, P * i:P * i + P], ada_rows[:, g % 2, P * i:P * i + P], ident)
                last.then_inc(full_sem("adaT", g), 1)

            pe.wait_ge(*drained("cT"))
            ada(0)
            turn_ada(0)

            pe.wait_ge(h_ready, 1)

            def token_major(name, pool, after=None):
                pe.wait_ge(*landed((name, 0)))
                w = unit((name, 0), 8)
                for j, (t0, n) in enumerate(TILES):
                    out = claim(pe, pool, name, j)
                    for k in range(KT):
                        last = mm(out[0:n, :], hT[:, k, t0:t0 + n], w[:, k, :], k == 0, k == KT - 1)
                    last.then_inc(full_sem(name, j), 1)
                    if after:
                        after(j)
                last_use[(name, 0)] = full(name, 2)

            def turn_heads(name, j):
                t0, n = TILES[j]
                pe.wait_ge(rotated, (0 if name == "q" else 3) + j + 1)
                out = claim(pe, HIGH, name + "T", j)
                src = q_rot[:, j % 2, :] if name == "q" else k_rot[:, j, :]
                for h in range(H):
                    last = pe.transpose(out[:, P * h:P * h + n], src[0:n, P * h:P * h + P], ident[0:n, 0:n])
                last.then_inc(full_sem(name + "T", j), 1)

            token_major("q", LOW)
            turn_heads("q", 0)
            token_major("k", LOW, lambda j: turn_heads("q", j + 1) if j < 2 else None)
            token_major("v", LOW, lambda j: turn_heads("k", j))

            items = [(h, qb) for h in range(H) for qb in range(2)]

            def att_scores(i):
                h, qb = items[i]
                for c in range(2):
                    out = claim(pe, LOW, "S", i, c)
                    mm(out[:, 0:P * (qb + 1)], qT[DK * c:DK * c + DK, h, P * qb:P * qb + P],
                       kT[DK * c:DK * c + DK, h, 0:P * (qb + 1)], True, True).then_inc(full_sem("S", i, c), 1)

            for w in "qk":
                for j in range(3):
                    pe.wait_ge(*drained(w + "T", j))
            for j in range(3):
                pe.wait_ge(*drained("v", j))
            att_scores(0)
            for i, (h, qb) in enumerate(items):
                if i + 1 < len(items):
                    att_scores(i + 1)
                pe.wait_ge(att_a, i + 1)
                out = claim(pe, (4, 5), "aT", i)
                for t in range(qb + 1):
                    last = pe.transpose(out[:, P * t:P * t + P], s_pair[:, i % 2, 0, P * t:P * t + P], ident)
                last.then_inc(full_sem("aT", i), 1)
                out = claim(pe, (6, 7), "PV", i)
                pe.wait_ge(*drained("aT", i))
                for t in range(qb + 1):
                    last = mm(out[:, 0:P], va[:, t, P * h:P * h + P], aT[:, i % 2, P * t:P * t + P],
                              t == 0, t == qb)
                last.then_inc(full_sem("PV", i), 1)

            def turn_keys(b):
                pe.wait_ge(*landed(("K", b)))
                kc = unit(("K", b), PAGES)
                for g in range(PAGES):
                    out = claim(pe, (0, 1), "kTb", b, g)
                    for h in range(H):
                        last = pe.transpose(out[:, P * h:P * h + P], kc[:, g, P * h:P * h + P], ident)
                    last.then_inc(full_sem("kTb", b, g), 1)
                last_use[("K", b)] = full("kTb", b, PAGES - 1)

            HEAD = [slice(32 * h, 32 * h + 32) for h in range(H)]

            def dec_scores(b):
                for half in range(2):
                    out = claim(pe, (4 + half,), "Sd", b, half)
                    for g in range(4 * half, 4 * half + 4):
                        pe.wait_ge(*drained("kTb", b, g))
                    for h in range(H):
                        last = mm(out[HEAD[h], :], q_blocks[:, b, HEAD[h]],
                                  kTb[:, h, 512 * half:512 * half + 512], True, True)
                    last.then_inc(full_sem("Sd", b, half), 1)
                out = claim(pe, (2,), "Sn", b)
                for h in range(H):
                    last = mm(out[HEAD[h], 0:TS], q_blocks[:, b, HEAD[h]], kT[:, h, TP:NT], True, True)
                last.then_inc(full_sem("Sn", b), 1)

            pe.wait_ge(q_blocked, 1)
            turn_keys(0)
            dec_scores(0)
            turn_keys(1)
            for b in range(NB):
                pe.wait_ge(dec_exp, b + 1)
                for half in range(2):
                    out = claim(pe, (6 + half,), "pT", b, half)
                    for i in range(4):
                        g = 4 * half + i
                        last = pe.transpose(out[:, P * i:P * i + P], p_dec[:, P * g:P * g + P], ident)
                    last.then_inc(full_sem("pT", b, half), 1)
                out = claim(pe, (3,), "pTn", b)
                pe.transpose(out[0:TS, 0:P], p_dec[:, PAGES * PAGE:PAGES * PAGE + TS], ident)\
                    .then_inc(full_sem("pTn", b), 1)
                if b + 1 < NB:
                    dec_scores(b + 1)
                pe.wait_ge(*landed(("V", b)))
                vc = unit(("V", b), PAGES)
                for half in range(2):
                    pe.wait_ge(*drained("pT", b, half))
                out = claim(pe, (3,), "od", b)
                for g in range(PAGES):
                    for h in range(H):
                        mm(out[HEAD[h], 0:P], pT_dec[:, g, HEAD[h]], vc[:, g, P * h:P * h + P], g == 0, False)
                for h in range(H):
                    last = mm(out[HEAD[h], 0:P], pTn[0:TS, HEAD[h]], va[0:TS, 2, P * h:P * h + P],
                              False, True)
                last.then_inc(full_sem("od", b), 1)
                last_use[("V", b)] = full("od", b)
                if b + 2 < NB:
                    turn_keys(b + 2)
                pe.wait_ge(*drained("od", b))
                out = claim(pe, (3,), "odT", b)
                pe.transpose(out[:, 0:P], o_rows, ident).then_inc(full_sem("odT", b), 1)
            pe.wait_ge(o_squared, 1)
            for h in range(H):
                out = claim(pe, LOW, "oss", h)
                mm(out[:, 0:NT], ones, o_sq[:, h, :], True, True).then_inc(full_sem("oss", h), 1)

            def feature_major(name, key, pool):
                pe.wait_ge(*landed((name, 0)))
                w = unit((name, 0), 8)
                for m in range(4):
                    out = claim(pe, pool, key, m)
                    for k in range(KT):
                        last = mm(out[:, 0:NT], w[:, k, P * m:P * m + P], hT[:, k, :], k == 0, k == KT - 1)
                    last.then_inc(full_sem(key, m), 1)
                last_use[(name, 0)] = full(key, 3)

            feature_major("qm", "qm", ALLB)
            feature_major("km", "km", ALLB)
            pe.wait_ge(mrows_in, 48)
            for r, key in enumerate(("gi", "gf")):
                out = claim(pe, ALLB, key)
                for k in range(KT):
                    last = mm(out[0:H, 0:NT], w_if[:, k, 4 * r:4 * r + 4], hT[:, k, :], k == 0, k == KT - 1)
                last.then_inc(full_sem(key), 1)
            out = claim(pe, ALLB, "cs")
            for m in range(8):
                pe.transpose(out[:, 24 * m:24 * m + 24], cs_rows[0:24, P * m:P * m + P], ident[0:24, 0:24])
            pe.transpose(out[:, 192:224], n_rows[0:32, :], ident[0:32, 0:32]).then_inc(full_sem("cs"), 1)
            token_major("vm", ALLB)
            feature_major("om", "om", ALLB)
            ada(1)
            ada(2)
            pe.wait_ge(tail_ready, 1)
            for half in range(2):
                out = claim(pe, ALLB, "tail", half)
                for i in range(4):
                    last = pe.transpose(out[0:27, P * i:P * i + P], tail[:, 4 * half + i, :], ident)
                last.then_inc(full_sem("tail", half), 1)
            pe.wait_ge(m_exp, 3)
            out = claim(pe, ALLB, "uw")
            for j, (t0, n) in enumerate(TILES):
                pe.transpose(out[0:n, 8 * j:8 * j + 4], rows_u[0:H, t0:t0 + n], ident[0:H, 0:H])
                last = pe.transpose(out[0:n, 8 * j + 4:8 * j + 8], rows_w[0:H, t0:t0 + n], ident[0:H, 0:H])
            last.then_inc(full_sem("uw"), 1)
            turn_ada(1)
            turn_ada(2)
            pe.wait_ge(conv_ready, 2)
            hsel = const("hsel").rearrange("p (h m) -> p h m", h=H)
            pe.wait_ge(*landed(("C", 0)))
            c0 = unit(("C", 0), 32)
            for j in range(3):
                pe.wait_ge(*drained("vm", j))
            for h in range(H):
                cq, ck = cv[:, h, :], cv[:, 4 + h, :]
                out = claim(pe, ALLB, "bc0", h)
                mm(out[:, 0:NT], hsel[0:H, h, :], rowsR[0:H, 0:NT], True, True).then_inc(full_sem("bc0", h), 1)
                out = claim(pe, ALLB, "bc1", h)
                mm(out[:, 0:384], hsel[0:H, h, :], rowsR[0:H, NT:704], True, True)\
                    .then_inc(full_sem("bc1", h), 1)
                out = claim(pe, ALLB, "st", h)
                mm(out[:, 0:256], ck[:, 0:P], cq[:, 0:TP], True, True)
                mm(out[:, 256:384], ck[:, P:TP], cq[:, P:TP], True, True)
                mm(out[0:TS, 384:448], ck[:, TP:NT], cq[:, TP:NT], True, True).then_inc(full_sem("st", h), 1)
                out = claim(pe, ALLB, "kt", h)
                for j, (t0, n) in enumerate(TILES):
                    last = pe.transpose(out[0:n, P * j:P * j + P], ck[:, t0:t0 + n], ident)
                last.then_inc(full_sem("kt", h), 1)
                pe.wait_ge(kw_ready, h + 1)
                out = claim(pe, ALLB, "C", h)
                for j in range(2):
                    mm(out[:, 0:P], kw[:, j, :], vm[:, j, P * h:P * h + P], j == 0, j == 1)
                for j in range(2):
                    mm(out[:, P:P + 1], kw[:, j, :], ones[:, 0:1], j == 0, j == 1)
                mm(out[:, 130:138], kw[0:TS, 2, :], const("blkind", TS), True, True)\
                    .then_inc(full_sem("C", h), 1)
                for half in range(2):
                    out = claim(pe, ALLB, "Cs", h, half)
                    mm(out[:, :], kw[0:TS, 2, :],
                       v_blk[0:TS, 4 * half:4 * half + 4, :].rearrange("p a b -> p (a b)"),
                       True, True).then_inc(full_sem("Cs", h, half), 1)
                pe.wait_ge(p_ready, h + 1)
                pe.wait_ge(*drained("st", h))
                pe.wait_ge(qe_ready, h + 1)
                out = claim(pe, ALLB, "num", h)
                vh = vm[:, :, P * h:P * h + P]
                mm(out[:, 0:TP], vh[:, 0, :], dT[:, 0:TP], True, False)
                mm(out[:, P:TP], vh[:, 1, :], dT[:, 256:384], False, True)
                mm(out[:, TP:NT], vh[0:TS, 2, :], dT[0:TS, 384:448], False, False)
                for b in range(NB):
                    last = mm(out[:, TP + TD * b:TP + TD * b + TD], c0[:, H * b + h, :],
                              qe[:, 0, TD * b:TD * b + TD], False, True)
                last.then_inc(full_sem("num", h), 1)
                out = claim(pe, ALLB, "den", h)
                mm(out[:, 0:TP], ones, dT[:, 0:TP], True, False)
                mm(out[:, P:TP], ones, dT[:, 256:384], False, True)
                mm(out[:, TP:NT], ones[0:TS, :], dT[0:TS, 384:448], False, False)
                mm(out[:, TP:NT], ones, qe[:, 1, :], False, True).then_inc(full_sem("den", h), 1)
                pe.wait_ge(h_squared, h + 1)
                out = claim(pe, ALLB, "hss", h)
                mm(out[:, 0:NT], ones, hsq, True, True).then_inc(full_sem("hss", h), 1)
            pe.wait_ge(c_ready, H)
            out = claim(pe, ALLB, "n_out")
            pe.transpose(out[0:36, 0:P], nT, ident).then_inc(full_sem("n_out"), 1)

            def up(name, w, src):
                pe.wait_ge(*landed((w, 0)))
                u = unit((w, 0), 4)
                for m in range(KT):
                    out = claim(pe, ALLB, w, m)
                    for k in range(4):
                        last = mm(out[:, 0:NT], u[:, k, P * m:P * m + P], src[:, k, :], k == 0, k == 3)
                    last.then_inc(full_sem(w, m), 1)
                last_use[(w, 0)] = full(w, KT - 1)

            feature_major("ga0", "ga0", ALLB)
            feature_major("ga1", "ga1", ALLB)
            pe.wait_ge(o_ready, 1)
            up("a", "upa", oT)
            feature_major("gb0", "gb0", ALLB)
            feature_major("gb1", "gb1", ALLB)
            pe.wait_ge(hm_ready, 1)
            up("b", "upb", hmT)
            pe.wait_ge(*landed(("wo0", 0)))
            pe.wait_ge(*landed(("wo1", 0)))
            pe.wait_ge(merged, 1)
            for m in range(KT):
                out = claim(pe, ALLB, "wo", m)
                for k in range(KT):
                    w = unit(("wo0" if k < 4 else "wo1", 0), 4)
                    last = mm(out[:, 0:NT], w[:, k % 4, P * m:P * m + P], mT[:, k, :], k == 0, k == KT - 1)
                last.then_inc(full_sem("wo", m), 1)
            last_use[("wo0", 0)] = last_use[("wo1", 0)] = full("wo", KT - 1)

            pe.wait_ge(x1_squared, 1)
            out = claim(pe, ALLB, "ss2")
            for k in range(KT):
                last = mm(out[:, 0:NT], ones, fin_sq[:, k, :], k == 0, k == KT - 1)
            last.then_inc(full_sem("ss2"), 1)
            pe.wait_ge(h2_ready, 1)
            pe.wait_ge(moe_in, 48)
            out = claim(pe, ALLB, "logit")
            for j, (t0, n) in enumerate(TILES):
                for k in range(KT):
                    last = mm(out[0:n, NE * j:NE * j + NE], hT[:, k, t0:t0 + n], w_rt[:, k, :],
                              k == 0, k == KT - 1)
            last.then_inc(full_sem("logit"), 1)
            for j, (t0, n) in enumerate(TILES):
                for half in range(2):
                    out = claim(pe, ALLB, "h2", j, half)
                    for i in range(4):
                        last = pe.transpose(out[0:n, P * i:P * i + P], hT[:, 4 * half + i, t0:t0 + n], ident)
                    last.then_inc(full_sem("h2", j, half), 1)
            pe.wait_ge(routed, 1)
            out = claim(pe, ALLB, "pos")
            for j in range(3):
                for i in range(j + 1):
                    mm(out[:, NE * j:NE * j + NE], const("before") if i == j else ones, mask[:, i, :],
                       i == 0, i == j)
            for i in range(3):
                mm(out[:, 96:128], ones, mask[:, i, :], i == 0, i == 2)
            for i in range(3):
                last = mm(out[0:NE, 128:129], mask[:, i, :], ones[:, 0:1], i == 0, i == 2)
            last.then_inc(full_sem("pos"), 1)
            out = claim(pe, ALLB, "wT")
            for j, (t0, n) in enumerate(TILES):
                last = pe.transpose(out[0:NE, t0:t0 + n], wts[0:n, j, :], ident[0:n, 0:n])
            last.then_inc(full_sem("wT"), 1)
            pe.wait_ge(blocks_ready, 1)
            out = claim(pe, ALLB, "cum")
            upto = const("causal", NE)[:, 0:NE]
            mm(out[0:NE, 0:1], upto, plan[0:NE, 0:1], True, True)
            mm(out[0:1, NE:2 * NE], plan[0:NE, 0:1], upto, True, True).then_inc(full_sem("cum"), 1)
            pe.wait_ge(begun_ready, 1)
            out = claim(pe, ALLB, "list")
            mm(out[0:1, 0:MAX_BLOCKS + 1], ones[0:NE, 0:1], begun[0:NE, :], True, True)
            mm(out[0:1, 64:64 + MAX_BLOCKS + 1], plan[0:NE, 0:1], begun[0:NE, :], True, True)\
                .then_inc(full_sem("list"), 1)
            pe.wait_ge(*drained("wT"))
            for m in range(KT):
                out = claim(pe, ALLB, "bd", m)
                mm(out[:, 0:NT], bd_rows[0:NE, P * m:P * m + P], wT[0:NE, :], True, True)\
                    .then_inc(full_sem("bd", m), 1)

            H0, H1 = slice(0, SLOTS), slice(SLOTS, P)

            def pair(out_bank, lhsT, rhs_at, start, stop):
                for h, rows in enumerate((H0, H1)):
                    last = mm(psum[rows, out_bank, :], lhsT, rhs_at(h), start, stop)
                return last

            def gather(b):
                for j, (t0, m) in enumerate(TILES):
                    last = pair(B_HG, sel[0:m, j, :],
                                lambda h: h2_tok[0:m, j, 512 * h:512 * h + 512], j == 0, j == 2)
                last.then_inc(gathered, 1)

            def turn_gathered():
                for i in range(4):
                    last = pe.transpose(psum[:, B_HG_T, P * i:P * i + P], hg_rows[:, P * i:P * i + P], ident)
                last.then_inc(hg_turned, 1)

            def column_products(bank_, u, halves, lhsT_at, first, last_k, done):
                for k in range(4):
                    last = pair(bank_, lhsT_at(k), lambda h: u[:, k, halves(h)], first and k == 0,
                                last_k and k == 3)
                last.then_inc(done, 1)

            def gate_or_up(b, expert, q, bank_, between):
                pair(bank_, bias_hot[0:3 * NE, :],
                     lambda h: gu_bias[:, FF * q + 512 * h:FF * q + 512 * h + 512], True, False)
                for half in range(2):
                    i = 2 * q + half
                    if half == 1:
                        between()
                    pe.wait_ge(unit_landed[moe_slot[i]], 16 * expert + (landed_base[i] + 16))
                    u = ring[:, moe_slot[i], :].rearrange("p (k f) -> p k f", k=4)
                    column_products(bank_, u, lambda h: slice(512 * h, 512 * h + 512),
                                    lambda k: hgT[:, k, SLOTS * half:SLOTS * half + SLOTS],
                                    False, half == 1, unit_read[i])

            def combine(i):
                for h, rows in enumerate((H0, H1)):
                    last = mm(psum[:, B_SUM[i % 2] + h, 0:NT], y_rows[rows, P * i:P * i + P],
                              selwT[rows, :], True, True)
                last.then_inc(combined, 1)

            def expert_block(b, expert, first):
                if not first:
                    pe.wait_ge(gate_clamped, b)
                pe.wait_ge(bias_hot_ready, b + 1)
                pe.wait_ge(hgT_copied, b + 1)
                gate_or_up(b, expert, 0, B_GATE, lambda: None)
                if not first:
                    pe.wait_ge(y_copied, b)
                    pe.wait_ge(selwT_copied, b)
                    pe.wait_ge(hgT_copied, b + 1)
                    combine(0)
                    pe.wait_ge(actT_copied, b)
                    combine(1)
                    pe.wait_ge(up_clamped, b)

                def rest():
                    if not first:
                        pe.wait_ge(added, 4 * b - 3)
                        combine(2)
                        pe.wait_ge(added, 4 * b - 2)
                        combine(3)
                gate_or_up(b, expert, 1, B_UP, rest)
                pe.wait_ge(sel_ready, b + 2)
                pe.wait_ge(hg_copied, b + 1)
                gather(b + 1)
                if not first:
                    pe.wait_ge(added, 4 * b)
                pe.wait_ge(act_ready, b + 1)
                for i in range(4):
                    last = pe.transpose(psum[:, B_ACT_T, P * i:P * i + P], act_u[:, P * i:P * i + P], ident)
                last.then_inc(act_turned, 1)
                pe.wait_ge(hg_copied, b + 2)
                turn_gathered()
                pe.wait_ge(selw_ready, b + 1)
                for j, (t0, m) in enumerate(TILES):
                    last = pe.transpose(psum[:, B_SEL_T, t0:t0 + m], selw[0:m, j, :], ident[0:m, 0:m])
                last.then_inc(selw_turned, 1)
                pe.wait_ge(actT_copied, b + 1)
                if not first:
                    pe.wait_ge(y_copied, b)
                for half in range(2):
                    i = 4 + half
                    pe.wait_ge(unit_landed[moe_slot[i]], 16 * expert + (landed_base[i] + 16))
                    u = ring[:, moe_slot[i], :].rearrange("p (k f) -> p k f", k=4)
                    column_products(B_Y, u, lambda h: slice(512 * h, 512 * h + 512),
                                    lambda k: actT[:, k, SLOTS * half:SLOTS * half + SLOTS],
                                    half == 0, half == 1, unit_read[i])

            pe.wait_ge(tables, 1)
            pe.wait_ge(sel_ready, 1)
            gather(0)
            pe.wait_ge(hg_copied, 1)
            turn_gathered()
            expert_block(0, 0, True)
            later = pe.value_load(ints[0:1, AT_LATER:AT_LATER + 1], min_val=NE - 1, max_val=MAX_BLOCKS - 1)
            with pe.Fori(0, later) as p:
                b = p + 1
                expert = pe.value_load(ints[0:1, bass.ds(b + AT_EXPERT, 1)], min_val=0, max_val=NE - 1)
                expert_block(b, expert, False)
            blocks = later + 1
            pe.wait_ge(y_copied, blocks)
            pe.wait_ge(selwT_copied, blocks)
            pe.wait_ge(hgT_copied, blocks + 1)
            pe.wait_ge(actT_copied, blocks)
            for i in range(4):
                if i >= 2:
                    pe.wait_ge(added, 4 * blocks + (i - 5))
                combine(i)
            pe.wait_ge(acc_final, 1)

            pe.wait_ge(x2_squared, 1)
            out = claim(pe, ALLB, "ss3")
            for k in range(KT):
                last = mm(out[:, 0:NT], ones, fin_sq[:, k, :], k == 0, k == KT - 1)
            last.then_inc(full_sem("ss3"), 1)
            pe.wait_ge(x2_ready, 1)
            for j, (t0, n) in enumerate(TILES):
                for half in range(2):
                    out = claim(pe, ALLB, "y", j, half)
                    for i in range(4):
                        last = pe.transpose(out[0:n, P * i:P * i + P], xT[:, 4 * half + i, t0:t0 + n], ident)
                    last.then_inc(full_sem("y", j, half), 1)

        own_count = {}

        def own(s):
            own_count[s.name] = own_count.get(s.name, 0) + 1
            return s, own_count[s.name]

        def over(ap, axis, n):
            v = ap.unsqueeze(axis)
            shape = list(v.shape)
            shape[axis] = n
            return v.to_broadcast(shape)

        @block.vector
        def _(dve):
            steps = [0, dve_step]

            def step(ins):
                steps[0] += 1
                ins.then_inc(steps[1], 1)
                dve.wait_ge(steps[1], steps[0])

            iota, valid = const("iota"), const("valid")
            step(dve.memset(M0[:, 0:1], 0.0))

            norms = [0]

            def mean_square(out, src, n, *key):
                dve.tensor_scalar(out, src, 1.0 / n, EPS, ALU.mult, ALU.add).then_inc(free_sem(*key), 1)
                dve.wait_ge(*drained(*key))

            def rsqrt(t):
                norms[0] += 1
                dve.reciprocal(t, t).then_inc(mean_inverse, 1)
                dve.wait_ge(mean_root, norms[0])

            dve.wait_ge(c_sig_done, 1)
            dve.tensor_tensor(c_rows[0:9, :], c_rows[0:9, :], c_sig[0:9, :], ALU.mult).then_inc(c_silu, 1)
            dve.wait_ge(*own(c_silu))
            dve.wait_ge(*full("vec"))
            dve.tensor_copy(vecT[:, 0:117], bank("vec")[:, 0:117]).then_inc(free_sem("vec"), 1)
            dve.wait_ge(*drained("vec"))
            dve.wait_ge(*full("cT"))
            step(dve.memset(cT[:], 0.0))
            dve.tensor_copy(cT[:, :, 0:9], bank("cT")[:, 0:72].rearrange("p (k r) -> p k r", k=KT))\
                .then_inc(free_sem("cT"), 1)
            dve.wait_ge(*drained("cT"))
            dve.wait_ge(table_in, 16 * 7)
            for i in range(2):
                step(dve.tensor_tensor(lam_rows[:, 2 * i, :], lam_rows[:, 2 * i, :],
                                       lam_rows[:, 2 * i + 1, :], ALU.mult))
                step(dve.tensor_reduce(LAM[:, i:i + 1], lam_rows[:, 2 * i, :], AX, ALU.add))
            dve.tensor_copy(LAM[:, 0:2], LAM[:, 0:2]).then_inc(lam_dot, 1)
            dve.wait_ge(*own(lam_dot))
            dve.wait_ge(lam_exp, 1)
            step(dve.tensor_tensor(NLAM, LAM[:, 3:4], LAM[:, 2:3], ALU.subtract))
            step(dve.tensor_scalar(NLAM, NLAM, -LAM_INIT, None, ALU.add))
            comp = const("comp")
            step(dve.scalar_tensor_tensor(COEF, comp[:, 1:2], NLAM, comp[:, 0:1], ALU.mult, ALU.add))
            step(dve.tensor_scalar(GS, vecT[:, V_GS:V_GS + 1], 1.0 - LAM_INIT, None, ALU.mult))

            for j in range(3):
                for half in range(2):
                    dve.wait_ge(*drained("xT", j, half))
            dve.tensor_tensor(x_sq, xT[:], xT[:], ALU.mult).then_inc(x_squared, 1)
            dve.wait_ge(*own(x_squared))
            dve.wait_ge(*full("ss1"))
            mean_square(rstd[:], bank("ss1")[:, 0:NT], D, "ss1")
            rsqrt(rstd[:])
            step(dve.tensor_tensor(hT[:], xT[:], over(rstd[:], 1, KT), ALU.mult))

            def copy_ada(g):
                dve.wait_ge(*full("ada", g))
                if g == 2:
                    dve.wait_ge(*full("adaT", 0))
                dve.tensor_copy(ada_rows[:, g % 2, :], bank("ada", g)).then_inc(free_sem("ada", g), 1)
                dve.wait_ge(*drained("ada", g))

            def ada_bias(g):
                dve.wait_ge(*full("adaT", g))
                turned = bank("adaT", g).rearrange("p (m r) -> p m r", m=16)[:, :, 0:9]
                dve.tensor_tensor(modT[:, 16 * g:16 * g + 16, :], turned,
                                  over(vecT[:, V_ADA + 16 * g:V_ADA + 16 * g + 16], 2, 9), ALU.add)\
                    .then_inc(free_sem("adaT", g), 1)
                dve.wait_ge(*drained("adaT", g))

            def modulate(which, g_col, shift_m, scale_m, done):
                gain, shift = gainT[:, which], modT[:, shift_m:shift_m + KT, :]
                step(dve.scalar_tensor_tensor(gain, modT[:, scale_m:scale_m + KT, :], 1.0,
                                              over(vecT[:, g_col:g_col + KT], 2, 9), ALU.add, ALU.mult))
                samples = hT[:, :, TP:NT].rearrange("p k (b t) -> p k b t", b=NB)
                for k in range(KT):
                    dve.tensor_scalar(hT[:, k, 0:TP], hT[:, k, 0:TP], gain[:, k, 0:1], shift[:, k, 0:1],
                                      ALU.mult, ALU.add)
                step(dve.tensor_tensor(samples, samples, over(gain[:, :, 1:9], 3, TD), ALU.mult))
                dve.tensor_tensor(samples, samples, over(shift[:, :, 1:9], 3, TD), ALU.add)\
                    .then_inc(done, 1)
                dve.wait_ge(*own(done))

            copy_ada(0)
            ada_bias(0)
            modulate(0, V_G1, 0, 8, h_ready)

            cos = const("cos").rearrange("p (j c) -> p j c", j=3)
            sin = const("sin").rearrange("p (j c) -> p j c", j=3)
            flat = pairs.rearrange("p a b -> p (a b)")
            for w in "qk":
                for j, (t0, n) in enumerate(TILES):
                    dve.wait_ge(*full(w, j))
                    z = bank(w, j)[0:n, :].rearrange("p (g s c) -> p g s c", g=8, s=2)
                    tc_ = flat[0:n, 0:512].rearrange("p (g s c) -> p g s c", g=8, s=2)
                    ts_ = flat[0:n, 512:1024].rearrange("p (g s c) -> p g s c", g=8, s=2)
                    cj = over(over(cos[0:n, j, :], 1, 2), 1, 8)
                    sj = over(over(sin[0:n, j, :], 1, 2), 1, 8)
                    dve.tensor_tensor(tc_, z, cj, ALU.mult)
                    dve.tensor_tensor(ts_, z, sj, ALU.mult).then_inc(free_sem(w, j), 1)
                    dve.wait_ge(*drained(w, j))
                    if w == "q" and j == 2:
                        dve.wait_ge(*full("qT", 0))
                    dst = (q_rot[0:n, j % 2, :] if w == "q" else k_rot[0:n, j, :])\
                        .rearrange("p (g s c) -> p g s c", g=8, s=2)
                    dve.tensor_tensor(dst[:, :, 0, :], tc_[:, :, 0, :], ts_[:, :, 1, :], ALU.subtract)
                    dve.tensor_tensor(dst[:, :, 1, :], tc_[:, :, 1, :], ts_[:, :, 0, :], ALU.add)\
                        .then_inc(rotated, 1)
                    dve.wait_ge(*own(rotated))
            step(dve.memset(q_blocks, 0.0))
            dve.wait_ge(*drained("qT", 2))
            qb_v = q_blocks.rearrange("p b (h c) -> p b h c", h=H)
            for h in range(H):
                for c in range(2):
                    rows = slice(DK * c, DK * c + DK)
                    last = dve.tensor_copy(qb_v[rows, :, h, 8 * c:8 * c + 8],
                                           qT[rows, h, TP:NT].rearrange("p (b t) -> p b t", b=NB))
            last.then_inc(q_blocked, 1)
            dve.wait_ge(*own(q_blocked))

            items = [(h, qb) for h in range(H) for qb in range(2)]
            am = const("attmask")

            def att_mask_max(i):
                h, qb = items[i]
                n = P * (qb + 1)
                if i >= 2:
                    dve.wait_ge(*full("aT", i - 2))
                for c in range(2):
                    dve.wait_ge(*full("S", i, c))
                    dve.tensor_tensor(s_pair[:, i % 2, c, 0:n], bank("S", i, c)[:, 0:n], am[:, 256 - n:256],
                                      ALU.add).then_inc(free_sem("S", i, c), 1)
                    dve.wait_ge(*drained("S", i, c))
                mx = MX[:, 2 * (i % 2):2 * (i % 2) + 2]
                step(dve.tensor_reduce(mx, s_pair[:, i % 2, :, 0:n], AX, ALU.max))
                dve.tensor_scalar(mx, mx, -DK ** -0.5, None, ALU.mult).then_inc(att_max, 1)
                dve.wait_ge(*own(att_max))

            att_mask_max(0)
            for i, (h, qb) in enumerate(items):
                if i + 1 < len(items):
                    att_mask_max(i + 1)
                n = P * (qb + 1)
                dve.wait_ge(att_exp, 2 * i + 2)
                rc = RC[:, 2 * (i % 2):2 * (i % 2) + 2]
                step(dve.reciprocal(rc, LS[:, 2 * (i % 2):2 * (i % 2) + 2]))
                step(dve.tensor_tensor(rc[:, 1:2], rc[:, 1:2], NLAM, ALU.mult))
                step(dve.tensor_scalar(s_pair[:, i % 2, 0, 0:n], s_pair[:, i % 2, 0, 0:n], rc[:, 0:1], None,
                                       ALU.mult))
                dve.scalar_tensor_tensor(s_pair[:, i % 2, 0, 0:n], s_pair[:, i % 2, 1, 0:n], rc[:, 1:2],
                                         s_pair[:, i % 2, 0, 0:n], ALU.mult, ALU.add).then_inc(att_a, 1)
                dve.wait_ge(*own(att_a))

            nm = const("newmask").rearrange("p (b k) -> p b k", b=NB)
            last_key = PAGES * PAGE

            def key_pages(b):
                if b:
                    dve.wait_ge(*full("Sn", b - 1))
                for g in range(1, PAGES, 2):
                    dve.wait_ge(*full("kTb", b, g))
                    dve.tensor_copy(kTb[:, :, PAGE * g:PAGE * g + PAGE],
                                    bank("kTb", b, g).rearrange("p (h k) -> p h k", h=H))\
                        .then_inc(free_sem("kTb", b, g), 1)
                    dve.wait_ge(*drained("kTb", b, g))

            def dec_row_max(b):
                dve.wait_ge(*full("Sn", b))
                step(dve.tensor_reduce(SC[:, 0:1], psum[:, 4:6, :], mybir.AxisListType.XY, ALU.max))
                dve.tensor_tensor(s_new, bank("Sn", b)[:, 0:TS], nm[:, b, :], ALU.add)\
                    .then_inc(free_sem("Sn", b), 1)
                dve.wait_ge(*drained("Sn", b))
                step(dve.tensor_reduce(SC[:, 1:2], s_new, AX, ALU.max))
                step(dve.tensor_tensor(SC[:, 0:1], SC[:, 0:1], SC[:, 1:2], ALU.max))
                dve.tensor_scalar(SC[:, 2:3], SC[:, 0:1], -DK ** -0.5, None, ALU.mult).then_inc(dec_max, 1)
                dve.wait_ge(*own(dec_max))

            key_pages(0)
            dec_row_max(0)
            key_pages(1)
            for b in range(NB):
                dve.wait_ge(dec_exp, b + 1)
                step(dve.tensor_reduce(SC[:, 6:7], SC[:, 3:6], AX, ALU.add))
                step(dve.reciprocal(SC[:, 6:7], SC[:, 6:7]))
                step(dve.tensor_tensor(SC[:, 6:7], SC[:, 6:7], COEF, ALU.mult))
                if b:
                    dve.wait_ge(*full("od", b - 1))
                dve.wait_ge(*full("pT", b, 0))
                dve.tensor_copy(pT_dec[:, 0:4, :], bank("pT", b, 0).rearrange("p (g c) -> p g c", g=4))\
                    .then_inc(free_sem("pT", b, 0), 1)
                dve.wait_ge(*drained("pT", b, 0))
                if b + 1 < NB:
                    dec_row_max(b + 1)
                dve.wait_ge(*full("od", b))
                if b:
                    dve.wait_ge(*full("odT", b - 1))
                dve.tensor_scalar(o_rows, bank("od", b)[:, 0:P], SC[:, 6:7], None, ALU.mult)\
                    .then_inc(free_sem("od", b), 1)
                dve.wait_ge(*drained("od", b))
                if b + 2 < NB:
                    key_pages(b + 2)
                dve.wait_ge(*full("odT", b))
                turned = bank("odT", b)[:, 0:P].rearrange("p (h z) -> p h z", h=H)[:, :, 0:2 * TD]
                dve.tensor_reduce(oT[:, :, TP + TD * b:TP + TD * b + TD],
                                  turned.rearrange("p h (c q) -> p h q c", c=2), AX, ALU.add)\
                    .then_inc(free_sem("odT", b), 1)
                dve.wait_ge(*drained("odT", b))
            dve.wait_ge(*drained("PV", len(items) - 1))
            dve.wait_ge(k_stored, 96)
            dve.tensor_tensor(o_sq, oT[:], oT[:], ALU.mult).then_inc(o_squared, 1)
            dve.wait_ge(*own(o_squared))
            for h in range(H):
                dve.wait_ge(*full("oss", h))
                mean_square(o_rms[:, h, :], bank("oss", h)[:, 0:NT], P, "oss", h)
            rsqrt(o_rms)
            dve.scalar_tensor_tensor(oT[:], oT[:], GS, o_rms, ALU.mult, ALU.mult).then_inc(o_ready, 1)
            dve.wait_ge(*own(o_ready))
            step(dve.memset(raw_p[:, :, 0:3], 0.0))
            dve.memset(nT, 0.0).then_inc(region_m, 1)
            dve.wait_ge(*own(region_m))

            dve.wait_ge(mrows_in, 48)
            dve.wait_ge(*full("gi"))
            dve.tensor_scalar(rows_li[0:H, :], bank("gi")[0:H, 0:NT], BG[:, 0:1], None, ALU.add)\
                .then_inc(free_sem("gi"), 1)
            dve.wait_ge(*drained("gi"))
            dve.wait_ge(*full("gf"))
            dve.tensor_scalar(rows_f[0:H, :], bank("gf")[0:H, 0:NT], BG[:, 1:2], None, ALU.add)\
                .then_inc(free_sem("gf"), 1)
            dve.wait_ge(*drained("gf"))
            dve.wait_ge(*drained("gi"))
            dve.wait_ge(*drained("gf"))
            dve.scalar_tensor_tensor(rows_t[0:H, :], rows_f[0:H, :], -1.0, rows_f[0:H, :], ALU.mult,
                                     ALU.max).then_inc(f_abs, 1)
            dve.wait_ge(*own(f_abs))
            dve.wait_ge(*full("cs"))
            step(dve.tensor_copy(n0T, bank("cs")[:, 192:224]))
            dve.tensor_copy(raw_s[:, :, :, 0:3],
                            bank("cs")[:, 0:192].rearrange("p (m b j) -> p m b j", m=8, b=NB))\
                .then_inc(free_sem("cs"), 1)
            dve.wait_ge(*drained("cs"))

            def conv(m0):
                for m in range(m0, m0 + 4):
                    dve.wait_ge(*drained("qm" if m < 4 else "km", m % 4))
                    cp, cs_ = cv[:, m, 0:TP], cv[:, m, TP:NT].rearrange("p (b t) -> p b t", b=NB)
                    for tap in range(4):
                        w = vecT[:, V_WC + 8 * tap + m:V_WC + 8 * tap + m + 1]
                        sp_, ss_ = raw_p[:, m, tap:tap + TP], raw_s[:, m, :, tap:tap + TD]
                        if tap == 0:
                            bias = vecT[:, V_BC + m:V_BC + m + 1]
                            dve.tensor_scalar(cp, sp_, w, bias, ALU.mult, ALU.add)
                            step(dve.tensor_scalar(cs_, ss_, w, bias, ALU.mult, ALU.add))
                        else:
                            dve.scalar_tensor_tensor(cp, sp_, w, cp, ALU.mult, ALU.add)
                            last = dve.scalar_tensor_tensor(cs_, ss_, w, cs_, ALU.mult, ALU.add)
                            if m < m0 + 3 or tap < 3:
                                step(last)
                last.then_inc(conv_done, 1)
                dve.wait_ge(*own(conv_done))

            conv(0)
            dve.wait_ge(f_ln, 1)
            F, u, M_, up = rows_f[0:H, :], rows_u[0:H, :], rows_w[0:H, :], rows_t[0:H, :]
            step(dve.scalar_tensor_tensor(up, F, 0.0, up, ALU.min, ALU.subtract))
            step(dve.tensor_tensor_scan(F, const("carry", H), up, 0.0, ALU.mult, ALU.add))
            step(dve.tensor_tensor(u, rows_li[0:H, :], F, ALU.subtract))
            step(dve.tensor_copy(up, u))
            step(dve.tensor_tensor(up[:, 0:1], up[:, 0:1], M0[:, 0:1], ALU.max))
            step(dve.tensor_tensor(up[:, TP:NT:TD], up[:, TP:NT:TD], M0[:, 1:9], ALU.max))
            step(dve.tensor_tensor_scan(M_, const("drop", H), up, 0.0, ALU.add, ALU.max))
            negM = rowsR[0:H, 0:NT]
            step(dve.tensor_tensor(up, F, M_, ALU.add))
            step(dve.tensor_scalar(negM, M_, -1.0, None, ALU.mult))
            nms = negM[:, TP:NT].rearrange("p (b t) -> p b t", b=NB)
            step(dve.tensor_tensor(rowsR[0:H, 2 * NT:2 * NT + TS].rearrange("p (b t) -> p b t", b=NB), nms,
                                   over(M0[:, 1:9], 2, TD), ALU.add))
            step(dve.tensor_scalar(rows_w[0:H, 0:TP], u[:, 0:TP], negM[:, TP - 1:TP], None, ALU.add))
            dve.tensor_tensor(rows_w[0:H, TP:NT].rearrange("p (b t) -> p b t", b=NB),
                              u[:, TP:NT].rearrange("p (b t) -> p b t", b=NB),
                              over(nms[:, :, TD - 1], 2, TD), ALU.add).then_inc(m_rows, 1)
            dve.wait_ge(*own(m_rows))
            conv(4)
            dve.wait_ge(conv_sig, 1)
            dve.tensor_tensor(cv[:, 0:4, :], cv[:, 0:4, :], cv_sig, ALU.mult).then_inc(conv_ready, 1)
            dve.wait_ge(*own(conv_ready))
            step(dve.tensor_copy(tail[:, :, 0:3], raw_p[:, :, TP:TP + 3]))
            dve.tensor_copy(tail[:, :, 3:27].rearrange("p m (b j) -> p m b j", b=NB),
                            raw_s[:, :, :, 8:11]).then_inc(tail_ready, 1)
            dve.wait_ge(*own(tail_ready))
            dve.wait_ge(conv_sig, 2)
            dve.scalar_tensor_tensor(cv[:, 4:8, :], cv[:, 4:8, :], P ** -0.5, cv_sig, ALU.mult, ALU.mult)\
                .then_inc(conv_ready, 1)
            dve.wait_ge(*own(conv_ready))
            copy_ada(1)
            copy_ada(2)
            dve.wait_ge(*full("uw"))
            step(dve.tensor_copy(uw[:, 0:2, :], bank("uw")[:, 0:16].rearrange("p (j c) -> p j c", j=2)))
            dve.tensor_copy(uw[0:TS, 2, :], bank("uw")[0:TS, 16:24]).then_inc(free_sem("uw"), 1)
            dve.wait_ge(*drained("uw"))
            ada_bias(1)
            ada_bias(2)
            dve.wait_ge(conv_ready, 2)
            for j in range(3):
                dve.wait_ge(*drained("vm", j))
            for m in range(4):
                dve.wait_ge(*drained("om", m))
            causal = const("causal")
            blkind = const("blkind", TS)
            dve.wait_ge(*landed(("C", 0)))
            c0 = unit(("C", 0), 32)
            for h in range(H):
                dve.wait_ge(*full("bc0", h))
                if h:
                    dve.wait_ge(*full("hss", h - 1))
                bc = bank("bc0", h)
                dve.tensor_scalar(dT[:, 0:256], bc[:, 0:256], uw[:, 0, h:h + 1], 0.0, ALU.add, ALU.min)
                dve.tensor_scalar(dT[:, 256:384], bc[:, P:TP], uw[:, 1, h:h + 1], 0.0, ALU.add, ALU.min)
                dve.tensor_scalar(dT[0:TS, 384:448], bc[0:TS, TP:NT], uw[0:TS, 2, h:h + 1], 0.0, ALU.add,
                                  ALU.min).then_inc(free_sem("bc0", h), 1)
                dve.wait_ge(*drained("bc0", h))
                dve.wait_ge(*full("kt", h))
                for j, (t0, n) in enumerate(TILES):
                    last = dve.tensor_scalar(kw[0:n, j, :], bank("kt", h)[0:n, P * j:P * j + P],
                                             uw[0:n, j, 4 + h:5 + h], None, ALU.mult)
                last.then_inc(free_sem("kt", h), 1)
                dve.wait_ge(*drained("kt", h))
                dve.tensor_tensor(v_blk[0:TS], over(vm[0:TS, 2, P * h:P * h + P], 1, NB),
                                  over(blkind, 2, P), ALU.mult).then_inc(kw_ready, 1)
                dve.wait_ge(*own(kw_ready))
                dve.wait_ge(*drained("bc1", h))
                ei = bcS[:, NT:NT + TS]
                step(dve.tensor_tensor(qe[:, 0, :], cv[:, h, TP:NT], ei, ALU.mult))
                n0 = n0T.rearrange("p (b h) -> p b h", b=NB)[:, :, h]
                dve.tensor_tensor(qe[:, 1, :].rearrange("p (b t) -> p b t", b=NB),
                                  qe[:, 0, :].rearrange("p (b t) -> p b t", b=NB),
                                  over(n0, 2, TD), ALU.mult).then_inc(qe_ready, 1)
                dve.wait_ge(*own(qe_ready))
                dve.wait_ge(d_exp, h + 1)
                step(dve.tensor_tensor(dT[:, 0:384], dT[:, 0:384], causal[:, 0:384], ALU.mult))
                step(dve.tensor_tensor(dT[0:TS, 384:448], dT[0:TS, 384:448], causal[0:TS, 384:448],
                                       ALU.mult))
                dve.wait_ge(*full("st", h))
                dve.tensor_tensor(dT[:, 0:384], dT[:, 0:384], bank("st", h)[:, 0:384], ALU.mult)\
                    .then_inc(p_ready, 1)
                dve.wait_ge(*own(p_ready))
                dve.tensor_tensor(dT[0:TS, 384:448], dT[0:TS, 384:448], bank("st", h)[0:TS, 384:448],
                                  ALU.mult).then_inc(free_sem("st", h), 1)
                dve.wait_ge(*drained("st", h))
                dve.wait_ge(*full("C", h))
                dec = ei.rearrange("p (b t) -> p b t", b=NB)[:, :, TD - 1]
                step(dve.tensor_copy(C_p[:, h, :], bank("C", h)[:, 0:P]))
                step(dve.tensor_copy(nT[:, h:h + 1], bank("C", h)[:, P:P + 1]))
                nTs = nT[:, 4:36].rearrange("p (b h) -> p b h", b=NB)[:, :, h]
                step(dve.tensor_tensor(nTs, n0, dec, ALU.mult))
                dve.tensor_tensor(nTs, nTs, bank("C", h)[:, 130:138], ALU.add).then_inc(free_sem("C", h), 1)
                dve.wait_ge(*drained("C", h))
                dve.wait_ge(*full("num", h))
                dve.wait_ge(*full("den", h))
                step(dve.tensor_tensor(den_s, bank("den", h)[:, 0:NT], bcS[:, 0:NT], ALU.max))
                dve.scalar_tensor_tensor(den_s, bank("den", h)[:, 0:NT], -1.0, den_s, ALU.mult,
                                         ALU.max).then_inc(free_sem("den", h), 1)
                dve.wait_ge(*drained("den", h))
                step(dve.reciprocal(den_s, den_s))
                dve.tensor_tensor(hr[:, h, :], bank("num", h)[:, 0:NT], den_s, ALU.mult)\
                    .then_inc(free_sem("num", h), 1)
                dve.wait_ge(*drained("num", h))
                dve.tensor_tensor(hsq, hr[:, h, :], hr[:, h, :], ALU.mult).then_inc(h_squared, 1)
                dve.wait_ge(*own(h_squared))
                ch = c0.rearrange("p (b h) e -> p b h e", b=NB)[:, :, h, :]
                step(dve.tensor_tensor(ch, ch, over(dec, 2, P), ALU.mult))
                for half in range(2):
                    dve.wait_ge(*full("Cs", h, half))
                    dve.tensor_tensor(ch[:, 4 * half:4 * half + 4, :], ch[:, 4 * half:4 * half + 4, :],
                                      bank("Cs", h, half).rearrange("p (b e) -> p b e", b=4), ALU.add)\
                        .then_inc(free_sem("Cs", h, half), 1)
                    dve.wait_ge(*drained("Cs", h, half))
                dve.wait_ge(*drained("C", h))
                step(dve.tensor_copy(SC[:, 7:8], den_s[:, 0:1]))
                dve.tensor_copy(SC[:, 7:8], den_s[:, 0:1]).then_inc(c_ready, 1)
                dve.wait_ge(*own(c_ready))
                dve.wait_ge(*full("hss", h))
                mean_square(hmT[:, h, :], bank("hss", h)[:, 0:NT], P, "hss", h)
            rsqrt(hmT[:])
            for h in range(H):
                dve.scalar_tensor_tensor(hr[:, h, :], hr[:, h, :], vecT[:, V_GM + h:V_GM + h + 1],
                                         hmT[:, h, :], ALU.mult, ALU.mult).then_inc(dve_step, 1)
                steps[0] += 1
            dve.wait_ge(dve_step, steps[0])
            dve.tensor_tensor(hmT[:], hr, so, ALU.mult).then_inc(hm_ready, 1)
            dve.wait_ge(*own(hm_ready))

            for m in range(KT):
                dve.wait_ge(*full("upa", m))
                dve.wait_ge(*drained("ga0" if m < 4 else "ga1", m % 4))
                dve.tensor_tensor(mT[:, m, :], bank("upa", m)[:, 0:NT], sg[:, m, :], ALU.mult)\
                    .then_inc(free_sem("upa", m), 1)
                dve.wait_ge(*drained("upa", m))
            for m in range(KT):
                dve.wait_ge(*full("upb", m))
                dve.wait_ge(*drained("gb0" if m < 4 else "gb1", m % 4))
                dve.tensor_tensor(sg[:, m, :], bank("upb", m)[:, 0:NT], sg[:, m, :], ALU.mult)\
                    .then_inc(free_sem("upb", m), 1)
                dve.wait_ge(*drained("upb", m))
            dve.wait_ge(*drained("upa", KT - 1))
            for m in range(KT):
                dve.wait_ge(*drained("upb", m))
            dve.tensor_tensor(mT, mT, sg, ALU.add).then_inc(merged, 1)
            dve.wait_ge(*own(merged))

            def gated_add(m, src, gate_m, *key):
                gate = modT[:, gate_m + m, :]
                samples = rstd[:, 0:TS].rearrange("p (b t) -> p b t", b=NB)
                step(dve.tensor_tensor(samples, src[:, TP:NT].rearrange("p (b t) -> p b t", b=NB),
                                       over(gate[:, 1:9], 2, TD), ALU.mult))
                dve.tensor_tensor(xT[:, m, TP:NT], xT[:, m, TP:NT], rstd[:, 0:TS], ALU.add)
                last = dve.scalar_tensor_tensor(xT[:, m, 0:TP], src[:, 0:TP], gate[:, 0:1], xT[:, m, 0:TP],
                                                ALU.mult, ALU.add)
                if key:
                    last.then_inc(free_sem(*key), 1)
                    dve.wait_ge(*drained(*key))
                else:
                    step(last)

            dve.wait_ge(bias_in, 48)
            for m in range(KT):
                dve.wait_ge(*drained("upa", m))
            for rows in (3 * NE, 2 * NE, NE):
                step(dve.tensor_copy(gu_bias[0:rows, :], bias_f32[0:rows, :]))
                if rows > NE:
                    rest = bias_f32[0:rows - NE, :]
                    step(dve.tensor_tensor(rest, rest, gu_bias[0:rows - NE, :], ALU.subtract))

            for m in range(KT):
                dve.wait_ge(*full("wo", m))
                gated_add(m, bank("wo", m), 16, "wo", m)

            dve.tensor_tensor(fin_sq, xT[:], xT[:], ALU.mult).then_inc(x1_squared, 1)
            dve.wait_ge(*own(x1_squared))
            dve.wait_ge(*full("ss2"))
            mean_square(rstd[:], bank("ss2")[:, 0:NT], D, "ss2")
            rsqrt(rstd[:])
            step(dve.tensor_tensor(hT[:], xT[:], over(rstd[:], 1, KT), ALU.mult))
            modulate(1, V_G2, 24, 32, h2_ready)

            step(dve.memset(logits, 0.0))
            dve.wait_ge(moe_in, 48)
            dve.wait_ge(*full("logit"))
            lg = bank("logit")[:, 0:96].rearrange("p (j e) -> p j e", j=3)
            step(dve.tensor_tensor(logits[:, 0:2, :], lg[:, 0:2, :], over(b_rt, 1, 2), ALU.add))
            dve.tensor_tensor(logits[0:TS, 2, :], lg[0:TS, 2, :], b_rt[0:TS, :], ALU.add)\
                .then_inc(free_sem("logit"), 1)
            dve.wait_ge(*drained("logit"))
            for j in range(3):
                step(dve.max(top8[:, j, :], logits[:, j, :]))
                step(dve.max_index(top_ix[:, j, :], top8[:, j, :], logits[:, j, :]))
            step(dve.tensor_copy(idxf, top_ix[:]))
            dve.tensor_tensor(ew, top8[:, :, 0:4], top8[:, :, 0:1].to_broadcast([P, 3, 4]), ALU.subtract)\
                .then_inc(top_diff, 1)
            dve.wait_ge(*own(top_diff))
            dve.wait_ge(top_exp, 1)
            step(dve.tensor_reduce(esum, ew, AX, ALU.add))
            step(dve.reciprocal(esum, esum))
            step(dve.tensor_tensor(esum, esum, valid, ALU.mult))
            step(dve.tensor_tensor(ew, ew, over(esum, 2, 4), ALU.mult))
            iota_e = over(iota[:, 0:NE], 1, 3)
            for s in range(TOPK):
                step(dve.tensor_tensor(eq, iota_e, idxf[:, :, s:s + 1].to_broadcast([P, 3, NE]),
                                       ALU.is_equal))
                if s == 0:
                    step(dve.tensor_copy(mask, eq))
                    step(dve.tensor_tensor(wts, eq, ew[:, :, s:s + 1].to_broadcast([P, 3, NE]), ALU.mult))
                else:
                    step(dve.tensor_tensor(mask, mask, eq, ALU.add))
                    step(dve.tensor_tensor(eqw, eq, ew[:, :, s:s + 1].to_broadcast([P, 3, NE]), ALU.mult))
                    step(dve.tensor_tensor(wts, wts, eqw, ALU.add))
            dve.tensor_tensor(mask, mask, over(valid, 2, NE), ALU.mult).then_inc(routed, 1)
            dve.wait_ge(*own(routed))
            dve.wait_ge(*full("pos"))
            pp = bank("pos")
            step(dve.scalar_tensor_tensor(eq, pp[:, 0:96].rearrange("p (j e) -> p j e", j=3), 1.0, mask,
                                          ALU.add, ALU.mult))
            for r in range(ROUNDS):
                step(dve.tensor_scalar(pos[:, :, NE * r:NE * r + NE], eq, -1.0 - SLOTS * r, None, ALU.add))
                step(dve.tensor_copy(wts3[:, :, NE * r:NE * r + NE], wts))
            dve.tensor_tensor(plan[0:NE, 2:1 + ROUNDS], pp[0:NE, 128:129].to_broadcast([NE, ROUNDS - 1]),
                              const("rounds", NE), ALU.is_gt).then_inc(free_sem("pos"), 1)
            dve.wait_ge(*drained("pos"))
            step(dve.tensor_reduce(plan[0:NE, 1:2], plan[0:NE, 2:1 + ROUNDS], AX, ALU.add))
            dve.tensor_scalar(plan[0:NE, 0:1], plan[0:NE, 1:2], 1.0, None, ALU.add).then_inc(blocks_ready, 1)
            dve.wait_ge(*own(blocks_ready))
            dve.wait_ge(*full("cum"))
            step(dve.tensor_copy(plan[0:NE, 1:2], bank("cum")[0:NE, 0:1]))
            step(dve.tensor_scalar(ints[0:1, AT_LATER:AT_LATER + 1], bank("cum")[0:1, 2 * NE - 1:2 * NE], -1.0,
                                   None, ALU.add))
            dve.tensor_copy(ints[0:1, AT_BLOCKS:AT_BLOCKS + NE], bank("cum")[0:1, NE:2 * NE])\
                .then_inc(free_sem("cum"), 1)
            dve.wait_ge(*drained("cum"))
            dve.tensor_scalar(begun[0:NE, :], iota[0:NE, 0:MAX_BLOCKS + 1], plan[0:NE, 1:2], None,
                              ALU.is_ge).then_inc(begun_ready, 1)
            dve.wait_ge(*own(begun_ready))
            dve.wait_ge(*full("wT"))
            dve.tensor_copy(wT[0:NE, :], bank("wT")[0:NE, 0:NT]).then_inc(free_sem("wT"), 1)
            dve.wait_ge(*drained("wT"))
            dve.wait_ge(*full("list"))
            ls = bank("list")
            step(dve.tensor_copy(ints[0:1, AT_EXPERT:AT_EXPERT + MAX_BLOCKS + 1], ls[0:1, 0:MAX_BLOCKS + 1]))
            step(dve.tensor_tensor(plan_row[0:1, :], iota[0:1, 0:MAX_BLOCKS + 1],
                                   ls[0:1, 64:64 + MAX_BLOCKS + 1], ALU.subtract))
            dve.scalar_tensor_tensor(ints[0:1, AT_COLUMN:AT_COLUMN + MAX_BLOCKS + 1], plan_row[0:1, :],
                                     float(NE), ls[0:1, 0:MAX_BLOCKS + 1], ALU.mult, ALU.add)\
                .then_inc(free_sem("list"), 1)
            dve.wait_ge(*drained("list"))

            lanes = const("slots")

            def slots(column):
                for j in range(3):
                    last = dve.tensor_scalar(sel[:, j, :], lanes[:, 0:SLOTS], pos[:, j, column], None,
                                             ALU.is_equal)
                last.then_inc(sel_ready, 1)

            def slot_weights(column):
                for j in range(3):
                    last = dve.tensor_scalar(selw[:, j, :], lanes, pos[:, j, column], wts3[:, j, column],
                                             ALU.is_equal, ALU.mult)
                last.then_inc(selw_ready, 1)

            def hot(expert):
                dve.tensor_copy(bias_hot[0:3 * NE, :],
                                const("expert_hot", 3 * NE)[:, expert].to_broadcast([3 * NE, SLOTS]))\
                    .then_inc(bias_hot_ready, 1)

            for m in range(KT):
                dve.wait_ge(*drained("bd", m))
            for j in range(3):
                for half in range(2):
                    dve.wait_ge(*drained("h2", j, half))
            hot(slice(0, 1))
            slots(slice(0, 1))
            dve.tensor_copy(plan_row[0:1, 0:1], plan_row[0:1, 1:2]).then_inc(tables, 1)
            dve.wait_ge(*own(tables))

            def add_sums(last_blocks, i):
                dve.wait_ge(combined, 4 * last_blocks + (i - 3))
                acc = accT.rearrange("p (h i) t -> p i h t", h=2)[:, i]
                dve.tensor_tensor(acc, acc, psum[:, B_SUM[i % 2]:B_SUM[i % 2] + 2, 0:NT], ALU.add)\
                    .then_inc(added, 1)

            def expert_block(b, column, next_column, next_expert, first):
                dve.wait_ge(unit_read[1], b + 1)
                if not first:
                    dve.wait_ge(gs_ready, b)
                dve.tensor_scalar(act_g, psum[:, B_GATE, :], LIMIT, None, ALU.min).then_inc(gate_clamped, 1)
                if not first:
                    add_sums(b, 0)
                    add_sums(b, 1)
                dve.wait_ge(gate_sig, b + 1)
                dve.wait_ge(gate_clamped, b + 1)
                if not first:
                    dve.wait_ge(act_ready, b)
                dve.tensor_tensor(act_g, act_g, act_s, ALU.mult).then_inc(gs_ready, 1)
                if not first:
                    add_sums(b, 2)
                    add_sums(b, 3)
                dve.wait_ge(gathered, b + 1)
                slots(next_column)
                if not first:
                    dve.wait_ge(selw_turned, b)
                slot_weights(column)
                dve.wait_ge(unit_read[3], b + 1)
                if not first:
                    dve.wait_ge(act_turned, b)
                dve.tensor_scalar(act_u, psum[:, B_UP, :], LIMIT, -LIMIT, ALU.min, ALU.max)\
                    .then_inc(up_clamped, 1)
                dve.wait_ge(up_clamped, b + 1)
                dve.wait_ge(gs_ready, b + 1)
                dve.scalar_tensor_tensor(act_u, act_u, 1.0, act_g, ALU.add, ALU.mult).then_inc(act_ready, 1)
                hot(next_expert)
                if not first:
                    dve.wait_ge(added, 4 * b)

            expert_block(0, slice(0, 1), bass.ds(dve.value_load(
                ints[0:1, AT_COLUMN + 1:AT_COLUMN + 2], min_val=0, max_val=ROUNDS * NE - 1), 1),
                bass.ds(dve.value_load(ints[0:1, AT_EXPERT + 1:AT_EXPERT + 2], min_val=0, max_val=NE), 1), True)
            later = dve.value_load(ints[0:1, AT_LATER:AT_LATER + 1], min_val=NE - 1, max_val=MAX_BLOCKS - 1)
            with dve.Fori(0, later) as p:
                b = p + 1
                column, next_column = [dve.value_load(ints[0:1, bass.ds(b + at, 1)], min_val=0,
                                                      max_val=ROUNDS * NE - 1)
                                       for at in (AT_COLUMN, AT_COLUMN + 1)]
                next_expert = dve.value_load(ints[0:1, bass.ds(b + (AT_EXPERT + 1), 1)], min_val=0, max_val=NE)
                expert_block(b, bass.ds(column, 1), bass.ds(next_column, 1), bass.ds(next_expert, 1), False)
            blocks = later + 1
            for i in range(4):
                add_sums(blocks, i)
            dve.wait_ge(added, 4 * blocks)
            steps[0], steps[1] = 0, tail_step
            dve.tensor_copy(plan_row[0:1, 0:1], plan_row[0:1, 1:2]).then_inc(acc_final, 1)
            dve.wait_ge(*own(acc_final))
            for m in range(KT):
                gated_add(m, accT[:, m, :], 40)
            dve.tensor_tensor(fin_sq, xT[:], xT[:], ALU.mult).then_inc(x2_squared, 1)
            dve.wait_ge(*own(x2_squared))
            dve.wait_ge(*full("ss3"))
            mean_square(rstd[:], bank("ss3")[:, 0:NT], D, "ss3")
            rsqrt(rstd[:])
            step(dve.tensor_tensor(xT[:], xT[:], over(rstd[:], 1, KT), ALU.mult))
            dve.tensor_tensor(xT[:], xT[:], over(vecT[:, V_GF:V_GF + KT], 2, NT), ALU.mult)\
                .then_inc(x2_ready, 1)
            dve.wait_ge(*own(x2_ready))

        @block.scalar
        def _(act):
            def copy(out, src):
                return act.activation(out, src, ACT.Copy)

            norms = [0]

            def root(t):
                norms[0] += 1
                act.wait_ge(mean_inverse, norms[0])
                act.activation(t, t, ACT.Sqrt).then_inc(mean_root, 1)

            act.wait_ge(c_in, 32)
            act.activation(c_sig[0:9, :], c_rows[0:9, :], ACT.Sigmoid).then_inc(c_sig_done, 1)
            act.wait_ge(*own(c_sig_done))
            for j, (t0, n) in enumerate(TILES):
                for half in range(2):
                    act.wait_ge(*full("xT", j, half))
                    src = bank("xT", j, half).rearrange("p (k t) -> p k t", k=4)[:, :, 0:n]
                    copy(xT[:, 4 * half:4 * half + 4, t0:t0 + n], src).then_inc(free_sem("xT", j, half), 1)
                    act.wait_ge(*drained("xT", j, half))
            act.wait_ge(lam_dot, 1)
            act.activation(LAM[:, 2:4], LAM[:, 0:2], ACT.Exp).then_inc(lam_exp, 1)
            act.wait_ge(*own(lam_exp))
            root(rstd[:])

            def heads_T(name, j):
                t0, n = TILES[j]
                act.wait_ge(*full(name + "T", j))
                src = bank(name + "T", j).rearrange("p (h t) -> p h t", h=H)[:, :, 0:n]
                copy((qT if name == "q" else kT)[:, :, t0:t0 + n], src).then_inc(free_sem(name + "T", j), 1)
                act.wait_ge(*drained(name + "T", j))

            for j in range(3):
                heads_T("q", j)
            for j, (t0, n) in enumerate(TILES):
                act.wait_ge(*full("v", j))
                copy(va[0:n, j, :], bank("v", j)[0:n, :]).then_inc(free_sem("v", j), 1)
                act.wait_ge(*drained("v", j))
                heads_T("k", j)

            items = [(h, qb) for h in range(H) for qb in range(2)]

            def exps(i):
                n = P * (items[i][1] + 1)
                act.wait_ge(att_max, i + 1)
                for c in range(2):
                    col = 2 * (i % 2) + c
                    act.activation(s_pair[:, i % 2, c, 0:n], s_pair[:, i % 2, c, 0:n], ACT.Exp,
                                   bias=MX[:, col:col + 1], scale=DK ** -0.5,
                                   accum_out=LS[:, col:col + 1]).then_inc(att_exp, 1)
                    act.wait_ge(*own(att_exp))

            exps(0)
            for i, (h, qb) in enumerate(items):
                if i + 1 < len(items):
                    exps(i + 1)
                act.wait_ge(*full("aT", i))
                if i >= 2:
                    act.wait_ge(*full("PV", i - 2))
                n = P * (qb + 1)
                copy(aT[:, i % 2, 0:n], bank("aT", i)[:, 0:n]).then_inc(free_sem("aT", i), 1)
                act.wait_ge(*drained("aT", i))
                act.wait_ge(*full("PV", i))
                copy(oT[:, h, P * qb:P * qb + P], bank("PV", i)[:, 0:P]).then_inc(free_sem("PV", i), 1)
                act.wait_ge(*drained("PV", i))

            def key_pages(b):
                if b:
                    act.wait_ge(*full("Sn", b - 1))
                for g in range(0, PAGES, 2):
                    act.wait_ge(*full("kTb", b, g))
                    copy(kTb[:, :, PAGE * g:PAGE * g + PAGE],
                         bank("kTb", b, g).rearrange("p (h k) -> p h k", h=H))\
                        .then_inc(free_sem("kTb", b, g), 1)
                    act.wait_ge(*drained("kTb", b, g))

            nk = PAGES * PAGE

            def dec_exps(b):
                act.wait_ge(dec_max, b + 1)
                if b:
                    act.wait_ge(*full("pTn", b - 1))
                for half in range(2):
                    act.activation(p_dec[:, 512 * half:512 * half + 512], bank("Sd", b, half),
                                   ACT.Exp, bias=SC[:, 2:3], scale=DK ** -0.5,
                                   accum_out=SC[:, 3 + half:4 + half])\
                        .then_inc(free_sem("Sd", b, half), 1)
                    act.wait_ge(*drained("Sd", b, half))
                act.activation(p_dec[:, nk:nk + TS], s_new, ACT.Exp, bias=SC[:, 2:3],
                               scale=DK ** -0.5, accum_out=SC[:, 5:6]).then_inc(dec_exp, 1)
                act.wait_ge(*own(dec_exp))

            key_pages(0)
            dec_exps(0)
            key_pages(1)
            for b in range(NB):
                if b:
                    act.wait_ge(*full("od", b - 1))
                act.wait_ge(*full("pT", b, 1))
                copy(pT_dec[:, 4:8, :], bank("pT", b, 1).rearrange("p (g c) -> p g c", g=4))\
                    .then_inc(free_sem("pT", b, 1), 1)
                act.wait_ge(*drained("pT", b, 1))
                act.wait_ge(*full("pTn", b))
                copy(pTn[0:TS, :], bank("pTn", b)[0:TS, 0:P]).then_inc(free_sem("pTn", b), 1)
                act.wait_ge(*drained("pTn", b))
                if b + 1 < NB:
                    dec_exps(b + 1)
                if b + 2 < NB:
                    key_pages(b + 2)

            root(o_rms)

            act.wait_ge(region_m, 1)
            for i, key in enumerate(("qm", "km")):
                for m in range(4):
                    act.wait_ge(*full(key, m))
                    copy(raw_p[:, 4 * i + m, 3:TP + 3], bank(key, m)[:, 0:TP])
                    copy(raw_s[:, 4 * i + m, :, 3:11],
                         bank(key, m)[:, TP:NT].rearrange("p (b t) -> p b t", b=NB))\
                        .then_inc(free_sem(key, m), 1)
                    act.wait_ge(*drained(key, m))
            act.wait_ge(f_abs, 1)
            act.activation(rows_t[0:H, :], rows_t[0:H, :], ACT.Exp, scale=-1.0).then_inc(act_step, 1)
            act.wait_ge(act_step, 1)
            act.activation(rows_t[0:H, :], rows_t[0:H, :], ACT.Ln, bias=1.0).then_inc(f_ln, 1)
            act.wait_ge(*own(f_ln))
            for j, (t0, n) in enumerate(TILES):
                act.wait_ge(*full("vm", j))
                copy(vm[0:n, j, :], bank("vm", j)[0:n, :]).then_inc(free_sem("vm", j), 1)
                act.wait_ge(*drained("vm", j))
            for m in range(4):
                act.wait_ge(*full("om", m))
                act.activation(so[:, m, :], bank("om", m)[:, 0:NT], ACT.Sigmoid).then_inc(free_sem("om", m), 1)
                act.wait_ge(*drained("om", m))
            act.wait_ge(conv_done, 1)
            act.activation(cv_sig, cv[:, 0:4, :], ACT.Sigmoid).then_inc(conv_sig, 1)
            act.wait_ge(*own(conv_sig))
            act.wait_ge(conv_done, 2)
            act.wait_ge(conv_ready, 1)
            act.activation(cv_sig, cv[:, 4:8, :], ACT.Sigmoid).then_inc(conv_sig, 1)
            act.wait_ge(*own(conv_sig))
            act.wait_ge(tail_ready, 1)
            for half in range(2):
                act.wait_ge(*full("tail", half))
                copy(tail_rows[0:27, 512 * half:512 * half + 512], bank("tail", half)[0:27, :])\
                    .then_inc(free_sem("tail", half), 1)
                act.wait_ge(*drained("tail", half))
            act.wait_ge(m_rows, 1)
            act.activation(rowsR[0:H, NT:2 * NT], rows_t[0:H, :], ACT.Exp, scale=-1.0).then_inc(m_exp, 1)
            act.wait_ge(*own(m_exp))
            act.activation(rowsR[0:H, 2 * NT:2 * NT + TS], rowsR[0:H, 2 * NT:2 * NT + TS], ACT.Exp)\
                .then_inc(m_exp, 1)
            act.wait_ge(*own(m_exp))
            act.activation(rows_w[0:H, :], rows_w[0:H, :], ACT.Exp).then_inc(m_exp, 1)
            act.wait_ge(*own(m_exp))
            for h in range(H):
                act.wait_ge(*full("bc1", h))
                if h:
                    act.wait_ge(c_ready, h)
                copy(bcS, bank("bc1", h)[:, 0:384]).then_inc(free_sem("bc1", h), 1)
                act.wait_ge(*drained("bc1", h))
                act.wait_ge(*drained("bc0", h))
                act.activation(dT[:, 0:384], dT[:, 0:384], ACT.Exp)
                act.activation(dT[0:TS, 384:448], dT[0:TS, 384:448], ACT.Exp).then_inc(d_exp, 1)
                act.wait_ge(*own(d_exp))
            act.wait_ge(*full("n_out"))
            copy(n_rows[0:36, :], bank("n_out")[0:36, 0:P]).then_inc(free_sem("n_out"), 1)
            act.wait_ge(*drained("n_out"))

            root(hmT[:])

            act.wait_ge(tail_out, 32)
            for w in ("ga0", "ga1", "gb0", "gb1"):
                for m in range(4):
                    mm_ = m + 4 * int(w[2])
                    act.wait_ge(*full(w, m))
                    if w[1] == "b":
                        act.wait_ge(*drained("upa", mm_))
                    act.activation(sg[:, mm_, :], bank(w, m)[:, 0:NT], ACT.Sigmoid)\
                        .then_inc(free_sem(w, m), 1)
                    act.wait_ge(*drained(w, m))
            root(rstd[:])
            for j, (t0, n) in enumerate(TILES):
                for half in range(2):
                    act.wait_ge(*full("h2", j, half))
                    copy(h2_tok[0:n, j, 512 * half:512 * half + 512], bank("h2", j, half)[0:n, :])\
                        .then_inc(free_sem("h2", j, half), 1)
                    act.wait_ge(*drained("h2", j, half))
            act.wait_ge(top_diff, 1)
            act.activation(ew, ew, ACT.Exp).then_inc(top_exp, 1)
            act.wait_ge(*own(top_exp))
            for m in range(KT):
                act.wait_ge(*full("bd", m))
                copy(accT[:, m, :], bank("bd", m)[:, 0:NT]).then_inc(free_sem("bd", m), 1)
                act.wait_ge(*drained("bd", m))

            def copy_gathered(b, first):
                act.wait_ge(gathered, b + 1)
                if not first:
                    act.wait_ge(hg_turned, b)
                copy(hg_rows, psum[:, B_HG, :]).then_inc(hg_copied, 1)

            def copy_turned_gathered(b, first):
                act.wait_ge(hg_turned, b + 1)
                if not first:
                    act.wait_ge(unit_read[3], b)
                copy(hgT, psum[:, B_HG_T, :].rearrange("p (k s) -> p k s", k=4)).then_inc(hgT_copied, 1)

            def expert_block(b, first):
                act.wait_ge(gate_clamped, b + 1)
                if not first:
                    act.wait_ge(gs_ready, b)
                act.activation(act_s, act_g, ACT.Sigmoid, scale=ALPHA).then_inc(gate_sig, 1)
                copy_gathered(b + 1, False)
                act.wait_ge(act_turned, b + 1)
                if not first:
                    act.wait_ge(unit_read[5], b)
                copy(actT, psum[:, B_ACT_T, :].rearrange("p (k s) -> p k s", k=4)).then_inc(actT_copied, 1)
                copy_turned_gathered(b + 1, False)
                act.wait_ge(selw_turned, b + 1)
                if not first:
                    act.wait_ge(combined, 4 * b)
                copy(selwT, psum[:, B_SEL_T, 0:NT]).then_inc(selwT_copied, 1)
                act.wait_ge(unit_read[5], b + 1)
                copy(y_rows, psum[:, B_Y, :]).then_inc(y_copied, 1)

            act.wait_ge(tables, 1)
            copy_gathered(0, True)
            copy_turned_gathered(0, True)
            expert_block(0, True)
            later = act.value_load(ints[0:1, AT_LATER:AT_LATER + 1], min_val=NE - 1, max_val=MAX_BLOCKS - 1)
            with act.Fori(0, later) as p:
                expert_block(p + 1, False)
            root(rstd[:])
            for j, (t0, n) in enumerate(TILES):
                for half in range(2):
                    act.wait_ge(*full("y", j, half))
                    copy(y_out[0:n, j, 512 * half:512 * half + 512], bank("y", j, half)[0:n, :])\
                        .then_inc(free_sem("y", j, half), 1)
                    act.wait_ge(*drained("y", j, half))

        @block.gpsimd
        def _(pool):
            pool.dma_start(keep[:], I["const"][:, 0:n_keep]).then_inc(const_in, 16)
            c2 = I["c_sample"]
            pool.dma_start(c_rows[0:1, :], I["c_prompt"]).then_inc(c_in, 16)
            pool.dma_start(c_rows[1:9, :], c2).then_inc(c_in, 16)
            row = 0
            for name, n in (("b_ada", 48), ("g_norm1", 8), ("g_norm2", 8), ("g_final", 8), ("w_conv", 32),
                            ("b_conv", 8), ("g_subln", 1), ("g_mnorm", 4)):
                src = I[name].rearrange("a b -> (a b)").rearrange("(r c) -> r c", c=P)
                pool.dma_start(vec_rows[row:row + n, :], src).then_inc(vec_in, 16)
                row += n
            pool.dma_start(front_const, I["const"][:, n_keep:n_const]).then_inc(vec_in, 16)
            for i, name in enumerate(("lambda_q1", "lambda_k1", "lambda_q2", "lambda_k2")):
                pool.dma_start(lam_rows[:, i, :], I[name].to_broadcast([P, DK])).then_inc(table_in, 16)
            with nc.allow_non_contiguous_dma(reason="a few words"):
                pool.dma_start(small[0:H, 21:29], I["state_m"].rearrange("b h -> h b")).then_inc(table_in, 16)
                pool.dma_start(small[0:H, 29:30], I["b_gates"].rearrange("o h -> h o")[0:H])\
                    .then_inc(table_in, 16)
                pool.dma_start(small[0:H, 30:31], I["b_gates"].rearrange("o h -> h o")[H:2 * H])\
                    .then_inc(table_in, 16)
            for w, tile_, name in (("k", k_rot, "k"), ("v", va, "v")):
                for j, (t0, n) in enumerate(TILES):
                    if w == "k":
                        pool.wait_ge(rotated, 4 + j)
                    else:
                        pool.wait_ge(*drained("v", j))
                    dst = O[name + "_prompt"][t0:t0 + n, :] if j < 2 else O[name + "_sample"]
                    pool.dma_start(dst, tile_[0:n, j, :]).then_inc(k_stored, 16)
            pool.wait_ge(region_m, 1)
            pool.wait_ge(k_stored, 96)
            pool.dma_start(cs_rows[0:24, :], I["state_conv"]).then_inc(mrows_in, 16)
            pool.dma_start(n_rows[0:32, :], I["state_n"]).then_inc(mrows_in, 16)
            with nc.allow_non_contiguous_dma(reason="eight gate columns"):
                pool.dma_start(w_if, W_IN.rearrange("(k p) c -> p k c", p=P)[:, :, 3584:3592])\
                    .then_inc(mrows_in, 16)
            for half in range(2):
                pool.wait_ge(*drained("tail", half))
            pool.dma_start(O["conv_prompt"], tail_rows[0:3, :]).then_inc(tail_out, 16)
            pool.dma_start(O["conv_sample"], tail_rows[3:27, :]).then_inc(tail_out, 16)
            pool.wait_ge(m_rows, 1)
            with nc.allow_non_contiguous_dma(reason="a few words"):
                pool.dma_start(O["m_prompt"], rows_t[0:H, TP - 1:TP]).then_inc(state_out, 16)
                pool.dma_start(O["m_sample"].rearrange("b h -> h b"), rows_t[0:H, TP + TD - 1:NT:TD])\
                    .then_inc(state_out, 16)
            pool.wait_ge(c_ready, H)
            pool.dma_start(O["C_prompt"].rearrange("h d e -> d h e"), C_p).then_inc(state_out, 16)
            pool.dma_start(O["C_sample"].rearrange("b h d e -> d (b h) e"), unit(("C", 0), 32))\
                .then_inc(state_out, 16)
            pool.wait_ge(*drained("n_out"))
            pool.dma_start(O["n_prompt"], n_rows[0:4, :]).then_inc(state_out, 16)
            pool.dma_start(O["n_sample"], n_rows[4:36, :]).then_inc(state_out, 16)
            pool.wait_ge(state_out, 96)
            pool.wait_ge(hm_ready, 1)
            for part in range(3):
                pool.dma_start(bias_f32[NE * part:NE * part + NE, :], I["b_gu"]).then_inc(bias_in, 16)
            pool.dma_start(w_rt, I["w_router"].rearrange("(k p) e -> p k e", p=P)).then_inc(moe_in, 16)
            pool.dma_start(b_rt, I["b_router"].to_broadcast([P, NE])).then_inc(moe_in, 16)
            pool.dma_start(bd_rows[0:NE, :], I["b_down"]).then_inc(moe_in, 16)
            for j, (t0, n) in enumerate(TILES):
                for half in range(2):
                    pool.wait_ge(*drained("y", j, half))
                dst = O["y_prompt"][t0:t0 + n, :] if j < 2 else O["y_sample"]
                pool.dma_start(dst, y_out[0:n, j, :]).then_inc(y_stored, 16)
            pool.wait_ge(y_stored, 48)

        @block.sync
        def _(sp):
            sp.dma_start(ints[0:1, 0:64], I["page_table"]).then_inc(page_in, 16)
            x = I["x_prompt"]
            for j in range(2):
                sp.dma_start(x_tok[:, j, :], x[P * j:P * j + P, :]).then_inc(x_in, 16)
            sp.dma_start(x_tok[0:TS, 2, :], I["x_sample"]).then_inc(x_in, 16)
            sp.wait_ge(page_in, 16)
            for i, (name, n_dma) in enumerate(units):
                if i >= RING:
                    freed = units[i - RING][0]
                    if freed == ("C", 0):
                        sp.wait_ge(state_out, 96)
                    else:
                        sp.wait_ge(*last_use[freed])
                s = slot_of[name]
                if name[0] in "KV" and len(name[0]) == 1:
                    cache = I["cache_k" if name[0] == "K" else "cache_v"]
                    dst = unit(name, PAGES)
                    for g in range(PAGES):
                        page = sp.value_load(ints[0:1, PAGES * name[1] + g:PAGES * name[1] + g + 1],
                                             min_val=0, max_val=N_POOL - 1)
                        sp.dma_start(dst[:, g, :],
                                     cache[bass.ds(page, 1), :, :].rearrange("o p c -> p (o c)"))\
                            .then_inc(unit_landed[s], 16)
                else:
                    src, a = unit_source(name)
                    sp.dma_start(unit(name, a), src).then_inc(unit_landed[s], 16)

            gu = I["w_gu"].rearrange("e (k p) f -> e p k f", p=P)
            dn = I["w_down"].rearrange("e (k p) f -> e p k f", p=P)

            def expert_weights(expert, blocks_before):
                for i in range(RING):
                    if blocks_before is None:
                        sp.wait_ge(*last_use[units[len(units) - RING + i][0]])
                    else:
                        sp.wait_ge(unit_read[i], blocks_before)
                    q, half = i // 2, i % 2
                    w, f = (gu, FF * q) if q < 2 else (dn, 0)
                    src = w[expert, :, 4 * half:4 * half + 4, f:f + FF].rearrange("o p k f -> p (o k) f")
                    dst = ring[:, moe_slot[i], :].rearrange("p (k f) -> p k f", k=4)
                    sp.dma_start(dst, src).then_inc(unit_landed[moe_slot[i]], 16)

            expert_weights(slice(0, 1), None)
            sp.wait_ge(tables, 1)
            with sp.Fori(1, NE) as e:
                before = sp.value_load(ints[0:1, bass.ds(e + (AT_BLOCKS - 1), 1)], min_val=1,
                                       max_val=MAX_BLOCKS)
                expert_weights(bass.ds(e, 1), before)


_OUTS = [
    ("y_prompt", (TP, D), (1, TP, D)), ("y_sample", (TS, D), (NB, TD, D)),
    ("k_prompt", (TP, 512), (1, 1, TP, H, 2, DK)), ("v_prompt", (TP, 512), (1, 1, TP, H, P)),
    ("conv_prompt", (3, D), (1, 1, 3, D)), ("C_prompt", (H, P, P), (1, 1, H, P, P)),
    ("n_prompt", (H, P), (1, 1, H, P)), ("m_prompt", (H, 1), (1, 1, H)),
    ("k_sample", (TS, 512), (1, NB, TD, H, 2, DK)), ("v_sample", (TS, 512), (1, NB, TD, H, P)),
    ("conv_sample", (NB * 3, D), (1, NB, 3, D)), ("C_sample", (NB, H, P, P), (1, NB, H, P, P)),
    ("n_sample", (NB * H, P), (1, NB, H, P)), ("m_sample", (NB, H), (1, NB, H)),
]
_INS = {
    "x_prompt": (TP, D), "x_sample": (TS, D), "c_prompt": (1, D), "c_sample": (NB, D),
    "cache_k": (N_POOL, P, 512), "cache_v": (N_POOL, P, 512), "state_conv": (NB * 3, D),
    "state_C": (NB, H, P, P), "state_n": (NB * H, P), "state_m": (NB, H), "page_table": (1, 64),
    "w_ada": (D, 6 * D), "b_ada": (1, 6 * D), "g_norm1": (1, D), "g_norm2": (1, D), "w_in": (D, 5640),
    "b_gates": (1, 8), "lambda_q1": (1, DK), "lambda_k1": (1, DK), "lambda_q2": (1, DK),
    "lambda_k2": (1, DK), "g_subln": (1, P), "w_conv": (4, D), "b_conv": (1, D), "g_mnorm": (1, 512),
    "w_up_a": (512, D), "w_up_b": (512, D), "w_out": (D, D), "w_router": (D, NE), "b_router": (1, NE),
    "w_gu": (NE, D, 2 * FF), "b_gu": (NE, 2 * FF), "w_down": (NE, FF, D), "b_down": (NE, D),
    "g_final": (1, D),
}


def kernel(**inputs):
    import concourse.bacc as _bacc
    from concourse.bass_utils import run_bass_kernel_spmd as _run

    nc = _bacc.Bacc("TRN2", target_bir_lowering=False, num_devices=1)
    pack, const_at, n_keep = const_pack()
    arrays = {"in_const": pack}
    I = {"const": nc.dram_tensor("in_const", pack.shape, F32, kind="ExternalInput").ap()}
    for name, shape in _INS.items():
        a = np.ascontiguousarray(inputs[name]).reshape(shape)
        arrays["in_" + name] = a
        I[name] = nc.dram_tensor("in_" + name, shape, mybir.dt.from_np(a.dtype), kind="ExternalInput").ap()
    O = {name: nc.dram_tensor("out_" + name, shape, F32, kind="ExternalOutput").ap()
         for name, shape, _ in _OUTS}
    build(nc, I, O, const_at, pack.shape[1], n_keep)
    r = _run(nc, [arrays], core_ids=[0])
    return tuple(r.results[0]["out_" + name].reshape(final) for name, _, final in _OUTS)
```

```python
from contextlib import ExitStack

import concourse.bass as bass
import numpy as np
from concourse import mybir

F32 = mybir.dt.float32
BF16 = mybir.dt.bfloat16
I32 = mybir.dt.int32
U32 = mybir.dt.uint32
ALU = mybir.AluOpType
ACT = mybir.ActivationFunctionType
AX = mybir.AxisListType.X

P = 128
D = 1024
KT = D // P
TP = 256
NB, TD = 8, 8
TS = NB * TD
NT = TP + TS
TILES = [(0, 128), (128, 128), (256, 64)]
H = 4
DK = 64
PAGES, PAGE = 8, 128
N_POOL = 80
NE = 32
TOPK = 4
FF = 1024
EPS = 1e-6
LAM_INIT = 0.8 - 0.6
LIMIT, ALPHA = 7.0, 1.702
BIG = -1e30
RING = 6
REGION = 18120
UNIT = 4096
SLOTS = 64
ROUNDS = -(-NT // SLOTS)
MAX_BLOCKS = NE + NT * TOPK // SLOTS
AT_EXPERT = 64
AT_COLUMN = AT_EXPERT + MAX_BLOCKS + 1
AT_BLOCKS = AT_COLUMN + MAX_BLOCKS + 1
AT_LATER = AT_BLOCKS + NE
N_INTS = AT_LATER + 1


def const_pack():
    cols, at, n = [], {}, 0

    def put(name, a):
        nonlocal n
        full = np.zeros((P, a.shape[1]), np.float32)
        full[:a.shape[0]] = a
        at[name] = (n, a.shape[1])
        cols.append(full)
        n += a.shape[1]

    i = np.arange(P)
    le = (i[:, None] <= i[None, :]).astype(np.float32)
    s = np.arange(TS)
    blk = ((s[:, None] // TD == s[None, :] // TD) & (s[:, None] <= s[None, :])).astype(np.float32)
    blk128 = np.zeros((P, TS), np.float32)
    blk128[:TS] = blk
    put("ident", np.eye(P, dtype=np.float32))
    put("causal", np.concatenate([le, np.ones((P, P), np.float32), le, blk128], 1))
    put("before", (i[:, None] < i[None, :]).astype(np.float32))
    put("iota", np.tile(i.astype(np.float32), (P, 1)))
    put("valid", np.stack([np.ones(P), np.ones(P), i < TS], 1).astype(np.float32))
    put("blkind", (s[:, None] // TD == np.arange(NB)[None, :]).astype(np.float32))
    put("slots", np.tile(i % SLOTS, (P, 1)).astype(np.float32))
    put("round_start", np.tile(np.repeat(-1.0 - SLOTS * np.arange(ROUNDS), NE), (P, 1)).astype(np.float32))
    put("rounds", np.tile(np.arange(1, ROUNDS) * SLOTS + 0.5, (P, 1)).astype(np.float32))
    put("expert_hot", np.concatenate([np.tile(np.eye(NE), (4, 1)), np.zeros((4 * NE, 1))],
                                     1).astype(np.float32))
    keep = n
    put("attmask", np.concatenate([np.zeros((P, P)), np.where(i[None, :] <= i[:, None], 0, BIG)],
                                  1).astype(np.float32))
    r = np.arange(P)
    key = s
    ok = (key[None, None, :] // TD == np.arange(NB)[None, :, None]) & \
         (key[None, None, :] % TD <= (r % TD)[:, None, None])
    put("newmask", np.where(ok, 0, BIG).astype(np.float32).reshape(len(r), -1))
    pos = np.concatenate([np.arange(TP), PAGES * PAGE + np.arange(TS) % TD]).astype(np.float32)
    inv = np.float32(10000.0) ** (-np.arange(DK // 2, dtype=np.float32) * np.float32(2.0) / np.float32(DK))
    ang = pos[:, None] * inv[None, :].astype(np.float32)
    for name, f in (("cos", np.cos), ("sin", np.sin)):
        t = np.zeros((P, 3, DK // 2), np.float32)
        for j, (t0, m) in enumerate(TILES):
            t[:m, j] = f(ang[t0:t0 + m])
        put(name, t.reshape(P, -1))
    put("comp", np.stack([(r // TD) % 2 == 0, (r // TD) % 2 == 1], 1).astype(np.float32))
    sel = np.zeros((H, H, P), np.float32)
    for h in range(H):
        sel[h, h] = 1
    put("hsel", sel.reshape(H, -1))
    start = np.zeros(NT, bool)
    start[[0] + [TP + TD * b for b in range(NB)]] = True
    put("carry", np.tile(np.where(start, 0, 1).astype(np.float32), (H, 1)))
    put("drop", np.tile(np.where(start, BIG, 0).astype(np.float32), (H, 1)))
    return np.concatenate(cols, 1), at, keep


def build(nc, I, O, const_at, n_const, n_keep):
    ctx = ExitStack()
    with ctx:
        def sb(name, shape, dt=F32):
            return ctx.enter_context(nc.sbuf_tensor(name, shape, dt))

        def sem(name):
            return ctx.enter_context(nc.semaphore(name))

        ring = sb("ring", [P, RING, UNIT])
        xT = sb("xT", [P, KT, NT])
        hT = sb("hT", [P, KT, NT])
        keep = sb("keep", [P, n_keep])
        vecT = sb("vecT", [P, 128])
        bias_hot = sb("bias_hot", [P, SLOTS], BF16)
        modT = sb("modT", [P, 48, 9])
        gainT = sb("gainT", [P, 2, KT, 9])
        rstd = sb("rstd", [P, NT])
        cT = sb("cT", [P, KT, 32])
        small = sb("small", [P, 64])
        oT = sb("oT", [P, H, NT])
        hmT = sb("hmT", [P, H, NT])
        region = sb("region", [P, REGION])
        ints = sb("ints", [1, N_INTS], I32)
        psum = ctx.enter_context(nc.psum_tensor("psum", [P, 8, 512], F32))

        def const(name, rows=P):
            a, m = const_at[name]
            if a + m <= n_keep:
                return keep[0:rows, a:a + m]
            return front_const[0:rows, a - n_keep:a - n_keep + m]

        class Area:
            def __init__(self, start):
                self.at = start

            def take(self, *shape):
                m = int(np.prod(shape))
                v = region[:, self.at:self.at + m]
                self.at += m
                assert self.at <= REGION, self.at
                if len(shape) == 2:
                    v = v.rearrange("p (a b) -> p a b", a=shape[0])
                if len(shape) == 3:
                    v = v.rearrange("p (a b c) -> p a b c", a=shape[0], b=shape[1])
                return v

        front_area = Area(0)
        front_const = front_area.take(n_const - n_keep)
        A = Area(front_area.at)
        va = A.take(3, 512)
        qT = A.take(H, NT)
        kT = A.take(H, NT)
        q_rot = A.take(2, 512)
        k_rot = A.take(3, 512)
        pairs = A.take(H, 256)
        q_blocks = A.take(NB, P)
        kTb = A.take(H, PAGES * PAGE)
        B = Area(A.at - H * PAGES * PAGE)
        x_tok = B.take(3, D)
        c_rows = B.take(D)
        B = Area(A.at - H * PAGES * PAGE)
        s_pair = B.take(2, 2, 256)
        aT = B.take(2, 256)
        x_sq = Area(front_area.at).take(KT, NT)
        c_sig = q_rot.rearrange("p a b -> p (a b)")
        vec_rows = k_rot[:, 0, 0:P]
        lam_rows = k_rot[:, 1, 0:256].rearrange("p (a b) -> p a b", a=4)
        p_dec = A.take(PAGES * PAGE + TS)
        pT_dec = A.take(PAGES, P)
        pTn = A.take(P)
        o_rows = A.take(P)
        s_new = A.take(64)
        o_sq = Area(front_area.at).take(H, NT)
        o_rms = Area(front_area.at + H * NT).take(H, NT)
        M = Area(front_area.at)
        raw_p = M.take(8, TP + 3)
        raw_s = M.take(8, NB, 11)
        cv = M.take(8, NT)
        cv_sig = M.take(H, NT)
        vm = M.take(3, 512)
        h_rms = M.take(H, NT)
        rowsR = M.take(704)
        rows_u = M.take(NT)
        rows_w = M.take(NT)
        rows_f = M.take(NT)
        rows_li = M.take(NT)
        rows_t = M.take(NT)
        w_if = M.take(KT, 8)
        uw = M.take(3, 8)
        dT = M.take(448)
        bcS = M.take(384)
        qe = M.take(2, 64)
        kw = M.take(3, P)
        v_blk = M.take(NB, P)
        hr = M.take(H, NT)
        hsq = M.take(NT)
        den_s = rstd[:]
        C_p = cv_sig.rearrange("p a b -> p (a b)")[:, 0:512].rearrange("p (a b) -> p a b", a=H)
        tail = dT[:, 0:216].rearrange("p (a b) -> p a b", a=8)
        tail_rows = raw_p.rearrange("p a b -> p (a b)")[:, 0:D]
        n0T = M.take(32)
        nT = M.take(36)
        n_rows = M.take(P)
        cs_rows = cv.rearrange("p a b -> p (a b)")[:, 0:D]
        ada_rows = []
        for tile in (hmT[:], hmT[:], h_rms, hr, v_blk, h_rms):
            flat = tile.rearrange("p a b -> p (a b)")
            ada_rows += [flat[:, 0:512], flat[:, 512:1024]]
        G = Area(front_area.at)
        sg = G.take(KT, NT)
        mT = G.take(KT, NT)
        E = Area(0)
        h2_tok = E.take(3, D)
        accT = E.take(KT, NT)
        fin_at = E.at
        fin_sq = Area(fin_at).take(KT, NT)
        bias_f32 = Area(E.at + KT * NT).take(2 * FF)
        act_g = E.take(512)
        act_s = E.take(512)
        act_u = E.take(512)
        hg_rows = E.take(512)
        y_rows = E.take(512)
        actT = E.take(4, P)
        hgT = E.take(4, P)
        sel = E.take(3, SLOTS)
        selw = E.take(3, P)
        selwT = E.take(NT)
        E.at = max(E.at, fin_at + KT * NT + 2 * FF)
        logits = E.take(3, NE)
        mask = E.take(3, NE)
        wts = E.take(3, NE)
        eq = E.take(3, NE)
        pos = E.take(3, ROUNDS * NE)
        part_logits = E.take(NT)
        hot4 = E.take(3, TOPK, NE)
        hot4w = E.take(3, TOPK, NE)
        top8 = E.take(3, 8)
        idxf = E.take(3, 8)
        ew = E.take(3, 4)
        esum = E.take(3)
        b_rt = E.take(NE)
        w_rt = E.take(KT, NE)
        wT = E.take(NT)
        bd_rows = E.take(D)
        plan = E.take(2 + ROUNDS)
        begun = E.take(MAX_BLOCKS + 1)
        plan_row = E.take(MAX_BLOCKS + 1)
        fin_ss = E.take(6)
        fin_rstd = E.take(3)
        fin_gain = E.take(D)
        x1_sq = Area(REGION - KT * NT).take(KT, NT)
        assert E.at <= REGION - KT * NT
        y_out = h2_tok
        top_ix = sb("top_ix", [P, 3, 8], U32)
        gu_bias = oT[:].rearrange("p h t -> p (h t)").bitcast(BF16)[0:3 * NE, 0:2 * FF]

        V_ADA, V_G1, V_G2, V_GF, V_WC, V_BC, V_GS, V_GM = 0, 48, 56, 64, 72, 104, 112, 113

        LAM, NLAM, COEF, GS = small[:, 0:4], small[:, 4:5], small[:, 5:6], small[:, 6:7]
        MX, LS, RC = small[:, 8:12], small[:, 12:16], small[:, 16:20]
        M0 = small[0:H, 20:29]
        BG = small[0:H, 29:31]
        SC = small[:, 32:40]

        bank_full = [sem(f"bank_full{i}") for i in range(8)]
        bank_free = [sem(f"bank_free{i}") for i in range(8)]
        unit_landed = [sem(f"unit_landed{i}") for i in range(RING)]
        values_landed = [sem(f"values_landed{i}") for i in range(3)]
        const_in = sem("const_in")
        x_in = sem("x_in")
        c_in = sem("c_in")
        vec_in = sem("vec_in")
        table_in = sem("table_in")
        mrows_in = sem("mrows_in")
        moe_in = sem("moe_in")
        h_scaled = sem("h_scaled")
        h_shifted = sem("h_shifted")
        bd_cleared = sem("bd_cleared")
        dve_step = sem("dve_step")
        act_step = sem("act_step")
        unit_used = sem("unit_used")
        c_sig_done = sem("c_sig_done")
        c_silu = sem("c_silu")
        x_squared = sem("x_squared")
        ada_turned = sem("ada_turned")
        lam_dot = sem("lam_dot")
        lam_exp = sem("lam_exp")
        h_ready = sem("h_ready")
        rotated = sem("rotated")
        k_stored = sem("k_stored")
        q_blocked = sem("q_blocked")
        att_max = sem("att_max")
        att_exp = sem("att_exp")
        att_a = sem("att_a")
        dec_max = sem("dec_max")
        dec_exp = sem("dec_exp")
        o_squared = sem("o_squared")
        o_ready = sem("o_ready")
        region_m = sem("region_m")
        conv_done = sem("conv_done")
        conv_sig = sem("conv_sig")
        conv_ready = sem("conv_ready")
        tail_ready = sem("tail_ready")
        tail_out = sem("tail_out")
        f_abs = sem("f_abs")
        f_ln = sem("f_ln")
        m_rows = sem("m_rows")
        m_exp = sem("m_exp")
        d_exp = sem("d_exp")
        p_ready = sem("p_ready")
        qe_ready = sem("qe_ready")
        kw_ready = sem("kw_ready")
        h_squared = sem("h_squared")
        om_sig = sem("om_sig")
        hm_ready = sem("hm_ready")
        c_ready = sem("c_ready")
        state_out = sem("state_out")
        merged = sem("merged")
        x1_squared = sem("x1_squared")
        h2_ready = sem("h2_ready")
        top_diff = sem("top_diff")
        top_exp = sem("top_exp")
        routed = sem("routed")
        blocks_ready = sem("blocks_ready")
        begun_ready = sem("begun_ready")
        bias_in = sem("bias_in")
        tables = sem("tables")
        mean_inverse = sem("mean_inverse")
        mean_root = sem("mean_root")
        page_in = sem("page_in")
        tail_step = sem("tail_step")
        unit_read = [sem(f"unit_read{i}") for i in range(RING)]
        gate_clamped = sem("gate_clamped")
        gate_sig = sem("gate_sig")
        gs_ready = sem("gs_ready")
        up_clamped = sem("up_clamped")
        act_ready = sem("act_ready")
        act_turned = sem("act_turned")
        actT_copied = sem("actT_copied")
        bias_hot_ready = sem("bias_hot_ready")
        sel_ready = sem("sel_ready")
        gathered = sem("gathered")
        hg_copied = sem("hg_copied")
        hg_turned = sem("hg_turned")
        hgT_copied = sem("hgT_copied")
        selw_ready = sem("selw_ready")
        selw_turned = sem("selw_turned")
        selwT_copied = sem("selwT_copied")
        y_copied = sem("y_copied")
        combined = sem("combined")
        added = sem("added")
        acc_final = sem("acc_final")
        x2_ready = sem("x2_ready")
        x2_squared = sem("x2_squared")
        fin_ss_set = sem("fin_ss_set")
        gain_in = sem("gain_in")
        y_stored = sem("y_stored")

        groups, used, turn = {}, [0] * 8, {}

        def claim(pe, pool, *key):
            k = turn.get(pool, 0)
            turn[pool] = k + 1
            b = pool[k % len(pool)]
            if used[b]:
                pe.wait_ge(bank_free[b], used[b])
            used[b] += 1
            groups[key] = (b, used[b])
            return psum[:, b, :]

        def bank(*key):
            return psum[:, groups[key][0], :]

        def full(*key):
            return bank_full[groups[key][0]], groups[key][1]

        def full_sem(*key):
            return bank_full[groups[key][0]]

        def drained(*key):
            return bank_free[groups[key][0]], groups[key][1]

        def free_sem(*key):
            return bank_free[groups[key][0]]

        units, last_use = [], {}

        def add_unit(name, n_dma=1):
            units.append((name, n_dma))

        for i in range(4):
            add_unit(("ada", i))
        for w in ("q", "k", "v", "om"):
            add_unit((w, 0))
        for b in range(NB):
            add_unit(("K", b), PAGES)
            add_unit(("V", b), PAGES)
        for w, modulations in (("qm", (4, 5)), ("km", (6, 7)), ("vm", (8, 9, 10, 11))):
            add_unit((w, 0))
            for i in modulations:
                add_unit(("ada", i))
        add_unit(("C", 0))
        for w in ("ga0", "ga1", "upa", "gb0", "gb1", "upb", "wo0", "wo1"):
            add_unit((w, 0))
        slot_of, landed_at, count = {}, {}, [0] * RING
        for i, (name, n_dma) in enumerate(units):
            s = i % RING
            if name[0] == "V":
                slot_of[name], landed_at[name] = s, 16 * PAGES * (name[1] // 3 + 1)
                continue
            count[s] += 16 * n_dma
            slot_of[name], landed_at[name] = s, count[s]
        first_slot = len(units) % RING
        moe_slot = [(first_slot + i) % RING for i in range(RING)]
        landed_base = [count[moe_slot[i]] for i in range(RING)]

        def unit(name, a, b=None):
            v = ring[:, slot_of[name], :]
            return v.rearrange("p (a b) -> p a b", a=a)

        def landed(name):
            if name[0] == "V":
                return values_landed[name[1] % 3], landed_at[name]
            return unit_landed[slot_of[name]], landed_at[name]

        W_IN = I["w_in"]
        PIECE = {"q": 0, "k": 512, "v": 1024, "qm": 1536, "km": 2048, "vm": 2560, "om": 3072,
                 "ga0": 3592, "ga1": 4104, "gb0": 4616, "gb1": 5128}

        def unit_source(name):
            w, i = name
            if w == "ada":
                return I["w_ada"].rearrange("(k p) c -> p k c", p=P)[:, :, 512 * i:512 * (i + 1)], 8
            if w in PIECE:
                return W_IN.rearrange("(k p) c -> p k c", p=P)[:, :, PIECE[w]:PIECE[w] + 512], 8
            if w in ("upa", "upb"):
                return I["w_up_a" if w == "upa" else "w_up_b"].rearrange("(k p) c -> p k c", p=P), 4
            if w in ("wo0", "wo1"):
                k = 4 * int(w[2])
                return I["w_out"].rearrange("(k p) c -> p k c", p=P)[:, k:k + 4, :], 4
            assert w == "C"
            return I["state_C"].rearrange("b h d e -> d (b h) e"), 32

        def load_pages(engine, name):
            cache = I["cache_k" if name[0] == "K" else "cache_v"]
            dst = unit(name, PAGES)
            for g in range(PAGES):
                at = PAGES * name[1] + g
                page = engine.value_load(ints[0:1, at:at + 1], min_val=0, max_val=N_POOL - 1)
                engine.dma_start(dst[:, g, :], cache[bass.ds(page, 1), :, :].rearrange("o p c -> p (o c)"))\
                    .then_inc(landed(name)[0], 16)

        KEY_PAGES = {"act": (0, 1, 5, 7), "dve": (2, 3, 4, 6)}
        B_GATE, B_UP, B_Y, B_HG, B_ACT_T, B_SEL_T, B_HG_T = 0, 1, 2, 3, 4, 5, 6
        B_SUM = (6, 4)

        block = ctx.enter_context(nc.Block())

        @block.tensor
        def _(pe):
            def mm(out, lhsT, rhs, start, stop):
                return pe.matmul(out, lhsT, rhs, start=start, stop=stop, skip_group_check=True)

            ident = const("ident")
            ones = const("causal")[:, P:2 * P]
            LOW, HIGH, ALLB = (0, 1, 2, 3), (4, 5, 6, 7), (0, 1, 2, 3, 4, 5, 6, 7)

            pe.wait_ge(const_in, 16)
            pe.wait_ge(c_silu, 1)
            out = claim(pe, ALLB, "cT")
            for k in range(KT):
                last = pe.transpose(out[:, 9 * k:9 * k + 9], c_rows[0:9, P * k:P * k + P], ident[0:9, 0:9])
            last.then_inc(full_sem("cT"), 1)
            pe.wait_ge(x_in, 48)
            for j, (t0, n) in enumerate(TILES):
                for half in range(2):
                    out = claim(pe, ALLB, "xT", j, half)
                    for i in range(4):
                        k = 4 * half + i
                        last = pe.transpose(out[:, P * i:P * i + n], x_tok[0:n, j, P * k:P * k + P],
                                            ident[0:n, 0:n])
                    last.then_inc(full_sem("xT", j, half), 1)


            def ada(i):
                pe.wait_ge(*landed(("ada", i)))
                w = unit(("ada", i), 8)
                out = claim(pe, ALLB, "ada", i)
                for r in range(2):
                    for j in range(4):
                        last = mm(out[32 * j:32 * j + 32, :], cT[:, 4 * r + j, :], w[:, 4 * r + j, :],
                                  r == 0, r == 1)
                last.then_inc(full_sem("ada", i), 1)
                last_use[("ada", i)] = full("ada", i)

            def turn_ada(i):
                if i % 4 == 0:
                    claim(pe, ALLB, "adaT", i // 4)
                out = bank("adaT", i // 4)
                pe.wait_ge(*drained("ada", i))
                for q in range(4):
                    c = P * (i % 4) + 32 * q
                    last = mm(out[:, c:c + 32], ada_rows[i][:, P * q:P * q + P],
                              const("expert_hot")[:, 0:32], True, True)
                last.then_inc(ada_turned if i % 4 < 3 else full_sem("adaT", i // 4), 1)

            pe.wait_ge(*drained("cT"))

            def sum_squares():
                pe.wait_ge(x_squared, 1)
                out = claim(pe, ALLB, "ss1")
                for k in range(KT):
                    last = mm(out[:, 0:NT], ones, x_sq[:, k, :], k == 0, k == KT - 1)
                last.then_inc(full_sem("ss1"), 1)

            ada(0)
            sum_squares()
            for i in range(1, 4):
                ada(i)
                turn_ada(i - 1)
            pe.wait_ge(vec_in, 16 * 9)
            out = claim(pe, ALLB, "vec")
            pe.transpose(out[:, 0:117], vec_rows[0:117, :], ident[0:117, 0:117]).then_inc(full_sem("vec"), 1)
            turn_ada(3)

            pe.wait_ge(h_ready, 1)
            pe.wait_ge(h_shifted, KT)

            def token_major(name, pool, after=None):
                pe.wait_ge(*landed((name, 0)))
                w = unit((name, 0), 8)
                for j, (t0, n) in enumerate(TILES):
                    out = claim(pe, pool, name, j)
                    for k in range(KT):
                        last = mm(out[0:n, :], hT[:, k, t0:t0 + n], w[:, k, :], k == 0, k == KT - 1)
                    last.then_inc(full_sem(name, j), 1)
                    if after:
                        after(j)
                last_use[(name, 0)] = full(name, 2)

            def turn_heads(name, j):
                t0, n = TILES[j]
                pe.wait_ge(rotated, (0 if name == "q" else 3) + j + 1)
                out = claim(pe, HIGH, name + "T", j)
                src = q_rot[:, j % 2, :] if name == "q" else k_rot[:, j, :]
                for h in range(H):
                    last = pe.transpose(out[:, P * h:P * h + n], src[0:n, P * h:P * h + P], ident[0:n, 0:n])
                last.then_inc(full_sem(name + "T", j), 1)

            token_major("q", LOW)
            turn_heads("q", 0)
            token_major("k", LOW, lambda j: turn_heads("q", j + 1) if j < 2 else None)
            token_major("v", LOW, lambda j: turn_heads("k", j))

            items = [(h, qb) for h in range(H) for qb in range(2)]

            def att_scores(i):
                h, qb = items[i]
                for c in range(2):
                    out = claim(pe, (0, 1), "S", i, c)
                    mm(out[:, 0:P * (qb + 1)], qT[DK * c:DK * c + DK, h, P * qb:P * qb + P],
                       kT[DK * c:DK * c + DK, h, 0:P * (qb + 1)], True, True).then_inc(full_sem("S", i, c), 1)

            for w in "qk":
                for j in range(3):
                    pe.wait_ge(*drained(w + "T", j))
            for j in range(3):
                pe.wait_ge(*drained("v", j))
            w_om = unit(("om", 0), 8)

            def output_gate(m, half):
                if half == 0:
                    pe.wait_ge(*landed(("om", 0)))
                    claim(pe, (2, 3), "om", m)
                for k in range(4 * half, 4 * half + 4):
                    last = mm(bank("om", m)[:, 0:NT], w_om[:, k, P * m:P * m + P], hT[:, k, :],
                              k == 0, k == KT - 1)
                if half == 1:
                    last.then_inc(full_sem("om", m), 1)
                    if m == 3:
                        last_use[("om", 0)] = full("om", 3)

            def att_values(i):
                h, qb = items[i]
                out = claim(pe, (6, 7), "PV", i)
                pe.wait_ge(*drained("aT", i))
                for t in range(qb + 1):
                    last = mm(out[:, 0:P], va[:, t, P * h:P * h + P], aT[:, i % 2, P * t:P * t + P],
                              t == 0, t == qb)
                last.then_inc(full_sem("PV", i), 1)

            att_scores(0)
            for i, (h, qb) in enumerate(items):
                if i + 1 < len(items):
                    att_scores(i + 1)
                output_gate(i // 2, i % 2)
                pe.wait_ge(att_a, i + 1)
                out = claim(pe, (4, 5), "aT", i)
                for t in range(qb + 1):
                    last = pe.transpose(out[:, P * t:P * t + P], s_pair[:, i % 2, 0, P * t:P * t + P], ident)
                last.then_inc(full_sem("aT", i), 1)
                if i:
                    att_values(i - 1)
            att_values(len(items) - 1)

            def turn_keys(b, pages=range(PAGES)):
                pe.wait_ge(*landed(("K", b)))
                kc = unit(("K", b), PAGES)
                for g in pages:
                    out = claim(pe, (0, 1), "kTb", b, g)
                    for h in range(H):
                        last = pe.transpose(out[:, P * h:P * h + P], kc[:, g, P * h:P * h + P], ident)
                    last.then_inc(full_sem("kTb", b, g), 1)
                if pages[-1] == PAGES - 1:
                    last_use[("K", b)] = full("kTb", b, PAGES - 1)

            HEAD = [slice(32 * h, 32 * h + 32) for h in range(H)]

            def dec_scores(b):
                for half in range(2):
                    out = claim(pe, (4 + half,), "Sd", b, half)
                    for g in range(4 * half, 4 * half + 4):
                        pe.wait_ge(*drained("kTb", b, g))
                    for h in range(H):
                        last = mm(out[HEAD[h], :], q_blocks[:, b, HEAD[h]],
                                  kTb[:, h, 512 * half:512 * half + 512], True, True)
                    last.then_inc(full_sem("Sd", b, half), 1)
                out = claim(pe, (2,), "Sn", b)
                for h in range(H):
                    last = mm(out[HEAD[h], 0:TS], q_blocks[:, b, HEAD[h]], kT[:, h, TP:NT], True, True)
                last.then_inc(full_sem("Sn", b), 1)

            pe.wait_ge(q_blocked, 1)
            turn_keys(0)
            dec_scores(0)
            turn_keys(1)
            for b in range(NB):
                pe.wait_ge(dec_exp, b + 1)
                for half in range(2):
                    out = claim(pe, (6 + half,), "pT", b, half)
                    for i in range(4):
                        g = 4 * half + i
                        last = pe.transpose(out[:, P * i:P * i + P], p_dec[:, P * g:P * g + P], ident)
                    last.then_inc(full_sem("pT", b, half), 1)
                out = claim(pe, (3,), "pTn", b)
                pe.transpose(out[0:TS, 0:P], p_dec[:, PAGES * PAGE:PAGES * PAGE + TS], ident)\
                    .then_inc(full_sem("pTn", b), 1)
                if b + 1 < NB:
                    dec_scores(b + 1)
                if b + 2 < NB:
                    turn_keys(b + 2, range(0, 2))
                pe.wait_ge(*landed(("V", b)))
                vc = unit(("V", b), PAGES)
                for half in range(2):
                    pe.wait_ge(*drained("pT", b, half))
                out = claim(pe, (3,), "od", b)
                for g in range(PAGES):
                    for h in range(H):
                        mm(out[HEAD[h], 0:P], pT_dec[:, g, HEAD[h]], vc[:, g, P * h:P * h + P], g == 0, False)
                for h in range(H):
                    last = mm(out[HEAD[h], 0:P], pTn[0:TS, HEAD[h]], va[0:TS, 2, P * h:P * h + P],
                              False, True)
                last.then_inc(full_sem("od", b), 1)
                last_use[("V", b)] = full("od", b)
                if b + 2 < NB:
                    turn_keys(b + 2, range(2, PAGES))
                pe.wait_ge(*drained("od", b))
                out = claim(pe, (3,), "odT", b)
                pe.transpose(out[:, 0:P], o_rows, ident).then_inc(full_sem("odT", b), 1)
            pe.wait_ge(o_squared, 1)
            for h in range(H):
                out = claim(pe, LOW, "oss", h)
                mm(out[:, 0:NT], ones, o_sq[:, h, :], True, True).then_inc(full_sem("oss", h), 1)

            def feature_major(name, key, pool, ms=range(4)):
                pe.wait_ge(*landed((name, 0)))
                w = unit((name, 0), 8)
                for m in ms:
                    out = claim(pe, pool, key, m)
                    for k in range(KT):
                        last = mm(out[:, 0:NT], w[:, k, P * m:P * m + P], hT[:, k, :], k == 0, k == KT - 1)
                    last.then_inc(full_sem(key, m), 1)
                    if m == 3:
                        last_use[(name, 0)] = full(key, 3)

            def up(w, src, ms=range(KT)):
                pe.wait_ge(*landed((w, 0)))
                u = unit((w, 0), 4)
                for m in ms:
                    out = claim(pe, ALLB, w, m)
                    for k in range(4):
                        last = mm(out[:, 0:NT], u[:, k, P * m:P * m + P], src[:, k, :], k == 0, k == 3)
                    last.then_inc(full_sem(w, m), 1)
                    if m == KT - 1:
                        last_use[(w, 0)] = full(w, KT - 1)

            feature_major("qm", "qm", ALLB)
            for i in range(4, 6):
                ada(i)
            pe.wait_ge(mrows_in, 48)
            for r, key in enumerate(("gi", "gf")):
                out = claim(pe, ALLB, key)
                for k in range(KT):
                    last = mm(out[0:H, 0:NT], w_if[:, k, 4 * r:4 * r + 4], hT[:, k, :], k == 0, k == KT - 1)
                last.then_inc(full_sem(key), 1)
            out = claim(pe, ALLB, "cs")
            for m in range(8):
                pe.transpose(out[:, 24 * m:24 * m + 24], cs_rows[0:24, P * m:P * m + P], ident[0:24, 0:24])
            pe.transpose(out[:, 192:224], n_rows[0:32, :], ident[0:32, 0:32]).then_inc(full_sem("cs"), 1)
            feature_major("km", "km", ALLB)
            for i in range(6, 8):
                ada(i)
            token_major("vm", ALLB)
            for i in range(4, 8):
                turn_ada(i)
            for i in range(8, 12):
                ada(i)
            pe.wait_ge(tail_ready, 1)
            for half in range(2):
                out = claim(pe, ALLB, "tail", half)
                for i in range(4):
                    last = pe.transpose(out[0:27, P * i:P * i + P], tail[:, 4 * half + i, :], ident)
                last.then_inc(full_sem("tail", half), 1)
            pe.wait_ge(m_exp, 3)
            out = claim(pe, ALLB, "uw")
            for j, (t0, n) in enumerate(TILES):
                pe.transpose(out[0:n, 8 * j:8 * j + 4], rows_u[0:H, t0:t0 + n], ident[0:H, 0:H])
                last = pe.transpose(out[0:n, 8 * j + 4:8 * j + 8], rows_w[0:H, t0:t0 + n], ident[0:H, 0:H])
            last.then_inc(full_sem("uw"), 1)
            for i in range(8, 12):
                turn_ada(i)
            pe.wait_ge(conv_ready, 2)
            hsel = const("hsel").rearrange("p (h m) -> p h m", h=H)
            pe.wait_ge(*landed(("C", 0)))
            c0 = unit(("C", 0), 32)
            for j in range(3):
                pe.wait_ge(*drained("vm", j))
            for h in range(H):
                cq, ck = cv[:, h, :], cv[:, 4 + h, :]
                out = claim(pe, ALLB, "bc0", h)
                mm(out[:, 0:NT], hsel[0:H, h, :], rowsR[0:H, 0:NT], True, True).then_inc(full_sem("bc0", h), 1)
                out = claim(pe, ALLB, "bc1", h)
                mm(out[:, 0:384], hsel[0:H, h, :], rowsR[0:H, NT:704], True, True)\
                    .then_inc(full_sem("bc1", h), 1)
                out = claim(pe, ALLB, "st", h)
                mm(out[:, 0:256], ck[:, 0:P], cq[:, 0:TP], True, True)
                mm(out[:, 256:384], ck[:, P:TP], cq[:, P:TP], True, True)
                mm(out[0:TS, 384:448], ck[:, TP:NT], cq[:, TP:NT], True, True).then_inc(full_sem("st", h), 1)
                out = claim(pe, ALLB, "kt", h)
                for j, (t0, n) in enumerate(TILES):
                    last = pe.transpose(out[0:n, P * j:P * j + P], ck[:, t0:t0 + n], ident)
                last.then_inc(full_sem("kt", h), 1)
                feature_major("ga0" if h < 2 else "ga1", "ga0" if h < 2 else "ga1", ALLB,
                              (2 * (h % 2), 2 * (h % 2) + 1))
                pe.wait_ge(kw_ready, h + 1)
                out = claim(pe, ALLB, "C", h)
                for j in range(2):
                    mm(out[:, 0:P], kw[:, j, :], vm[:, j, P * h:P * h + P], j == 0, j == 1)
                for j in range(2):
                    mm(out[:, P:P + 1], kw[:, j, :], ones[:, 0:1], j == 0, j == 1)
                mm(out[:, 130:138], kw[0:TS, 2, :], const("blkind", TS), True, True)\
                    .then_inc(full_sem("C", h), 1)
                for half in range(2):
                    out = claim(pe, ALLB, "Cs", h, half)
                    mm(out[:, :], kw[0:TS, 2, :],
                       v_blk[0:TS, 4 * half:4 * half + 4, :].rearrange("p a b -> p (a b)"),
                       True, True).then_inc(full_sem("Cs", h, half), 1)
                pe.wait_ge(p_ready, h + 1)
                pe.wait_ge(*drained("st", h))
                pe.wait_ge(qe_ready, h + 1)
                out = claim(pe, ALLB, "num", h)
                vh = vm[:, :, P * h:P * h + P]
                mm(out[:, 0:TP], vh[:, 0, :], dT[:, 0:TP], True, False)
                mm(out[:, P:TP], vh[:, 1, :], dT[:, 256:384], False, True)
                mm(out[:, TP:NT], vh[0:TS, 2, :], dT[0:TS, 384:448], False, False)
                for b in range(NB):
                    last = mm(out[:, TP + TD * b:TP + TD * b + TD], c0[:, H * b + h, :],
                              qe[:, 0, TD * b:TD * b + TD], False, True)
                last.then_inc(full_sem("num", h), 1)
                out = claim(pe, ALLB, "den", h)
                mm(out[:, 0:TP], ones, dT[:, 0:TP], True, False)
                mm(out[:, P:TP], ones, dT[:, 256:384], False, True)
                mm(out[:, TP:NT], ones[0:TS, :], dT[0:TS, 384:448], False, False)
                mm(out[:, TP:NT], ones, qe[:, 1, :], False, True).then_inc(full_sem("den", h), 1)
                pe.wait_ge(o_ready, 1)
                up("upa", oT, (2 * h, 2 * h + 1))
                pe.wait_ge(h_squared, h + 1)
                out = claim(pe, ALLB, "hss", h)
                mm(out[:, 0:NT], ones, hsq, True, True).then_inc(full_sem("hss", h), 1)
            pe.wait_ge(c_ready, H)
            out = claim(pe, ALLB, "n_out")
            pe.transpose(out[0:36, 0:P], nT, ident).then_inc(full_sem("n_out"), 1)

            feature_major("gb0", "gb0", ALLB)
            feature_major("gb1", "gb1", ALLB)
            pe.wait_ge(hm_ready, 1)
            up("upb", hmT)
            pe.wait_ge(*landed(("wo0", 0)))
            pe.wait_ge(*landed(("wo1", 0)))
            pe.wait_ge(merged, KT)
            for m in range(KT):
                out = claim(pe, ALLB, "wo", m)
                for k in range(KT):
                    w = unit(("wo0" if k < 4 else "wo1", 0), 4)
                    last = mm(out[:, 0:NT], w[:, k % 4, P * m:P * m + P], mT[:, k, :], k == 0, k == KT - 1)
                last.then_inc(full_sem("wo", m), 1)
                if m == 0:
                    ss2 = claim(pe, ALLB, "ss2")
                else:
                    pe.wait_ge(x1_squared, m)
                    mm(ss2[:, 0:NT], ones, x1_sq[:, m - 1, :], m == 1, False)
            last_use[("wo0", 0)] = last_use[("wo1", 0)] = full("wo", KT - 1)

            pe.wait_ge(x1_squared, KT)
            mm(ss2[:, 0:NT], ones, x1_sq[:, KT - 1, :], False, True).then_inc(full_sem("ss2"), 1)
            pe.wait_ge(h2_ready, 1)
            pe.wait_ge(h_shifted, 2 * KT)
            pe.wait_ge(moe_in, 48)
            out = claim(pe, ALLB, "part_logits")
            for i in range(2):
                for g in range(4):
                    last = mm(out[NE * g:NE * g + NE, 0:NT], w_rt[:, 4 * i + g, :], hT[:, 4 * i + g, :],
                              i == 0, i == 1)
            last.then_inc(full_sem("part_logits"), 1)
            pe.wait_ge(*drained("part_logits"))
            out = claim(pe, ALLB, "logit")
            for j, (t0, n) in enumerate(TILES):
                last = mm(out[0:n, NE * j:NE * j + NE], part_logits[:, t0:t0 + n],
                          const("expert_hot")[:, 0:NE], True, True)
            last.then_inc(full_sem("logit"), 1)
            for j, (t0, n) in enumerate(TILES):
                for half in range(2):
                    out = claim(pe, ALLB, "h2", j, half)
                    for i in range(4):
                        last = pe.transpose(out[0:n, P * i:P * i + P], hT[:, 4 * half + i, t0:t0 + n], ident)
                    last.then_inc(full_sem("h2", j, half), 1)
            pe.wait_ge(routed, 1)
            out = claim(pe, ALLB, "pos")
            before = const("before")
            mm(out[:, 0:3 * NE], before, mask.rearrange("p j e -> p (j e)"), True, False)
            mm(out[:, NE:2 * NE], ones, mask[:, 0, :], False, False)
            mm(out[:, 2 * NE:3 * NE], ones, mask[:, 0, :], False, False)
            mm(out[:, 2 * NE:3 * NE], ones, mask[:, 1, :], False, True)
            for i in range(3):
                last = mm(out[0:NE, 128:129], mask[:, i, :], ones[:, 0:1], i == 0, i == 2)
            last.then_inc(full_sem("pos"), 1)
            out = claim(pe, ALLB, "wT")
            for j, (t0, n) in enumerate(TILES):
                last = pe.transpose(out[0:NE, t0:t0 + n], wts[0:n, j, :], ident[0:n, 0:n])
            last.then_inc(full_sem("wT"), 1)
            def down_bias(ms):
                for m in ms:
                    out = claim(pe, ALLB, "bd", m)
                    mm(out[:, 0:NT], bd_rows[:, P * m:P * m + P], wT, True, True)\
                        .then_inc(full_sem("bd", m), 1)

            pe.wait_ge(*drained("wT"))
            down_bias(range(0, 2))
            pe.wait_ge(blocks_ready, 1)
            out = claim(pe, ALLB, "cum")
            upto = const("causal", NE)[:, 0:NE]
            mm(out[0:NE, 0:1], upto, plan[0:NE, 0:1], True, True)
            mm(out[0:1, NE:2 * NE], plan[0:NE, 0:1], upto, True, True).then_inc(full_sem("cum"), 1)
            down_bias(range(2, 4))
            pe.wait_ge(begun_ready, 1)
            out = claim(pe, ALLB, "list")
            mm(out[0:1, 0:MAX_BLOCKS + 1], ones[0:NE, 0:1], begun[0:NE, :], True, True)
            mm(out[0:1, 64:64 + MAX_BLOCKS + 1], plan[0:NE, 0:1], begun[0:NE, :], True, True)\
                .then_inc(full_sem("list"), 1)
            down_bias(range(4, KT))

            H0, H1 = slice(0, SLOTS), slice(SLOTS, P)

            def pair(out_bank, lhsT, rhs_at, start, stop):
                for h, rows in enumerate((H0, H1)):
                    last = mm(psum[rows, out_bank, :], lhsT, rhs_at(h), start, stop)
                return last

            def gather(b):
                for j, (t0, m) in enumerate(TILES):
                    last = pair(B_HG, sel[0:m, j, :],
                                lambda h: h2_tok[0:m, j, 512 * h:512 * h + 512], j == 0, j == 2)
                last.then_inc(gathered, 1)

            def turn_gathered():
                for i in range(4):
                    last = pe.transpose(psum[:, B_HG_T, P * i:P * i + P], hg_rows[:, P * i:P * i + P], ident)
                last.then_inc(hg_turned, 1)

            def column_products(bank_, u, halves, lhsT_at, first, last_k, done):
                for k in range(4):
                    last = pair(bank_, lhsT_at(k), lambda h: u[:, k, halves(h)], first and k == 0,
                                last_k and k == 3)
                last.then_inc(done, 1)

            def gate_or_up(b, expert, q, bank_, between):
                pair(bank_, bias_hot[0:3 * NE, :],
                     lambda h: gu_bias[:, FF * q + 512 * h:FF * q + 512 * h + 512], True, False)
                for half in range(2):
                    i = 2 * q + half
                    if half == 1:
                        between()
                    pe.wait_ge(unit_landed[moe_slot[i]], 16 * expert + (landed_base[i] + 16))
                    u = ring[:, moe_slot[i], :].rearrange("p (k f) -> p k f", k=4)
                    column_products(bank_, u, lambda h: slice(512 * h, 512 * h + 512),
                                    lambda k: hgT[:, k, SLOTS * half:SLOTS * half + SLOTS],
                                    False, half == 1, unit_read[i])

            def combine(i):
                for h, rows in enumerate((H0, H1)):
                    last = mm(psum[:, B_SUM[i % 2] + h, 0:NT], y_rows[rows, P * i:P * i + P],
                              selwT[rows, :], True, True)
                last.then_inc(combined, 1)

            def expert_block(b, expert, first):
                if not first:
                    pe.wait_ge(gate_clamped, b)
                pe.wait_ge(bias_hot_ready, b + 1)
                pe.wait_ge(hgT_copied, b + 1)
                gate_or_up(b, expert, 0, B_GATE, lambda: None)
                if not first:
                    pe.wait_ge(y_copied, b)
                    pe.wait_ge(selwT_copied, b)
                    pe.wait_ge(hgT_copied, b + 1)
                    combine(0)
                    pe.wait_ge(actT_copied, b)
                    combine(1)
                    pe.wait_ge(up_clamped, b)

                def rest():
                    if not first:
                        pe.wait_ge(added, 4 * b - 3)
                        combine(2)
                        pe.wait_ge(added, 4 * b - 2)
                        combine(3)
                gate_or_up(b, expert, 1, B_UP, rest)
                pe.wait_ge(sel_ready, b + 2)
                pe.wait_ge(hg_copied, b + 1)
                gather(b + 1)
                if not first:
                    pe.wait_ge(added, 4 * b)
                pe.wait_ge(act_ready, b + 1)
                for i in range(4):
                    last = pe.transpose(psum[:, B_ACT_T, P * i:P * i + P], act_u[:, P * i:P * i + P], ident)
                last.then_inc(act_turned, 1)
                pe.wait_ge(hg_copied, b + 2)
                turn_gathered()
                pe.wait_ge(selw_ready, b + 1)
                for j, (t0, m) in enumerate(TILES):
                    last = pe.transpose(psum[:, B_SEL_T, t0:t0 + m], selw[0:m, j, :], ident[0:m, 0:m])
                last.then_inc(selw_turned, 1)
                pe.wait_ge(actT_copied, b + 1)
                if not first:
                    pe.wait_ge(y_copied, b)
                for half in range(2):
                    i = 4 + half
                    pe.wait_ge(unit_landed[moe_slot[i]], 16 * expert + (landed_base[i] + 16))
                    u = ring[:, moe_slot[i], :].rearrange("p (k f) -> p k f", k=4)
                    column_products(B_Y, u, lambda h: slice(512 * h, 512 * h + 512),
                                    lambda k: actT[:, k, SLOTS * half:SLOTS * half + SLOTS],
                                    half == 0, half == 1, unit_read[i])

            for b in range(8):
                pe.wait_ge(bank_free[b], used[b])
            pe.wait_ge(sel_ready, 1)
            gather(0)
            pe.wait_ge(hg_copied, 1)
            turn_gathered()
            expert_block(0, 0, True)
            pe.wait_ge(tables, 1)
            later = pe.value_load(ints[0:1, AT_LATER:AT_LATER + 1], min_val=NE - 1, max_val=MAX_BLOCKS - 1)
            with pe.Fori(0, later) as p:
                b = p + 1
                expert = pe.value_load(ints[0:1, bass.ds(b + AT_EXPERT, 1)], min_val=0, max_val=NE - 1)
                expert_block(b, expert, False)
            blocks = later + 1
            pe.wait_ge(y_copied, blocks)
            pe.wait_ge(selwT_copied, blocks)
            pe.wait_ge(hgT_copied, blocks + 1)
            pe.wait_ge(actT_copied, blocks)
            for i in range(4):
                if i >= 2:
                    pe.wait_ge(added, 4 * blocks + (i - 5))
                combine(i)
            pe.wait_ge(acc_final, 1)

            for half in range(2):
                pe.wait_ge(x2_ready, half + 1)
                for j, (t0, n) in enumerate(TILES):
                    out = claim(pe, ALLB, "y", j, half)
                    for i in range(4):
                        last = pe.transpose(out[0:n, P * i:P * i + P], xT[:, 4 * half + i, t0:t0 + n], ident)
                    last.then_inc(full_sem("y", j, half), 1)

        own_count = {}

        def own(s):
            own_count[s.name] = own_count.get(s.name, 0) + 1
            return s, own_count[s.name]

        def over(ap, axis, n):
            v = ap.unsqueeze(axis)
            shape = list(v.shape)
            shape[axis] = n
            return v.to_broadcast(shape)

        @block.vector
        def _(dve):
            steps = [0, dve_step]

            def step(ins):
                steps[0] += 1
                ins.then_inc(steps[1], 1)
                dve.wait_ge(steps[1], steps[0])

            iota, valid = const("iota"), const("valid")
            step(dve.memset(M0[:, 0:1], 0.0))

            norms = [0]

            def mean_square(out, src, n, *key):
                dve.tensor_scalar(out, src, 1.0 / n, EPS, ALU.mult, ALU.add).then_inc(free_sem(*key), 1)
                dve.wait_ge(*drained(*key))

            def rsqrt(t):
                norms[0] += 1
                dve.reciprocal(t, t).then_inc(mean_inverse, 1)
                dve.wait_ge(mean_root, norms[0])

            dve.wait_ge(c_sig_done, 1)
            dve.tensor_tensor(c_rows[0:9, :], c_rows[0:9, :], c_sig[0:9, :], ALU.mult).then_inc(c_silu, 1)
            dve.wait_ge(*own(c_silu))
            dve.wait_ge(*full("cT"))
            step(dve.memset(cT[:], 0.0))
            dve.tensor_copy(cT[:, :, 0:9], bank("cT")[:, 0:72].rearrange("p (k r) -> p k r", k=KT))\
                .then_inc(free_sem("cT"), 1)
            dve.wait_ge(*drained("cT"))
            for j in range(3):
                for half in range(2):
                    dve.wait_ge(*drained("xT", j, half))
            dve.tensor_tensor(x_sq, xT[:], xT[:], ALU.mult).then_inc(x_squared, 1)
            dve.wait_ge(*own(x_squared))
            dve.wait_ge(*full("ss1"))
            mean_square(rstd[:], bank("ss1")[:, 0:NT], D, "ss1")
            rsqrt(rstd[:])

            def copy_ada(i):
                dve.wait_ge(*full("ada", i))
                if i >= 2:
                    dve.wait_ge(ada_turned, i - 1)
                dve.tensor_copy(ada_rows[i], bank("ada", i)).then_inc(free_sem("ada", i), 1)
                dve.wait_ge(*drained("ada", i))

            def ada_bias(g):
                dve.wait_ge(*full("adaT", g))
                turned = bank("adaT", g).rearrange("p (m r) -> p m r", m=16)[:, :, 0:9]
                dve.tensor_tensor(modT[:, 16 * g:16 * g + 16, :], turned,
                                  over(vecT[:, V_ADA + 16 * g:V_ADA + 16 * g + 16], 2, 9), ALU.add)\
                    .then_inc(free_sem("adaT", g), 1)
                dve.wait_ge(*drained("adaT", g))

            def modulate(which, g_col, shift_m, scale_m, done):
                gain, shift = gainT[:, which], modT[:, shift_m:shift_m + KT, :]
                step(dve.scalar_tensor_tensor(gain, modT[:, scale_m:scale_m + KT, :], 1.0,
                                              over(vecT[:, g_col:g_col + KT], 2, 9), ALU.add, ALU.mult))
                for k in range(KT):
                    dve.scalar_tensor_tensor(hT[:, k, 0:TP], xT[:, k, 0:TP], gain[:, k, 0:1],
                                             rstd[:, 0:TP], ALU.mult, ALU.mult).then_inc(h_scaled, 1)
                samples = hT[:, :, TP:NT].rearrange("p k (b t) -> p k b t", b=NB)
                step(dve.tensor_tensor(hT[:, :, TP:NT], xT[:, :, TP:NT], over(rstd[:, TP:NT], 1, KT),
                                       ALU.mult))
                step(dve.tensor_tensor(samples, samples, over(gain[:, :, 1:9], 3, TD), ALU.mult))
                dve.tensor_tensor(samples, samples, over(shift[:, :, 1:9], 3, TD), ALU.add)\
                    .then_inc(done, 1)
                dve.wait_ge(*own(done))

            for i in range(3):
                copy_ada(i)
            dve.wait_ge(*full("vec"))
            dve.tensor_copy(vecT[:, 0:117], bank("vec")[:, 0:117]).then_inc(free_sem("vec"), 1)
            dve.wait_ge(*drained("vec"))
            dve.wait_ge(table_in, 16 * 7)
            dve.wait_ge(vec_in, 16 * 9)
            for i in range(2):
                step(dve.tensor_tensor(lam_rows[:, 2 * i, :], lam_rows[:, 2 * i, :],
                                       lam_rows[:, 2 * i + 1, :], ALU.mult))
                step(dve.tensor_reduce(LAM[:, i:i + 1], lam_rows[:, 2 * i, :], AX, ALU.add))
            dve.tensor_copy(LAM[:, 0:2], LAM[:, 0:2]).then_inc(lam_dot, 1)
            dve.wait_ge(*own(lam_dot))
            dve.wait_ge(lam_exp, 1)
            step(dve.tensor_tensor(NLAM, LAM[:, 3:4], LAM[:, 2:3], ALU.subtract))
            step(dve.tensor_scalar(NLAM, NLAM, -LAM_INIT, None, ALU.add))
            comp = const("comp")
            step(dve.scalar_tensor_tensor(COEF, comp[:, 1:2], NLAM, comp[:, 0:1], ALU.mult, ALU.add))
            step(dve.tensor_scalar(GS, vecT[:, V_GS:V_GS + 1], 1.0 - LAM_INIT, None, ALU.mult))

            copy_ada(3)
            ada_bias(0)
            modulate(0, V_G1, 0, 8, h_ready)

            cos = const("cos").rearrange("p (j c) -> p j c", j=3)
            sin = const("sin").rearrange("p (j c) -> p j c", j=3)
            flat = pairs.rearrange("p a b -> p (a b)")
            for w in "qk":
                for j, (t0, n) in enumerate(TILES):
                    dve.wait_ge(*full(w, j))
                    z = bank(w, j)[0:n, :].rearrange("p (g s c) -> p g s c", g=8, s=2)
                    tc_ = flat[0:n, 0:512].rearrange("p (g s c) -> p g s c", g=8, s=2)
                    ts_ = flat[0:n, 512:1024].rearrange("p (g s c) -> p g s c", g=8, s=2)
                    cj = over(over(cos[0:n, j, :], 1, 2), 1, 8)
                    sj = over(over(sin[0:n, j, :], 1, 2), 1, 8)
                    dve.tensor_tensor(tc_, z, cj, ALU.mult)
                    dve.tensor_tensor(ts_, z, sj, ALU.mult).then_inc(free_sem(w, j), 1)
                    dve.wait_ge(*drained(w, j))
                    if w == "q" and j == 2:
                        dve.wait_ge(*full("qT", 0))
                    dst = (q_rot[0:n, j % 2, :] if w == "q" else k_rot[0:n, j, :])\
                        .rearrange("p (g s c) -> p g s c", g=8, s=2)
                    dve.tensor_tensor(dst[:, :, 0, :], tc_[:, :, 0, :], ts_[:, :, 1, :], ALU.subtract)
                    dve.tensor_tensor(dst[:, :, 1, :], tc_[:, :, 1, :], ts_[:, :, 0, :], ALU.add)\
                        .then_inc(rotated, 1)
                    dve.wait_ge(*own(rotated))
            step(dve.memset(q_blocks, 0.0))
            dve.wait_ge(*drained("qT", 2))
            qb_v = q_blocks.rearrange("p b (h c) -> p b h c", h=H)
            for h in range(H):
                for c in range(2):
                    rows = slice(DK * c, DK * c + DK)
                    last = dve.tensor_copy(qb_v[rows, :, h, 8 * c:8 * c + 8],
                                           qT[rows, h, TP:NT].rearrange("p (b t) -> p b t", b=NB))
            last.then_inc(q_blocked, 1)
            dve.wait_ge(*own(q_blocked))

            items = [(h, qb) for h in range(H) for qb in range(2)]
            am = const("attmask")

            def att_mask_max(i):
                h, qb = items[i]
                n = P * (qb + 1)
                if i >= 2:
                    dve.wait_ge(*full("aT", i - 2))
                for c in range(2):
                    dve.wait_ge(*full("S", i, c))
                    dve.tensor_tensor(s_pair[:, i % 2, c, 0:n], bank("S", i, c)[:, 0:n], am[:, 256 - n:256],
                                      ALU.add).then_inc(free_sem("S", i, c), 1)
                    dve.wait_ge(*drained("S", i, c))
                mx = MX[:, 2 * (i % 2):2 * (i % 2) + 2]
                step(dve.tensor_reduce(mx, s_pair[:, i % 2, :, 0:n], AX, ALU.max))
                dve.tensor_scalar(mx, mx, -DK ** -0.5, None, ALU.mult).then_inc(att_max, 1)
                dve.wait_ge(*own(att_max))

            att_mask_max(0)
            for i, (h, qb) in enumerate(items):
                if i + 1 < len(items):
                    att_mask_max(i + 1)
                n = P * (qb + 1)
                dve.wait_ge(att_exp, 2 * i + 2)
                rc = RC[:, 2 * (i % 2):2 * (i % 2) + 2]
                step(dve.reciprocal(rc, LS[:, 2 * (i % 2):2 * (i % 2) + 2]))
                step(dve.tensor_tensor(rc[:, 1:2], rc[:, 1:2], NLAM, ALU.mult))
                step(dve.tensor_scalar(s_pair[:, i % 2, 0, 0:n], s_pair[:, i % 2, 0, 0:n], rc[:, 0:1], None,
                                       ALU.mult))
                dve.scalar_tensor_tensor(s_pair[:, i % 2, 0, 0:n], s_pair[:, i % 2, 1, 0:n], rc[:, 1:2],
                                         s_pair[:, i % 2, 0, 0:n], ALU.mult, ALU.add).then_inc(att_a, 1)
                dve.wait_ge(*own(att_a))

            nm = const("newmask").rearrange("p (b k) -> p b k", b=NB)
            last_key = PAGES * PAGE

            def key_pages(b):
                if b:
                    dve.wait_ge(*full("Sn", b - 1))
                for g in KEY_PAGES["dve"]:
                    dve.wait_ge(*full("kTb", b, g))
                    dve.tensor_copy(kTb[:, :, PAGE * g:PAGE * g + PAGE],
                                    bank("kTb", b, g).rearrange("p (h k) -> p h k", h=H))\
                        .then_inc(free_sem("kTb", b, g), 1)
                    dve.wait_ge(*drained("kTb", b, g))

            def dec_row_max(b):
                dve.wait_ge(*full("Sn", b))
                step(dve.tensor_reduce(SC[:, 0:1], psum[:, 4:6, :], mybir.AxisListType.XY, ALU.max))
                dve.tensor_tensor(s_new, bank("Sn", b)[:, 0:TS], nm[:, b, :], ALU.add)\
                    .then_inc(free_sem("Sn", b), 1)
                dve.wait_ge(*drained("Sn", b))
                step(dve.tensor_reduce(SC[:, 1:2], s_new, AX, ALU.max))
                step(dve.tensor_tensor(SC[:, 0:1], SC[:, 0:1], SC[:, 1:2], ALU.max))
                dve.tensor_scalar(SC[:, 2:3], SC[:, 0:1], -DK ** -0.5, None, ALU.mult).then_inc(dec_max, 1)
                dve.wait_ge(*own(dec_max))

            key_pages(0)
            dec_row_max(0)
            key_pages(1)
            for b in range(NB):
                dve.wait_ge(dec_exp, b + 1)
                step(dve.tensor_reduce(SC[:, 6:7], SC[:, 3:6], AX, ALU.add))
                step(dve.reciprocal(SC[:, 6:7], SC[:, 6:7]))
                step(dve.tensor_tensor(SC[:, 6:7], SC[:, 6:7], COEF, ALU.mult))
                if b:
                    dve.wait_ge(*full("od", b - 1))
                dve.wait_ge(*full("pT", b, 0))
                dve.tensor_copy(pT_dec[:, 0:4, :], bank("pT", b, 0).rearrange("p (g c) -> p g c", g=4))\
                    .then_inc(free_sem("pT", b, 0), 1)
                dve.wait_ge(*drained("pT", b, 0))
                if b + 1 < NB:
                    dec_row_max(b + 1)
                dve.wait_ge(*full("od", b))
                if b:
                    dve.wait_ge(*full("odT", b - 1))
                dve.tensor_scalar(o_rows, bank("od", b)[:, 0:P], SC[:, 6:7], None, ALU.mult)\
                    .then_inc(free_sem("od", b), 1)
                dve.wait_ge(*drained("od", b))
                if b + 2 < NB:
                    key_pages(b + 2)
                dve.wait_ge(*full("odT", b))
                turned = bank("odT", b)[:, 0:P].rearrange("p (h z) -> p h z", h=H)[:, :, 0:2 * TD]
                dve.tensor_reduce(oT[:, :, TP + TD * b:TP + TD * b + TD],
                                  turned.rearrange("p h (c q) -> p h q c", c=2), AX, ALU.add)\
                    .then_inc(free_sem("odT", b), 1)
                dve.wait_ge(*drained("odT", b))
            dve.wait_ge(*drained("PV", len(items) - 1))
            dve.wait_ge(k_stored, 96)
            dve.tensor_tensor(o_sq, oT[:], oT[:], ALU.mult).then_inc(o_squared, 1)
            dve.wait_ge(*own(o_squared))
            for h in range(H):
                dve.wait_ge(*full("oss", h))
                mean_square(o_rms[:, h, :], bank("oss", h)[:, 0:NT], P, "oss", h)
            rsqrt(o_rms)
            dve.scalar_tensor_tensor(oT[:], oT[:], GS, o_rms, ALU.mult, ALU.mult).then_inc(o_ready, 1)
            dve.wait_ge(*own(o_ready))
            step(dve.memset(raw_p[:, :, 0:3], 0.0))
            dve.memset(nT, 0.0).then_inc(region_m, 1)
            dve.wait_ge(*own(region_m))

            dve.wait_ge(mrows_in, 48)
            dve.wait_ge(*full("gi"))
            dve.tensor_scalar(rows_li[0:H, :], bank("gi")[0:H, 0:NT], BG[:, 0:1], None, ALU.add)\
                .then_inc(free_sem("gi"), 1)
            dve.wait_ge(*drained("gi"))
            dve.wait_ge(*full("gf"))
            dve.tensor_scalar(rows_f[0:H, :], bank("gf")[0:H, 0:NT], BG[:, 1:2], None, ALU.add)\
                .then_inc(free_sem("gf"), 1)
            dve.wait_ge(*drained("gf"))
            dve.wait_ge(*drained("gi"))
            dve.wait_ge(*drained("gf"))
            dve.scalar_tensor_tensor(rows_t[0:H, :], rows_f[0:H, :], -1.0, rows_f[0:H, :], ALU.mult,
                                     ALU.max).then_inc(f_abs, 1)
            dve.wait_ge(*own(f_abs))
            dve.wait_ge(*full("cs"))
            step(dve.tensor_copy(n0T, bank("cs")[:, 192:224]))
            dve.tensor_copy(raw_s[:, :, :, 0:3],
                            bank("cs")[:, 0:192].rearrange("p (m b j) -> p m b j", m=8, b=NB))\
                .then_inc(free_sem("cs"), 1)
            dve.wait_ge(*drained("cs"))

            def conv(m0):
                for m in range(m0, m0 + 4):
                    dve.wait_ge(*drained("qm" if m < 4 else "km", m % 4))
                    cp, cs_ = cv[:, m, 0:TP], cv[:, m, TP:NT].rearrange("p (b t) -> p b t", b=NB)
                    for tap in range(4):
                        w = vecT[:, V_WC + 8 * tap + m:V_WC + 8 * tap + m + 1]
                        sp_, ss_ = raw_p[:, m, tap:tap + TP], raw_s[:, m, :, tap:tap + TD]
                        if tap == 0:
                            bias = vecT[:, V_BC + m:V_BC + m + 1]
                            dve.tensor_scalar(cp, sp_, w, bias, ALU.mult, ALU.add)
                            step(dve.tensor_scalar(cs_, ss_, w, bias, ALU.mult, ALU.add))
                        else:
                            dve.scalar_tensor_tensor(cp, sp_, w, cp, ALU.mult, ALU.add)
                            last = dve.scalar_tensor_tensor(cs_, ss_, w, cs_, ALU.mult, ALU.add)
                            if m < m0 + 3 or tap < 3:
                                step(last)
                last.then_inc(conv_done, 1)
                dve.wait_ge(*own(conv_done))

            conv(0)
            dve.wait_ge(f_ln, 1)
            F, u, M_, up = rows_f[0:H, :], rows_u[0:H, :], rows_w[0:H, :], rows_t[0:H, :]
            step(dve.scalar_tensor_tensor(up, F, 0.0, up, ALU.min, ALU.subtract))
            step(dve.tensor_tensor_scan(F, const("carry", H), up, 0.0, ALU.mult, ALU.add))
            step(dve.tensor_tensor(u, rows_li[0:H, :], F, ALU.subtract))
            step(dve.tensor_copy(up, u))
            step(dve.tensor_tensor(up[:, 0:1], up[:, 0:1], M0[:, 0:1], ALU.max))
            step(dve.tensor_tensor(up[:, TP:NT:TD], up[:, TP:NT:TD], M0[:, 1:9], ALU.max))
            step(dve.tensor_tensor_scan(M_, const("drop", H), up, 0.0, ALU.add, ALU.max))
            negM = rowsR[0:H, 0:NT]
            step(dve.tensor_tensor(up, F, M_, ALU.add))
            step(dve.tensor_scalar(negM, M_, -1.0, None, ALU.mult))
            nms = negM[:, TP:NT].rearrange("p (b t) -> p b t", b=NB)
            step(dve.tensor_tensor(rowsR[0:H, 2 * NT:2 * NT + TS].rearrange("p (b t) -> p b t", b=NB), nms,
                                   over(M0[:, 1:9], 2, TD), ALU.add))
            step(dve.tensor_scalar(rows_w[0:H, 0:TP], u[:, 0:TP], negM[:, TP - 1:TP], None, ALU.add))
            dve.tensor_tensor(rows_w[0:H, TP:NT].rearrange("p (b t) -> p b t", b=NB),
                              u[:, TP:NT].rearrange("p (b t) -> p b t", b=NB),
                              over(nms[:, :, TD - 1], 2, TD), ALU.add).then_inc(m_rows, 1)
            dve.wait_ge(*own(m_rows))
            conv(4)
            dve.wait_ge(conv_sig, 1)
            dve.tensor_tensor(cv[:, 0:4, :], cv[:, 0:4, :], cv_sig, ALU.mult).then_inc(conv_ready, 1)
            dve.wait_ge(*own(conv_ready))
            step(dve.tensor_copy(tail[:, :, 0:3], raw_p[:, :, TP:TP + 3]))
            dve.tensor_copy(tail[:, :, 3:27].rearrange("p m (b j) -> p m b j", b=NB),
                            raw_s[:, :, :, 8:11]).then_inc(tail_ready, 1)
            dve.wait_ge(*own(tail_ready))
            dve.wait_ge(conv_sig, 2)
            dve.scalar_tensor_tensor(cv[:, 4:8, :], cv[:, 4:8, :], P ** -0.5, cv_sig, ALU.mult, ALU.mult)\
                .then_inc(conv_ready, 1)
            dve.wait_ge(*own(conv_ready))
            dve.wait_ge(*full("uw"))
            step(dve.tensor_copy(uw[:, 0:2, :], bank("uw")[:, 0:16].rearrange("p (j c) -> p j c", j=2)))
            dve.tensor_copy(uw[0:TS, 2, :], bank("uw")[0:TS, 16:24]).then_inc(free_sem("uw"), 1)
            dve.wait_ge(*drained("uw"))
            ada_bias(1)
            ada_bias(2)
            dve.wait_ge(conv_ready, 2)
            for j in range(3):
                dve.wait_ge(*drained("vm", j))
            dve.wait_ge(om_sig, 1)
            causal = const("causal")
            blkind = const("blkind", TS)
            dve.wait_ge(*landed(("C", 0)))
            c0 = unit(("C", 0), 32)
            for h in range(H):
                dve.wait_ge(*full("bc0", h))
                if h:
                    dve.wait_ge(*full("hss", h - 1))
                bc = bank("bc0", h)
                dve.tensor_scalar(dT[:, 0:256], bc[:, 0:256], uw[:, 0, h:h + 1], 0.0, ALU.add, ALU.min)
                dve.tensor_scalar(dT[:, 256:384], bc[:, P:TP], uw[:, 1, h:h + 1], 0.0, ALU.add, ALU.min)
                dve.tensor_scalar(dT[0:TS, 384:448], bc[0:TS, TP:NT], uw[0:TS, 2, h:h + 1], 0.0, ALU.add,
                                  ALU.min).then_inc(free_sem("bc0", h), 1)
                dve.wait_ge(*drained("bc0", h))
                dve.wait_ge(*full("kt", h))
                for j, (t0, n) in enumerate(TILES):
                    last = dve.tensor_scalar(kw[0:n, j, :], bank("kt", h)[0:n, P * j:P * j + P],
                                             uw[0:n, j, 4 + h:5 + h], None, ALU.mult)
                last.then_inc(free_sem("kt", h), 1)
                dve.wait_ge(*drained("kt", h))
                dve.tensor_tensor(v_blk[0:TS], over(vm[0:TS, 2, P * h:P * h + P], 1, NB),
                                  over(blkind, 2, P), ALU.mult).then_inc(kw_ready, 1)
                dve.wait_ge(*own(kw_ready))
                dve.wait_ge(*drained("bc1", h))
                ei = bcS[:, NT:NT + TS]
                step(dve.tensor_tensor(qe[:, 0, :], cv[:, h, TP:NT], ei, ALU.mult))
                n0 = n0T.rearrange("p (b h) -> p b h", b=NB)[:, :, h]
                dve.tensor_tensor(qe[:, 1, :].rearrange("p (b t) -> p b t", b=NB),
                                  qe[:, 0, :].rearrange("p (b t) -> p b t", b=NB),
                                  over(n0, 2, TD), ALU.mult).then_inc(qe_ready, 1)
                dve.wait_ge(*own(qe_ready))
                dve.wait_ge(d_exp, h + 1)
                step(dve.tensor_tensor(dT[:, 0:384], dT[:, 0:384], causal[:, 0:384], ALU.mult))
                step(dve.tensor_tensor(dT[0:TS, 384:448], dT[0:TS, 384:448], causal[0:TS, 384:448],
                                       ALU.mult))
                dve.wait_ge(*full("st", h))
                dve.tensor_tensor(dT[:, 0:384], dT[:, 0:384], bank("st", h)[:, 0:384], ALU.mult)\
                    .then_inc(p_ready, 1)
                dve.wait_ge(*own(p_ready))
                dve.tensor_tensor(dT[0:TS, 384:448], dT[0:TS, 384:448], bank("st", h)[0:TS, 384:448],
                                  ALU.mult).then_inc(free_sem("st", h), 1)
                dve.wait_ge(*drained("st", h))
                dve.wait_ge(*full("C", h))
                dec = ei.rearrange("p (b t) -> p b t", b=NB)[:, :, TD - 1]
                step(dve.tensor_copy(C_p[:, h, :], bank("C", h)[:, 0:P]))
                step(dve.tensor_copy(nT[:, h:h + 1], bank("C", h)[:, P:P + 1]))
                nTs = nT[:, 4:36].rearrange("p (b h) -> p b h", b=NB)[:, :, h]
                step(dve.tensor_tensor(nTs, n0, dec, ALU.mult))
                dve.tensor_tensor(nTs, nTs, bank("C", h)[:, 130:138], ALU.add).then_inc(free_sem("C", h), 1)
                dve.wait_ge(*drained("C", h))
                dve.wait_ge(*full("num", h))
                dve.wait_ge(*full("den", h))
                step(dve.tensor_tensor(den_s, bank("den", h)[:, 0:NT], bcS[:, 0:NT], ALU.max))
                dve.scalar_tensor_tensor(den_s, bank("den", h)[:, 0:NT], -1.0, den_s, ALU.mult,
                                         ALU.max).then_inc(free_sem("den", h), 1)
                dve.wait_ge(*drained("den", h))
                step(dve.reciprocal(den_s, den_s))
                dve.tensor_tensor(hr[:, h, :], bank("num", h)[:, 0:NT], den_s, ALU.mult)\
                    .then_inc(free_sem("num", h), 1)
                dve.wait_ge(*drained("num", h))
                dve.tensor_tensor(hsq, hr[:, h, :], hr[:, h, :], ALU.mult).then_inc(h_squared, 1)
                dve.wait_ge(*own(h_squared))
                ch = c0.rearrange("p (b h) e -> p b h e", b=NB)[:, :, h, :]
                step(dve.tensor_tensor(ch, ch, over(dec, 2, P), ALU.mult))
                for half in range(2):
                    dve.wait_ge(*full("Cs", h, half))
                    dve.tensor_tensor(ch[:, 4 * half:4 * half + 4, :], ch[:, 4 * half:4 * half + 4, :],
                                      bank("Cs", h, half).rearrange("p (b e) -> p b e", b=4), ALU.add)\
                        .then_inc(free_sem("Cs", h, half), 1)
                    dve.wait_ge(*drained("Cs", h, half))
                dve.wait_ge(*drained("C", h))
                step(dve.tensor_copy(SC[:, 7:8], den_s[:, 0:1]))
                dve.tensor_copy(SC[:, 7:8], den_s[:, 0:1]).then_inc(c_ready, 1)
                dve.wait_ge(*own(c_ready))
                for m in (2 * h, 2 * h + 1):
                    dve.wait_ge(*full("upa", m))
                    dve.wait_ge(*drained("ga0" if m < 4 else "ga1", m % 4))
                    dve.tensor_tensor(sg[:, m, :], bank("upa", m)[:, 0:NT], sg[:, m, :], ALU.mult)\
                        .then_inc(free_sem("upa", m), 1)
                    dve.wait_ge(*drained("upa", m))
                dve.wait_ge(*full("hss", h))
                mean_square(h_rms[:, h, :], bank("hss", h)[:, 0:NT], P, "hss", h)
            rsqrt(h_rms)
            for h in range(H):
                dve.scalar_tensor_tensor(hr[:, h, :], hr[:, h, :], vecT[:, V_GM + h:V_GM + h + 1],
                                         h_rms[:, h, :], ALU.mult, ALU.mult).then_inc(dve_step, 1)
                steps[0] += 1
            dve.wait_ge(dve_step, steps[0])
            dve.tensor_tensor(hmT[:], hmT[:], hr, ALU.mult).then_inc(hm_ready, 1)
            dve.wait_ge(*own(hm_ready))

            for m in range(KT):
                dve.wait_ge(*full("upb", m))
                dve.wait_ge(*drained("gb0" if m < 4 else "gb1", m % 4))
                dve.tensor_tensor(mT[:, m, :], bank("upb", m)[:, 0:NT], mT[:, m, :], ALU.mult)\
                    .then_inc(free_sem("upb", m), 1)
                dve.wait_ge(*drained("upb", m))
                dve.tensor_tensor(mT[:, m, :], mT[:, m, :], sg[:, m, :], ALU.add).then_inc(merged, 1)
                dve.wait_ge(*own(merged))

            def gated_add(m, src, gate_m, *key):
                gate = modT[:, gate_m + m, :]
                samples = rstd[:, 0:TS].rearrange("p (b t) -> p b t", b=NB)
                step(dve.tensor_tensor(samples, src[:, TP:NT].rearrange("p (b t) -> p b t", b=NB),
                                       over(gate[:, 1:9], 2, TD), ALU.mult))
                dve.tensor_tensor(xT[:, m, TP:NT], xT[:, m, TP:NT], rstd[:, 0:TS], ALU.add)
                last = dve.scalar_tensor_tensor(xT[:, m, 0:TP], src[:, 0:TP], gate[:, 0:1], xT[:, m, 0:TP],
                                                ALU.mult, ALU.add)
                last.then_inc(free_sem(*key), 1)
                dve.wait_ge(*drained(*key))

            dve.wait_ge(bias_in, 48)
            for m in range(KT):
                dve.wait_ge(*drained("upa", m))
            for rows in (3 * NE, 2 * NE, NE):
                step(dve.tensor_copy(gu_bias[0:rows, :], bias_f32[0:rows, :]))
                if rows > NE:
                    rest = bias_f32[0:rows - NE, :]
                    step(dve.tensor_tensor(rest, rest, gu_bias[0:rows - NE, :], ALU.subtract))

            dve.memset(bd_rows, 0.0).then_inc(bd_cleared, 1)
            dve.wait_ge(*own(bd_cleared))
            for m in range(KT):
                dve.wait_ge(*full("wo", m))
                gated_add(m, bank("wo", m), 16, "wo", m)

            step(dve.memset(wT, 0.0))
            dve.wait_ge(*full("ss2"))
            mean_square(rstd[:], bank("ss2")[:, 0:NT], D, "ss2")
            rsqrt(rstd[:])
            modulate(1, V_G2, 24, 32, h2_ready)

            step(dve.memset(logits, 0.0))
            dve.wait_ge(moe_in, 48)
            dve.wait_ge(*full("logit"))
            lg = bank("logit")[:, 0:96].rearrange("p (j e) -> p j e", j=3)
            step(dve.tensor_tensor(logits[:, 0:2, :], lg[:, 0:2, :], over(b_rt, 1, 2), ALU.add))
            dve.tensor_tensor(logits[0:TS, 2, :], lg[0:TS, 2, :], b_rt[0:TS, :], ALU.add)\
                .then_inc(free_sem("logit"), 1)
            dve.wait_ge(*drained("logit"))
            for j in range(3):
                step(dve.max(top8[:, j, :], logits[:, j, :]))
                step(dve.max_index(top_ix[:, j, :], top8[:, j, :], logits[:, j, :]))
            step(dve.tensor_copy(idxf, top_ix[:]))
            dve.tensor_tensor(ew, top8[:, :, 0:4], top8[:, :, 0:1].to_broadcast([P, 3, 4]), ALU.subtract)\
                .then_inc(top_diff, 1)
            dve.wait_ge(*own(top_diff))
            dve.wait_ge(top_exp, 1)
            step(dve.tensor_reduce(esum, ew, AX, ALU.add))
            step(dve.reciprocal(esum, esum))
            step(dve.tensor_tensor(esum, esum, valid, ALU.mult))
            step(dve.tensor_tensor(ew, ew, over(esum, 2, 4), ALU.mult))
            step(dve.tensor_tensor(hot4, over(over(iota[:, 0:NE], 1, TOPK), 1, 3),
                                   over(idxf[:, :, 0:TOPK], 3, NE), ALU.is_equal))
            step(dve.tensor_tensor(hot4w, hot4, over(ew, 3, NE), ALU.mult))
            step(dve.tensor_reduce(mask, hot4.rearrange("p j s e -> p j e s"), AX, ALU.add))
            step(dve.tensor_reduce(wts, hot4w.rearrange("p j s e -> p j e s"), AX, ALU.add))
            dve.tensor_tensor(mask, mask, over(valid, 2, NE), ALU.mult).then_inc(routed, 1)
            dve.wait_ge(*own(routed))
            dve.wait_ge(*full("pos"))
            dve.wait_ge(*full("wT"))
            dve.tensor_copy(wT[0:NE, :], bank("wT")[0:NE, 0:NT]).then_inc(free_sem("wT"), 1)
            dve.wait_ge(*drained("wT"))
            pp = bank("pos")
            step(dve.scalar_tensor_tensor(eq, pp[:, 0:96].rearrange("p (j e) -> p j e", j=3), 1.0, mask,
                                          ALU.add, ALU.mult))
            rounds = pos.rearrange("p j (r e) -> p j r e", r=ROUNDS)
            step(dve.tensor_tensor(rounds, over(eq, 2, ROUNDS),
                                   over(const("round_start").rearrange("p (r e) -> p r e", r=ROUNDS), 1, 3),
                                   ALU.add))
            dve.tensor_tensor(plan[0:NE, 2:1 + ROUNDS], pp[0:NE, 128:129].to_broadcast([NE, ROUNDS - 1]),
                              const("rounds", NE), ALU.is_gt).then_inc(free_sem("pos"), 1)
            dve.wait_ge(*drained("pos"))
            step(dve.tensor_reduce(plan[0:NE, 1:2], plan[0:NE, 2:1 + ROUNDS], AX, ALU.add))
            dve.tensor_scalar(plan[0:NE, 0:1], plan[0:NE, 1:2], 1.0, None, ALU.add).then_inc(blocks_ready, 1)
            dve.wait_ge(*own(blocks_ready))
            dve.wait_ge(*full("cum"))
            step(dve.tensor_copy(plan[0:NE, 1:2], bank("cum")[0:NE, 0:1]))
            step(dve.tensor_scalar(ints[0:1, AT_LATER:AT_LATER + 1], bank("cum")[0:1, 2 * NE - 1:2 * NE], -1.0,
                                   None, ALU.add))
            dve.tensor_copy(ints[0:1, AT_BLOCKS:AT_BLOCKS + NE], bank("cum")[0:1, NE:2 * NE])\
                .then_inc(free_sem("cum"), 1)
            dve.wait_ge(*drained("cum"))
            dve.tensor_scalar(begun[0:NE, :], iota[0:NE, 0:MAX_BLOCKS + 1], plan[0:NE, 1:2], None,
                              ALU.is_ge).then_inc(begun_ready, 1)
            dve.wait_ge(*own(begun_ready))
            dve.wait_ge(*full("list"))
            ls = bank("list")
            step(dve.tensor_copy(ints[0:1, AT_EXPERT:AT_EXPERT + MAX_BLOCKS + 1], ls[0:1, 0:MAX_BLOCKS + 1]))
            step(dve.tensor_tensor(plan_row[0:1, :], iota[0:1, 0:MAX_BLOCKS + 1],
                                   ls[0:1, 64:64 + MAX_BLOCKS + 1], ALU.subtract))
            dve.scalar_tensor_tensor(ints[0:1, AT_COLUMN:AT_COLUMN + MAX_BLOCKS + 1], plan_row[0:1, :],
                                     float(NE), ls[0:1, 0:MAX_BLOCKS + 1], ALU.mult, ALU.add)\
                .then_inc(free_sem("list"), 1)
            dve.wait_ge(*drained("list"))

            lanes = const("slots")

            def slots(column):
                for j in range(3):
                    last = dve.tensor_scalar(sel[:, j, :], lanes[:, 0:SLOTS], pos[:, j, column], None,
                                             ALU.is_equal)
                last.then_inc(sel_ready, 1)

            def slot_weights(column, expert):
                for j in range(3):
                    last = dve.tensor_scalar(selw[:, j, :], lanes, pos[:, j, column], wts[:, j, expert],
                                             ALU.is_equal, ALU.mult)
                last.then_inc(selw_ready, 1)

            def hot(expert):
                dve.tensor_copy(bias_hot[0:3 * NE, :],
                                const("expert_hot", 3 * NE)[:, expert].to_broadcast([3 * NE, SLOTS]))\
                    .then_inc(bias_hot_ready, 1)

            hot(slice(0, 1))
            slots(slice(0, 1))
            dve.tensor_copy(plan_row[0:1, 0:1], plan_row[0:1, 1:2]).then_inc(tables, 1)
            dve.wait_ge(*own(tables))
            for m in range(KT):
                dve.wait_ge(*drained("bd", m))

            def add_sums(last_blocks, i):
                dve.wait_ge(combined, 4 * last_blocks + (i - 3))
                acc = accT.rearrange("p (h i) t -> p i h t", h=2)[:, i]
                dve.tensor_tensor(acc, acc, psum[:, B_SUM[i % 2]:B_SUM[i % 2] + 2, 0:NT], ALU.add)\
                    .then_inc(added, 1)

            def expert_block(b, column, expert, next_column, next_expert, first):
                dve.wait_ge(unit_read[1], b + 1)
                if not first:
                    dve.wait_ge(gs_ready, b)
                dve.tensor_scalar(act_g, psum[:, B_GATE, :], LIMIT, None, ALU.min).then_inc(gate_clamped, 1)
                if not first:
                    add_sums(b, 0)
                    add_sums(b, 1)
                dve.wait_ge(gate_sig, b + 1)
                dve.wait_ge(gate_clamped, b + 1)
                if not first:
                    dve.wait_ge(act_ready, b)
                dve.tensor_tensor(act_g, act_g, act_s, ALU.mult).then_inc(gs_ready, 1)
                if not first:
                    add_sums(b, 2)
                    add_sums(b, 3)
                dve.wait_ge(gathered, b + 1)
                slots(next_column)
                if not first:
                    dve.wait_ge(selw_turned, b)
                slot_weights(column, expert)
                dve.wait_ge(unit_read[3], b + 1)
                if not first:
                    dve.wait_ge(act_turned, b)
                dve.tensor_scalar(act_u, psum[:, B_UP, :], LIMIT, -LIMIT, ALU.min, ALU.max)\
                    .then_inc(up_clamped, 1)
                dve.wait_ge(up_clamped, b + 1)
                dve.wait_ge(gs_ready, b + 1)
                dve.scalar_tensor_tensor(act_u, act_u, 1.0, act_g, ALU.add, ALU.mult).then_inc(act_ready, 1)
                hot(next_expert)
                if not first:
                    dve.wait_ge(added, 4 * b)

            expert_block(0, slice(0, 1), slice(0, 1), bass.ds(dve.value_load(
                ints[0:1, AT_COLUMN + 1:AT_COLUMN + 2], min_val=0, max_val=ROUNDS * NE - 1), 1),
                bass.ds(dve.value_load(ints[0:1, AT_EXPERT + 1:AT_EXPERT + 2], min_val=0, max_val=NE), 1), True)
            later = dve.value_load(ints[0:1, AT_LATER:AT_LATER + 1], min_val=NE - 1, max_val=MAX_BLOCKS - 1)
            with dve.Fori(0, later) as p:
                b = p + 1
                column, next_column = [dve.value_load(ints[0:1, bass.ds(b + at, 1)], min_val=0,
                                                      max_val=ROUNDS * NE - 1)
                                       for at in (AT_COLUMN, AT_COLUMN + 1)]
                expert = dve.value_load(ints[0:1, bass.ds(b + AT_EXPERT, 1)], min_val=0, max_val=NE - 1)
                next_expert = dve.value_load(ints[0:1, bass.ds(b + (AT_EXPERT + 1), 1)], min_val=0, max_val=NE)
                expert_block(b, bass.ds(column, 1), bass.ds(expert, 1), bass.ds(next_column, 1),
                             bass.ds(next_expert, 1), False)
            blocks = later + 1
            for i in range(4):
                add_sums(blocks, i)
            dve.wait_ge(added, 4 * blocks)
            steps[0], steps[1] = 0, tail_step
            dve.tensor_copy(plan_row[0:1, 0:1], plan_row[0:1, 1:2]).then_inc(acc_final, 1)
            dve.wait_ge(*own(acc_final))
            for half in range(2):
                ms = slice(4 * half, 4 * half + 4)
                gate = modT[:, 40 + 4 * half:44 + 4 * half, :]
                at = slice(4 * half, 4 * half + 4)
                add = act_g[:, 256 * half:256 * half + 256].rearrange("p (m b t) -> p m b t", m=4, b=NB)
                step(dve.tensor_tensor(add, accT[:, at, TP:NT].rearrange("p m (b t) -> p m b t", b=NB),
                                       over(gate[:, :, 1:9], 3, TD), ALU.mult))
                x_s = xT[:, ms, TP:NT]
                dve.tensor_tensor(x_s, x_s, add.rearrange("p m b t -> p m (b t)"), ALU.add)
                for i in range(4):
                    m = 4 * half + i
                    last = dve.scalar_tensor_tensor(xT[:, m, 0:TP], accT[:, m, 0:TP], gate[:, i, 0:1],
                                                    xT[:, m, 0:TP], ALU.mult, ALU.add)
                last.then_inc(x2_ready, 1)
                dve.wait_ge(*own(x2_ready))
            step(dve.memset(fin_ss, 1.0))
            dve.tensor_copy(fin_ss[:, 0:1], fin_ss[:, 1:2]).then_inc(fin_ss_set, 1)
            dve.wait_ge(x2_squared, 6)
            fin = fin_ss.rearrange("p (j h) -> p j h", j=3)
            step(dve.tensor_tensor(fin_rstd, fin[:, :, 0], fin[:, :, 1], ALU.add))
            step(dve.tensor_scalar(fin_rstd, fin_rstd, 1.0 / D, EPS, ALU.mult, ALU.add))
            rsqrt(fin_rstd)
            dve.wait_ge(gain_in, 16)
            for j, (t0, n) in enumerate(TILES):
                for half in range(2):
                    cols = slice(512 * half, 512 * half + 512)
                    dve.scalar_tensor_tensor(y_out[0:n, j, cols], bank("y", j, half)[0:n, :],
                                             fin_rstd[0:n, j:j + 1], fin_gain[0:n, cols], ALU.mult, ALU.mult)\
                        .then_inc(free_sem("y", j, half), 1)
                    dve.wait_ge(*drained("y", j, half))

        @block.scalar
        def _(act):
            def copy(out, src):
                return act.activation(out, src, ACT.Copy)

            norms = [0]

            def root(t):
                norms[0] += 1
                act.wait_ge(mean_inverse, norms[0])
                act.activation(t, t, ACT.Sqrt).then_inc(mean_root, 1)

            act.wait_ge(c_in, 32)
            act.activation(c_sig[0:9, :], c_rows[0:9, :], ACT.Sigmoid).then_inc(c_sig_done, 1)
            act.wait_ge(*own(c_sig_done))
            for j, (t0, n) in enumerate(TILES):
                for half in range(2):
                    act.wait_ge(*full("xT", j, half))
                    src = bank("xT", j, half).rearrange("p (k t) -> p k t", k=4)[:, :, 0:n]
                    copy(xT[:, 4 * half:4 * half + 4, t0:t0 + n], src).then_inc(free_sem("xT", j, half), 1)
                    act.wait_ge(*drained("xT", j, half))
            root(rstd[:])
            act.wait_ge(lam_dot, 1)
            act.activation(LAM[:, 2:4], LAM[:, 0:2], ACT.Exp).then_inc(lam_exp, 1)
            act.wait_ge(*own(lam_exp))

            def shift_prompt(which, shift_m):
                for k in range(KT):
                    act.wait_ge(h_scaled, KT * which + k + 1)
                    act.activation(hT[:, k, 0:TP], hT[:, k, 0:TP], ACT.Identity,
                                   bias=modT[:, shift_m + k, 0:1]).then_inc(h_shifted, 1)

            shift_prompt(0, 0)

            def heads_T(name, j):
                t0, n = TILES[j]
                act.wait_ge(*full(name + "T", j))
                src = bank(name + "T", j).rearrange("p (h t) -> p h t", h=H)[:, :, 0:n]
                copy((qT if name == "q" else kT)[:, :, t0:t0 + n], src).then_inc(free_sem(name + "T", j), 1)
                act.wait_ge(*drained(name + "T", j))

            for j in range(3):
                heads_T("q", j)
            for j, (t0, n) in enumerate(TILES):
                act.wait_ge(*full("v", j))
                copy(va[0:n, j, :], bank("v", j)[0:n, :]).then_inc(free_sem("v", j), 1)
                act.wait_ge(*drained("v", j))
                heads_T("k", j)

            items = [(h, qb) for h in range(H) for qb in range(2)]

            def exps(i):
                n = P * (items[i][1] + 1)
                act.wait_ge(att_max, i + 1)
                for c in range(2):
                    col = 2 * (i % 2) + c
                    act.activation(s_pair[:, i % 2, c, 0:n], s_pair[:, i % 2, c, 0:n], ACT.Exp,
                                   bias=MX[:, col:col + 1], scale=DK ** -0.5,
                                   accum_out=LS[:, col:col + 1]).then_inc(att_exp, 1)
                    act.wait_ge(*own(att_exp))

            def att_output(i):
                h, qb = items[i]
                act.wait_ge(*full("PV", i))
                copy(oT[:, h, P * qb:P * qb + P], bank("PV", i)[:, 0:P]).then_inc(free_sem("PV", i), 1)
                act.wait_ge(*drained("PV", i))

            exps(0)
            for i, (h, qb) in enumerate(items):
                if i + 1 < len(items):
                    exps(i + 1)
                act.wait_ge(*full("aT", i))
                if i >= 2:
                    act.wait_ge(*full("PV", i - 2))
                n = P * (qb + 1)
                copy(aT[:, i % 2, 0:n], bank("aT", i)[:, 0:n]).then_inc(free_sem("aT", i), 1)
                act.wait_ge(*drained("aT", i))
                if i:
                    att_output(i - 1)
                if i % 2:
                    m = i // 2
                    act.wait_ge(*full("om", m))
                    if m == 0:
                        act.wait_ge(*full("adaT", 0))
                    copy(hmT[:, m, :], bank("om", m)[:, 0:NT]).then_inc(free_sem("om", m), 1)
                    act.wait_ge(*drained("om", m))
            att_output(len(items) - 1)

            def key_pages(b, pages=KEY_PAGES["act"]):
                if b:
                    act.wait_ge(*full("Sn", b - 1))
                for g in pages:
                    act.wait_ge(*full("kTb", b, g))
                    copy(kTb[:, :, PAGE * g:PAGE * g + PAGE],
                         bank("kTb", b, g).rearrange("p (h k) -> p h k", h=H))\
                        .then_inc(free_sem("kTb", b, g), 1)
                    act.wait_ge(*drained("kTb", b, g))

            nk = PAGES * PAGE

            def dec_exps(b):
                act.wait_ge(dec_max, b + 1)
                if b:
                    act.wait_ge(*full("pTn", b - 1))
                for half in range(2):
                    act.activation(p_dec[:, 512 * half:512 * half + 512], bank("Sd", b, half),
                                   ACT.Exp, bias=SC[:, 2:3], scale=DK ** -0.5,
                                   accum_out=SC[:, 3 + half:4 + half])\
                        .then_inc(free_sem("Sd", b, half), 1)
                    act.wait_ge(*drained("Sd", b, half))
                act.activation(p_dec[:, nk:nk + TS], s_new, ACT.Exp, bias=SC[:, 2:3],
                               scale=DK ** -0.5, accum_out=SC[:, 5:6]).then_inc(dec_exp, 1)
                act.wait_ge(*own(dec_exp))

            key_pages(0)
            dec_exps(0)
            key_pages(1)
            for b in range(NB):
                if b:
                    act.wait_ge(*full("od", b - 1))
                act.wait_ge(*full("pT", b, 1))
                copy(pT_dec[:, 4:8, :], bank("pT", b, 1).rearrange("p (g c) -> p g c", g=4))\
                    .then_inc(free_sem("pT", b, 1), 1)
                act.wait_ge(*drained("pT", b, 1))
                act.wait_ge(*full("pTn", b))
                copy(pTn[0:TS, :], bank("pTn", b)[0:TS, 0:P]).then_inc(free_sem("pTn", b), 1)
                act.wait_ge(*drained("pTn", b))
                if b + 2 < NB:
                    key_pages(b + 2, KEY_PAGES["act"][:2])
                if b + 1 < NB:
                    dec_exps(b + 1)
                if b + 2 < NB:
                    key_pages(b + 2, KEY_PAGES["act"][2:])

            root(o_rms)

            def copy_ada(i):
                act.wait_ge(*full("ada", i))
                if i >= 10:
                    act.wait_ge(*full("adaT", 1))
                copy(ada_rows[i], bank("ada", i)).then_inc(free_sem("ada", i), 1)
                act.wait_ge(*drained("ada", i))

            act.wait_ge(region_m, 1)

            def raw_inputs(i, key):
                for m in range(4):
                    act.wait_ge(*full(key, m))
                    copy(raw_p[:, 4 * i + m, 3:TP + 3], bank(key, m)[:, 0:TP])
                    copy(raw_s[:, 4 * i + m, :, 3:11],
                         bank(key, m)[:, TP:NT].rearrange("p (b t) -> p b t", b=NB))\
                        .then_inc(free_sem(key, m), 1)
                    act.wait_ge(*drained(key, m))

            raw_inputs(0, "qm")
            act.wait_ge(f_abs, 1)
            act.activation(rows_t[0:H, :], rows_t[0:H, :], ACT.Exp, scale=-1.0).then_inc(act_step, 1)
            act.wait_ge(act_step, 1)
            act.activation(rows_t[0:H, :], rows_t[0:H, :], ACT.Ln, bias=1.0).then_inc(f_ln, 1)
            act.wait_ge(*own(f_ln))
            for i in range(4, 6):
                copy_ada(i)
            raw_inputs(1, "km")
            for i in range(6, 8):
                copy_ada(i)
            act.wait_ge(conv_done, 1)
            act.activation(cv_sig, cv[:, 0:4, :], ACT.Sigmoid).then_inc(conv_sig, 1)
            act.wait_ge(*own(conv_sig))
            act.wait_ge(conv_done, 2)
            act.wait_ge(conv_ready, 1)
            act.activation(cv_sig, cv[:, 4:8, :], ACT.Sigmoid).then_inc(conv_sig, 1)
            act.wait_ge(*own(conv_sig))
            act.activation(hmT[:], hmT[:], ACT.Sigmoid).then_inc(om_sig, 1)
            act.wait_ge(*own(om_sig))
            for j, (t0, n) in enumerate(TILES):
                act.wait_ge(*full("vm", j))
                copy(vm[0:n, j, :], bank("vm", j)[0:n, :]).then_inc(free_sem("vm", j), 1)
                act.wait_ge(*drained("vm", j))
            for i in range(8, 12):
                copy_ada(i)
            act.wait_ge(tail_ready, 1)
            for half in range(2):
                act.wait_ge(*full("tail", half))
                copy(tail_rows[0:27, 512 * half:512 * half + 512], bank("tail", half)[0:27, :])\
                    .then_inc(free_sem("tail", half), 1)
                act.wait_ge(*drained("tail", half))
            act.wait_ge(m_rows, 1)
            act.activation(rowsR[0:H, NT:2 * NT], rows_t[0:H, :], ACT.Exp, scale=-1.0).then_inc(m_exp, 1)
            act.wait_ge(*own(m_exp))
            act.activation(rowsR[0:H, 2 * NT:2 * NT + TS], rowsR[0:H, 2 * NT:2 * NT + TS], ACT.Exp)\
                .then_inc(m_exp, 1)
            act.wait_ge(*own(m_exp))
            act.activation(rows_w[0:H, :], rows_w[0:H, :], ACT.Exp).then_inc(m_exp, 1)
            act.wait_ge(*own(m_exp))
            for h in range(H):
                act.wait_ge(*full("bc1", h))
                if h:
                    act.wait_ge(c_ready, h)
                copy(bcS, bank("bc1", h)[:, 0:384]).then_inc(free_sem("bc1", h), 1)
                act.wait_ge(*drained("bc1", h))
                act.wait_ge(*drained("bc0", h))
                act.activation(dT[:, 0:384], dT[:, 0:384], ACT.Exp)
                act.activation(dT[0:TS, 384:448], dT[0:TS, 384:448], ACT.Exp).then_inc(d_exp, 1)
                act.wait_ge(*own(d_exp))
                if h == 0:
                    act.wait_ge(conv_ready, 2)
                    act.wait_ge(tail_out, 32)
                w = "ga0" if h < 2 else "ga1"
                for m in (2 * (h % 2), 2 * (h % 2) + 1):
                    act.wait_ge(*full(w, m))
                    act.activation(sg[:, m + 4 * (h // 2), :], bank(w, m)[:, 0:NT], ACT.Sigmoid)\
                        .then_inc(free_sem(w, m), 1)
                    act.wait_ge(*drained(w, m))
            act.wait_ge(*full("n_out"))
            copy(n_rows[0:36, :], bank("n_out")[0:36, 0:P]).then_inc(free_sem("n_out"), 1)
            act.wait_ge(*drained("n_out"))

            root(h_rms)

            act.wait_ge(hm_ready, 1)
            for w in ("gb0", "gb1"):
                for m in range(4):
                    act.wait_ge(*full(w, m))
                    act.activation(mT[:, m + 4 * int(w[2]), :], bank(w, m)[:, 0:NT], ACT.Sigmoid)\
                        .then_inc(free_sem(w, m), 1)
                    act.wait_ge(*drained(w, m))
            for m in range(KT):
                act.wait_ge(*drained("wo", m))
                act.activation(x1_sq[:, m, :], xT[:, m, :], ACT.Square).then_inc(x1_squared, 1)
            root(rstd[:])
            shift_prompt(1, 24)
            act.wait_ge(*full("part_logits"))
            copy(part_logits, bank("part_logits")[:, 0:NT]).then_inc(free_sem("part_logits"), 1)
            act.wait_ge(*drained("part_logits"))
            act.wait_ge(top_diff, 1)
            act.activation(ew, ew, ACT.Exp).then_inc(top_exp, 1)
            act.wait_ge(*own(top_exp))
            for j, (t0, n) in enumerate(TILES):
                for half in range(2):
                    act.wait_ge(*full("h2", j, half))
                    copy(h2_tok[0:n, j, 512 * half:512 * half + 512], bank("h2", j, half)[0:n, :])\
                        .then_inc(free_sem("h2", j, half), 1)
                    act.wait_ge(*drained("h2", j, half))
            for m in range(KT):
                act.wait_ge(*full("bd", m))
                copy(accT[:, m, :], bank("bd", m)[:, 0:NT]).then_inc(free_sem("bd", m), 1)
                act.wait_ge(*drained("bd", m))

            def copy_gathered(b, first):
                act.wait_ge(gathered, b + 1)
                if not first:
                    act.wait_ge(hg_turned, b)
                copy(hg_rows, psum[:, B_HG, :]).then_inc(hg_copied, 1)

            def copy_turned_gathered(b, first):
                act.wait_ge(hg_turned, b + 1)
                if not first:
                    act.wait_ge(unit_read[3], b)
                copy(hgT, psum[:, B_HG_T, :].rearrange("p (k s) -> p k s", k=4)).then_inc(hgT_copied, 1)

            def expert_block(b, first):
                act.wait_ge(gate_clamped, b + 1)
                if not first:
                    act.wait_ge(gs_ready, b)
                act.activation(act_s, act_g, ACT.Sigmoid, scale=ALPHA).then_inc(gate_sig, 1)
                copy_gathered(b + 1, False)
                act.wait_ge(act_turned, b + 1)
                if not first:
                    act.wait_ge(unit_read[5], b)
                copy(actT, psum[:, B_ACT_T, :].rearrange("p (k s) -> p k s", k=4)).then_inc(actT_copied, 1)
                copy_turned_gathered(b + 1, False)
                act.wait_ge(selw_turned, b + 1)
                if not first:
                    act.wait_ge(combined, 4 * b)
                copy(selwT, psum[:, B_SEL_T, 0:NT]).then_inc(selwT_copied, 1)
                act.wait_ge(unit_read[5], b + 1)
                copy(y_rows, psum[:, B_Y, :]).then_inc(y_copied, 1)

            copy_gathered(0, True)
            copy_turned_gathered(0, True)
            expert_block(0, True)
            act.wait_ge(tables, 1)
            later = act.value_load(ints[0:1, AT_LATER:AT_LATER + 1], min_val=NE - 1, max_val=MAX_BLOCKS - 1)
            with act.Fori(0, later) as p:
                expert_block(p + 1, False)
            act.wait_ge(fin_ss_set, 1)
            act.wait_ge(hgT_copied, later + 2)
            for half in range(2):
                for j, (t0, n) in enumerate(TILES):
                    act.wait_ge(*full("y", j, half))
                    if half or j:
                        act.wait_ge(x2_squared, 3 * half + j)
                    act.activation(hg_rows[0:n, :], bank("y", j, half)[0:n, :], ACT.Square,
                                   accum_out=fin_ss[0:n, 2 * j + half:2 * j + half + 1]).then_inc(x2_squared, 1)
            root(fin_rstd)

        @block.gpsimd
        def _(pool):
            c2 = I["c_sample"]
            pool.dma_start(c_rows[0:1, :], I["c_prompt"]).then_inc(c_in, 16)
            pool.dma_start(c_rows[1:9, :], c2).then_inc(c_in, 16)
            row = 0
            for name, n in (("b_ada", 48), ("g_norm1", 8), ("g_norm2", 8), ("g_final", 8), ("w_conv", 32),
                            ("b_conv", 8), ("g_subln", 1), ("g_mnorm", 4)):
                src = I[name].rearrange("a b -> (a b)").rearrange("(r c) -> r c", c=P)
                pool.dma_start(vec_rows[row:row + n, :], src).then_inc(vec_in, 16)
                row += n
            pool.dma_start(front_const, I["const"][:, n_keep:n_const]).then_inc(vec_in, 16)
            for i, name in enumerate(("lambda_q1", "lambda_k1", "lambda_q2", "lambda_k2")):
                pool.dma_start(lam_rows[:, i, :], I[name].to_broadcast([P, DK])).then_inc(table_in, 16)
            with nc.allow_non_contiguous_dma(reason="a few words"):
                pool.dma_start(small[0:H, 21:29], I["state_m"].rearrange("b h -> h b")).then_inc(table_in, 16)
                pool.dma_start(small[0:H, 29:30], I["b_gates"].rearrange("o h -> h o")[0:H])\
                    .then_inc(table_in, 16)
                pool.dma_start(small[0:H, 30:31], I["b_gates"].rearrange("o h -> h o")[H:2 * H])\
                    .then_inc(table_in, 16)
            for w, tile_, name in (("k", k_rot, "k"), ("v", va, "v")):
                for j, (t0, n) in enumerate(TILES):
                    if w == "k":
                        pool.wait_ge(rotated, 4 + j)
                    else:
                        pool.wait_ge(*drained("v", j))
                    dst = O[name + "_prompt"][t0:t0 + n, :] if j < 2 else O[name + "_sample"]
                    pool.dma_start(dst, tile_[0:n, j, :]).then_inc(k_stored, 16)
            pool.wait_ge(page_in, 16)
            for i, (name, n_dma) in enumerate(units):
                if name[0] == "V":
                    pool.wait_ge(*last_use[units[i - RING][0]])
                    load_pages(pool, name)
            pool.wait_ge(region_m, 1)
            pool.wait_ge(k_stored, 96)
            pool.dma_start(cs_rows[0:24, :], I["state_conv"]).then_inc(mrows_in, 16)
            pool.dma_start(n_rows[0:32, :], I["state_n"]).then_inc(mrows_in, 16)
            with nc.allow_non_contiguous_dma(reason="eight gate columns"):
                pool.dma_start(w_if, W_IN.rearrange("(k p) c -> p k c", p=P)[:, :, 3584:3592])\
                    .then_inc(mrows_in, 16)
            for half in range(2):
                pool.wait_ge(*drained("tail", half))
            pool.dma_start(O["conv_prompt"], tail_rows[0:3, :]).then_inc(tail_out, 16)
            pool.dma_start(O["conv_sample"], tail_rows[3:27, :]).then_inc(tail_out, 16)
            pool.wait_ge(m_rows, 1)
            with nc.allow_non_contiguous_dma(reason="a few words"):
                pool.dma_start(O["m_prompt"], rows_t[0:H, TP - 1:TP]).then_inc(state_out, 16)
                pool.dma_start(O["m_sample"].rearrange("b h -> h b"), rows_t[0:H, TP + TD - 1:NT:TD])\
                    .then_inc(state_out, 16)
            pool.wait_ge(c_ready, H)
            pool.dma_start(O["C_prompt"].rearrange("h d e -> d h e"), C_p).then_inc(state_out, 16)
            pool.dma_start(O["C_sample"].rearrange("b h d e -> d (b h) e"), unit(("C", 0), 32))\
                .then_inc(state_out, 16)
            pool.wait_ge(*drained("n_out"))
            pool.dma_start(O["n_prompt"], n_rows[0:4, :]).then_inc(state_out, 16)
            pool.dma_start(O["n_sample"], n_rows[4:36, :]).then_inc(state_out, 16)
            pool.wait_ge(state_out, 96)
            pool.wait_ge(hm_ready, 1)
            for part in range(3):
                pool.dma_start(bias_f32[NE * part:NE * part + NE, :], I["b_gu"]).then_inc(bias_in, 16)
            pool.dma_start(w_rt, I["w_router"].rearrange("(k p) e -> p k e", p=P)).then_inc(moe_in, 16)
            pool.dma_start(b_rt, I["b_router"].to_broadcast([P, NE])).then_inc(moe_in, 16)
            pool.wait_ge(bd_cleared, 1)
            pool.dma_start(bd_rows[0:NE, :], I["b_down"]).then_inc(moe_in, 16)
            pool.dma_start(fin_gain, I["g_final"].to_broadcast([P, D])).then_inc(gain_in, 16)
            for j, (t0, n) in enumerate(TILES):
                for half in range(2):
                    pool.wait_ge(*drained("y", j, half))
                dst = O["y_prompt"][t0:t0 + n, :] if j < 2 else O["y_sample"]
                pool.dma_start(dst, y_out[0:n, j, :]).then_inc(y_stored, 16)
            pool.wait_ge(y_stored, 48)

        @block.sync
        def _(sp):
            sp.dma_start(ints[0:1, 0:64], I["page_table"]).then_inc(page_in, 16)
            sp.dma_start(keep[:], I["const"][:, 0:n_keep]).then_inc(const_in, 16)
            x = I["x_prompt"]
            for j in range(2):
                sp.dma_start(x_tok[:, j, :], x[P * j:P * j + P, :]).then_inc(x_in, 16)
            sp.dma_start(x_tok[0:TS, 2, :], I["x_sample"]).then_inc(x_in, 16)
            sp.wait_ge(page_in, 16)
            for i, (name, n_dma) in enumerate(units):
                if i == 0:
                    sp.wait_ge(c_in, 32)
                if i == 4:
                    sp.wait_ge(vec_in, 16 * 9)
                    sp.wait_ge(table_in, 16 * 7)
                if name[0] == "V":
                    continue
                if i >= RING:
                    freed = units[i - RING][0]
                    if freed == ("C", 0):
                        sp.wait_ge(state_out, 96)
                    else:
                        sp.wait_ge(*last_use[freed])
                s = slot_of[name]
                if name[0] == "K":
                    load_pages(sp, name)
                else:
                    src, a = unit_source(name)
                    sp.dma_start(unit(name, a), src).then_inc(unit_landed[s], 16)

            gu = I["w_gu"].rearrange("e (k p) f -> e p k f", p=P)
            dn = I["w_down"].rearrange("e (k p) f -> e p k f", p=P)

            def expert_weights(expert, blocks_before):
                for i in range(RING):
                    if blocks_before is None:
                        sp.wait_ge(*last_use[units[len(units) - RING + i][0]])
                    else:
                        sp.wait_ge(unit_read[i], blocks_before)
                    q, half = i // 2, i % 2
                    w, f = (gu, FF * q) if q < 2 else (dn, 0)
                    src = w[expert, :, 4 * half:4 * half + 4, f:f + FF].rearrange("o p k f -> p (o k) f")
                    dst = ring[:, moe_slot[i], :].rearrange("p (k f) -> p k f", k=4)
                    sp.dma_start(dst, src).then_inc(unit_landed[moe_slot[i]], 16)

            expert_weights(slice(0, 1), None)
            sp.wait_ge(tables, 1)
            with sp.Fori(1, NE) as e:
                before = sp.value_load(ints[0:1, bass.ds(e + (AT_BLOCKS - 1), 1)], min_val=1,
                                       max_val=MAX_BLOCKS)
                expert_weights(bass.ds(e, 1), before)


_OUTS = [
    ("y_prompt", (TP, D), (1, TP, D)), ("y_sample", (TS, D), (NB, TD, D)),
    ("k_prompt", (TP, 512), (1, 1, TP, H, 2, DK)), ("v_prompt", (TP, 512), (1, 1, TP, H, P)),
    ("conv_prompt", (3, D), (1, 1, 3, D)), ("C_prompt", (H, P, P), (1, 1, H, P, P)),
    ("n_prompt", (H, P), (1, 1, H, P)), ("m_prompt", (H, 1), (1, 1, H)),
    ("k_sample", (TS, 512), (1, NB, TD, H, 2, DK)), ("v_sample", (TS, 512), (1, NB, TD, H, P)),
    ("conv_sample", (NB * 3, D), (1, NB, 3, D)), ("C_sample", (NB, H, P, P), (1, NB, H, P, P)),
    ("n_sample", (NB * H, P), (1, NB, H, P)), ("m_sample", (NB, H), (1, NB, H)),
]
_INS = {
    "x_prompt": (TP, D), "x_sample": (TS, D), "c_prompt": (1, D), "c_sample": (NB, D),
    "cache_k": (N_POOL, P, 512), "cache_v": (N_POOL, P, 512), "state_conv": (NB * 3, D),
    "state_C": (NB, H, P, P), "state_n": (NB * H, P), "state_m": (NB, H), "page_table": (1, 64),
    "w_ada": (D, 6 * D), "b_ada": (1, 6 * D), "g_norm1": (1, D), "g_norm2": (1, D), "w_in": (D, 5640),
    "b_gates": (1, 8), "lambda_q1": (1, DK), "lambda_k1": (1, DK), "lambda_q2": (1, DK),
    "lambda_k2": (1, DK), "g_subln": (1, P), "w_conv": (4, D), "b_conv": (1, D), "g_mnorm": (1, 512),
    "w_up_a": (512, D), "w_up_b": (512, D), "w_out": (D, D), "w_router": (D, NE), "b_router": (1, NE),
    "w_gu": (NE, D, 2 * FF), "b_gu": (NE, 2 * FF), "w_down": (NE, FF, D), "b_down": (NE, D),
    "g_final": (1, D),
}


def kernel(**inputs):
    import concourse.bacc as _bacc
    from concourse.bass_utils import run_bass_kernel_spmd as _run

    nc = _bacc.Bacc("TRN2", target_bir_lowering=False, num_devices=1)
    pack, const_at, n_keep = const_pack()
    arrays = {"in_const": pack}
    I = {"const": nc.dram_tensor("in_const", pack.shape, F32, kind="ExternalInput").ap()}
    for name, shape in _INS.items():
        a = np.ascontiguousarray(inputs[name]).reshape(shape)
        arrays["in_" + name] = a
        I[name] = nc.dram_tensor("in_" + name, shape, mybir.dt.from_np(a.dtype), kind="ExternalInput").ap()
    O = {name: nc.dram_tensor("out_" + name, shape, F32, kind="ExternalOutput").ap()
         for name, shape, _ in _OUTS}
    build(nc, I, O, const_at, pack.shape[1], n_keep)
    r = _run(nc, [arrays], core_ids=[0])
    return tuple(r.results[0]["out_" + name].reshape(final) for name, _, final in _OUTS)
```
